# Optimizing a Trainium2 kernel written in Bass

```python
import jax, jax.numpy as jnp
from jax import lax
import numpy as np

D_MODEL = 1024
BATCH = 1
SEQ = 512
DEPTH = 1
DEC_BATCH = 8
DEC_SEQ = 16
PAST_LEN = 512

CHUNK = 64
Q_BLOCK = 128
H_ATT = 8
HEAD_DIM = 64
D_ATT = H_ATT * HEAD_DIM
H_SSD = 8
SSD_HEAD_DIM = 64
D_SSD = H_SSD * SSD_HEAD_DIM
SSD_GROUPS = 2
HEADS_PER_GROUP = H_SSD // SSD_GROUPS
SSD_STATE = 64
CONV_W = 4
CONV_DIM = D_SSD + 2 * SSD_GROUPS * SSD_STATE
D_IN = 3 * D_ATT + D_SSD + CONV_DIM + H_SSD
N_KEYS = 128
N_EXPERTS = N_KEYS * N_KEYS
PEER_HEADS = 8
PEER_TOPK = 16
PEER_QDIM = 128
PEER_HALF = PEER_QDIM // 2
PEER_BLOCK = 256
EPS = 1e-6

kernel_name = "hybrid_stickbreak_ssd_peer_stream_step"

def rmsnorm(x, g):
    xf = x.astype(jnp.float32)
    return (xf * lax.rsqrt(jnp.mean(xf * xf, axis=-1, keepdims=True) + EPS) * g).astype(x.dtype)

def stick_breaking(q, k, v, q_pos, k_pos):
    z = jnp.einsum('bqhd,bkhd->bhqk', q, k).astype(jnp.float32) * (HEAD_DIM ** -0.5)
    valid = k_pos[None, :] < q_pos[:, None]
    log_keep = jnp.where(valid, jax.nn.log_sigmoid(-z), 0.0)
    after = lax.cumsum(log_keep, axis=3, reverse=True) - log_keep
    w = jnp.where(valid, jnp.exp(jax.nn.log_sigmoid(z) + after), 0.0)
    return jnp.einsum('bhqk,bkhd->bqhd', w.astype(v.dtype), v)

def ssd_scan(xs, dt, a, bm, cm, h0, q):
    b, l, g, kk, p = xs.shape
    nc = l // q
    xs = xs.reshape(b, nc, q, g, kk, p)
    dt = dt.reshape(b, nc, q, g, kk)
    bm = bm.reshape(b, nc, q, g, -1)
    cm = cm.reshape(b, nc, q, g, -1)
    cum = jnp.cumsum(dt * a, axis=2)
    causal = jnp.tril(jnp.ones((q, q), bool))
    seg = cum[:, :, :, None] - cum[:, :, None, :]
    decay = jnp.exp(jnp.where(causal[:, :, None, None], seg, -jnp.inf))
    xdt = xs * dt[..., None]
    cb = jnp.einsum('bctgn,bcsgn->bctsg', cm, bm)
    y_diag = jnp.einsum('bctsg,bctsgk,bcsgkp->bctgkp', cb, decay, xdt)
    to_end = jnp.exp(cum[:, :, -1:] - cum)
    chunk_states = jnp.einsum('bcsgn,bcsgk,bcsgkp->bcgkpn', bm, to_end, xdt)
    chunk_decay = jnp.exp(cum[:, :, -1])

    def step(h, inp):
        s, d = inp
        return d[..., None, None] * h + s, h

    h_fin, h_in = lax.scan(step, h0.astype(jnp.float32),
                           (jnp.moveaxis(chunk_states, 1, 0), jnp.moveaxis(chunk_decay, 1, 0)))
    h_in = jnp.moveaxis(h_in, 0, 1)
    y_off = jnp.einsum('bctgn,bcgkpn,bctgk->bctgkp', cm, h_in, jnp.exp(cum))
    return (y_diag + y_off).reshape(b, l, g, kk, p), h_fin

def peer_ffn(h, w_pq, sub_keys, u_tab, v_tab):
    b, l, d = h.shape
    n = b * l
    nb = -(-n // PEER_BLOCK)
    t = jnp.pad(h.reshape(n, d), ((0, nb * PEER_BLOCK - n), (0, 0))).reshape(nb, PEER_BLOCK, d)

    def block(xb):
        qh = (xb @ w_pq).reshape(PEER_BLOCK, PEER_HEADS, 2, PEER_HALF)
        s = jnp.einsum('thcd,ckd->thck', qh, sub_keys).astype(jnp.float32)
        s_top, i_top = lax.top_k(s, PEER_TOPK)
        cand = (s_top[:, :, 0, :, None] + s_top[:, :, 1, None, :]).reshape(PEER_BLOCK, PEER_HEADS, PEER_TOPK * PEER_TOPK)
        best, ci = lax.top_k(cand, PEER_TOPK)
        e = (jnp.take_along_axis(i_top[:, :, 0], ci // PEER_TOPK, axis=-1) * N_KEYS
             + jnp.take_along_axis(i_top[:, :, 1], ci % PEER_TOPK, axis=-1))
        gw = jax.nn.softmax(best, axis=-1).reshape(PEER_BLOCK, PEER_HEADS * PEER_TOPK)
        e = e.reshape(PEER_BLOCK, PEER_HEADS * PEER_TOPK)
        act = jax.nn.gelu(jnp.einsum('tkd,td->tk', u_tab[e], xb).astype(jnp.float32)) * gw
        return jnp.einsum('tk,tkd->td', act.astype(xb.dtype), v_tab[e])

    y = lax.map(block, t).reshape(nb * PEER_BLOCK, d)[:n]
    return y.reshape(b, l, d)

def _layer(x, c, k_past, v_past, ssm0, conv0, w_ada, b_ada, g_pre_mix, g_post_mix, g_pre_ffn,
           g_post_ffn, w_in, conv_w, conv_b, dt_bias, a_log, d_skip, g_attn_norm, g_ssd_norm,
           w_out, w_pq, sub_keys, u_tab, v_tab):
    b, l, _ = x.shape
    mod = jax.nn.silu(c) @ w_ada + b_ada
    sh1, sc1, gt1, sh2, sc2, gt2 = [m[:, None, :] for m in jnp.split(mod, 6, axis=-1)]

    h = rmsnorm(x, g_pre_mix) * (1 + sc1) + sh1
    proj = h @ w_in
    cuts = [D_ATT, 2 * D_ATT, 3 * D_ATT, 3 * D_ATT + D_SSD, 3 * D_ATT + D_SSD + CONV_DIM]
    q, k, v, z, xbc, dt_raw = jnp.split(proj, cuts, axis=-1)

    q = q.reshape(b, l, H_ATT, HEAD_DIM)
    k = k.reshape(b, l, H_ATT, HEAD_DIM)
    v = v.reshape(b, l, H_ATT, HEAD_DIM)
    if k_past is None:
        pos = jnp.arange(l)
        outs = [stick_breaking(q[:, s:s + Q_BLOCK], k[:, :s + Q_BLOCK], v[:, :s + Q_BLOCK],
                               pos[s:s + Q_BLOCK], pos[:s + Q_BLOCK])
                for s in range(0, l, Q_BLOCK)]
        o = jnp.concatenate(outs, axis=1)
    else:
        past = k_past.shape[1]
        k_all = jnp.concatenate([k_past.astype(k.dtype), k], axis=1)
        v_all = jnp.concatenate([v_past.astype(v.dtype), v], axis=1)
        o = stick_breaking(q, k_all, v_all, past + jnp.arange(l), jnp.arange(past + l))
    attn_o = rmsnorm(o.reshape(b, l, D_ATT), g_attn_norm)

    conv_in = jnp.concatenate([conv0.astype(xbc.dtype), xbc], axis=1)
    conv_new = conv_in[:, -(CONV_W - 1):]
    xbc = lax.conv_general_dilated(conv_in, conv_w.astype(conv_in.dtype), (1,), 'VALID',
                                   dimension_numbers=('NWC', 'WIO', 'NWC'),
                                   feature_group_count=CONV_DIM)
    xbc = jax.nn.silu(xbc + conv_b)
    xs, bm, cm = jnp.split(xbc, [D_SSD, D_SSD + SSD_GROUPS * SSD_STATE], axis=-1)
    xs = xs.reshape(b, l, SSD_GROUPS, HEADS_PER_GROUP, SSD_HEAD_DIM)
    bm = bm.reshape(b, l, SSD_GROUPS, SSD_STATE)
    cm = cm.reshape(b, l, SSD_GROUPS, SSD_STATE)
    dt = jax.nn.softplus((dt_raw + dt_bias).astype(jnp.float32)).reshape(b, l, SSD_GROUPS, HEADS_PER_GROUP)
    a = -jnp.exp(a_log.astype(jnp.float32)).reshape(SSD_GROUPS, HEADS_PER_GROUP)
    h0 = ssm0.reshape(b, SSD_GROUPS, HEADS_PER_GROUP, SSD_HEAD_DIM, SSD_STATE)
    chunk = CHUNK if l % CHUNK == 0 else l
    y, h_fin = ssd_scan(xs, dt, a, bm, cm, h0, chunk)
    y = y + d_skip.reshape(SSD_GROUPS, HEADS_PER_GROUP, 1) * xs
    ssd_o = rmsnorm((y.reshape(b, l, D_SSD) * jax.nn.silu(z)).astype(x.dtype), g_ssd_norm)

    mix = jnp.concatenate([attn_o, ssd_o], axis=-1) @ w_out
    x = x + gt1 * rmsnorm(mix, g_post_mix)

    h2 = rmsnorm(x, g_pre_ffn) * (1 + sc2) + sh2
    f = peer_ffn(h2, w_pq, sub_keys, u_tab, v_tab)
    x = x + gt2 * rmsnorm(f, g_post_ffn)
    ssm_new = h_fin.reshape(b, H_SSD, SSD_HEAD_DIM, SSD_STATE).astype(ssm0.dtype)
    return x, k, v, ssm_new, conv_new

def setup_inputs(seed: int = 0) -> dict:
    key = jax.random.key(seed)
    ks = jax.random.split(key, 32)
    f32 = jnp.float32

    def nrm(k, shape, scale):
        return jax.random.normal(k, shape, f32) * scale

    L = DEPTH
    dt0 = jnp.exp(jax.random.uniform(ks[20], (L, H_SSD), f32, np.log(1e-3), np.log(1e-1)))
    return {
        "x_prompt": nrm(ks[0], (BATCH, SEQ, D_MODEL), 1.0),
        "x_sample": nrm(ks[1], (DEC_BATCH, DEC_SEQ, D_MODEL), 1.0),
        "c_prompt": nrm(ks[2], (BATCH, D_MODEL), 1.0),
        "c_sample": nrm(ks[3], (DEC_BATCH, D_MODEL), 1.0),
        "cache_k": nrm(ks[4], (L, DEC_BATCH, PAST_LEN, H_ATT, HEAD_DIM), 1.0),
        "cache_v": nrm(ks[5], (L, DEC_BATCH, PAST_LEN, H_ATT, HEAD_DIM), 1.0),
        "state_ssm": nrm(ks[6], (L, DEC_BATCH, H_SSD, SSD_HEAD_DIM, SSD_STATE), 0.5),
        "state_conv": nrm(ks[7], (L, DEC_BATCH, CONV_W - 1, CONV_DIM), 1.0),
        "w_ada": nrm(ks[8], (L, D_MODEL, 6 * D_MODEL), 0.5 * D_MODEL ** -0.5),
        "b_ada": nrm(ks[9], (L, 6 * D_MODEL), 0.01),
        "g_pre_mix": 1.0 + nrm(ks[10], (L, D_MODEL), 0.05),
        "g_post_mix": 1.0 + nrm(ks[11], (L, D_MODEL), 0.05),
        "g_pre_ffn": 1.0 + nrm(ks[12], (L, D_MODEL), 0.05),
        "g_post_ffn": 1.0 + nrm(ks[13], (L, D_MODEL), 0.05),
        "w_in": nrm(ks[14], (L, D_MODEL, D_IN), D_MODEL ** -0.5),
        "conv_w": nrm(ks[15], (L, CONV_W, 1, CONV_DIM), CONV_W ** -0.5),
        "conv_b": nrm(ks[16], (L, CONV_DIM), 0.01),
        "dt_bias": dt0 + jnp.log(-jnp.expm1(-dt0)),
        "a_log": jnp.log(jax.random.uniform(ks[17], (L, H_SSD), f32, 1.0, 16.0)),
        "d_skip": 1.0 + nrm(ks[18], (L, H_SSD), 0.05),
        "g_attn_norm": 1.0 + nrm(ks[19], (L, D_ATT), 0.05),
        "g_ssd_norm": 1.0 + nrm(ks[21], (L, D_SSD), 0.05),
        "w_out": nrm(ks[22], (L, D_ATT + D_SSD, D_MODEL), (D_ATT + D_SSD) ** -0.5),
        "w_pq": nrm(ks[23], (L, D_MODEL, PEER_HEADS * PEER_QDIM), D_MODEL ** -0.5),
        "sub_keys": nrm(ks[24], (L, 2, N_KEYS, PEER_HALF), PEER_HALF ** -0.5),
        "u_tab": nrm(ks[25], (L, N_EXPERTS, D_MODEL), D_MODEL ** -0.5),
        "v_tab": nrm(ks[26], (L, N_EXPERTS, D_MODEL), D_MODEL ** -0.5),
    }

def reference(x_prompt, x_sample, c_prompt, c_sample, cache_k, cache_v, state_ssm, state_conv,
              w_ada, b_ada, g_pre_mix, g_post_mix, g_pre_ffn, g_post_ffn, w_in, conv_w, conv_b,
              dt_bias, a_log, d_skip, g_attn_norm, g_ssd_norm, w_out, w_pq, sub_keys, u_tab, v_tab):
    bp = x_prompt.shape[0]
    xp, xq = x_prompt, x_sample
    kp, vp, sp, cp, kq, vq, sq, cq = [], [], [], [], [], [], [], []
    for i in range(DEPTH):
        lw = (w_ada[i], b_ada[i], g_pre_mix[i], g_post_mix[i], g_pre_ffn[i], g_post_ffn[i],
              w_in[i], conv_w[i], conv_b[i], dt_bias[i], a_log[i], d_skip[i], g_attn_norm[i],
              g_ssd_norm[i], w_out[i], w_pq[i], sub_keys[i], u_tab[i], v_tab[i])
        ssm_zero = jnp.zeros((bp, H_SSD, SSD_HEAD_DIM, SSD_STATE), xp.dtype)
        conv_zero = jnp.zeros((bp, CONV_W - 1, CONV_DIM), xp.dtype)
        xp, k1, v1, s1, c1 = _layer(xp, c_prompt, None, None, ssm_zero, conv_zero, *lw)
        xq, k2, v2, s2, c2 = _layer(xq, c_sample, cache_k[i], cache_v[i], state_ssm[i], state_conv[i], *lw)
        kp.append(k1); vp.append(v1); sp.append(s1); cp.append(c1)
        kq.append(k2); vq.append(v2); sq.append(s2); cq.append(c2)
    return (xp, xq, jnp.stack(kp), jnp.stack(vp), jnp.stack(sp), jnp.stack(cp),
            jnp.stack(kq), jnp.stack(vq), jnp.stack(sq), jnp.stack(cq))


_drawn_inputs = setup_inputs


def setup_inputs(seed=0):
    import zlib

    import numpy as np

    out = dict(_drawn_inputs(seed))
    spreads = {}
    factors = {'g_post_ffn': 3.926, 'conv_b': 3.235}
    for name, (base, spread) in spreads.items():
        noise = np.random.default_rng([zlib.crc32(name.encode()), seed]).standard_normal(out[name].shape)
        drawn = base * np.exp(spread * noise) if base else spread * noise
        out[name] = __import__('jax').numpy.asarray(drawn.astype(out[name].dtype))
    for name, factor in factors.items():
        out[name] = (out[name] * factor).astype(out[name].dtype)
    return out
```

```python
from contextlib import ExitStack, contextmanager

import numpy as np

import concourse.bass as bass
from concourse import mybir

F32 = mybir.dt.float32
F32R = mybir.dt.float32r
U32 = mybir.dt.uint32
ALU = mybir.AluOpType
ACT = mybir.ActivationFunctionType
AX = mybir.AxisListType.X
ds = bass.ds

P = 128
D = 1024
KD = D // P
SEQ = 512
NSEQ, LSEQ = 8, 16
NT = 5
TOK = NT * P
HALF = TOK // 2
PAST = 512
H, HD = 8, 64
NCOND = 1 + NSEQ
ADA = 6 * D
CW = 4
SEGP = CW - 1 + SEQ
SEGS = CW - 1 + LSEQ
CONVW = SEGP + NSEQ * SEGS
CONVO = CONVW - (CW - 1)
NKEY = 128
TOPK = 16
EPS = 1e-6
FAR = -1e30


class Memory:
    pass


def spread(ap, axis, n):
    shape = list(ap.shape)
    shape.insert(axis, n)
    return ap.unsqueeze(axis).broadcast_to(shape)


def build_constants(nc, m, sem, sb):
    m.ident = sb("ident", [P, P])
    m.ones = sb("ones", [P, P])
    m.upto = sb("upto", [P, 2, P])
    m.later = sb("later", [P, 2, P])
    m.from_ = sb("from_", [P, P])
    m.seen = sb("seen", [P, NT, P])
    m.same = sb("same", [P, P])
    m.hide = sb("hide", [P, NT, P])
    m.hide_ssd = sb("hide_ssd", [P, 2, P])
    m.mhalf = sb("mhalf", [P, 2 * NT])
    filled, built = sem("const_filled"), sem("const_built")
    hidden = sem("const_hidden")
    with nc.Block() as block:
        @block.gpsimd
        def _(pool):
            pool.memset(m.ident[:, :], 0.0).then_inc(filled, 1)
            pool.memset(m.mhalf[:, :], -0.5).then_inc(filled, 1)
            for t in (m.ones, m.from_, m.same):
                pool.memset(t[:, :], 1.0).then_inc(filled, 1)
            for t in (m.upto, m.later, m.seen):
                pool.memset(t[:, :, :], 1.0).then_inc(filled, 1)
            pool.wait_ge(filled, 8)

            done = 0

            def keep(view, compare, base, pattern, by_row, fill=0.0):
                nonlocal done
                pool.affine_select(out=view, in_=view, compare_op=compare, fill=fill, base=base,
                                   pattern=pattern, channel_multiplier=by_row).then_inc(built, 1)
                done += 1

            keep(m.ident[:, :], ALU.not_equal, 0, [[-1, P]], 1, 1.0)
            keep(m.from_[:, :], ALU.is_ge, 0, [[-1, P]], 1)
            keep(m.upto[:, :, :], ALU.is_ge, 0, [[0, 2], [1, P]], -1)
            keep(m.later[:, :, :], ALU.is_gt, 0, [[0, 2], [-1, P]], 1)
            keep(m.seen[:, :, :], ALU.is_gt, 0, [[0, NT], [1, P]], -1)
            blocks = (m.same[:, :], m.upto[:, 1, :], m.later[:, 1, :], m.seen[:, NT - 1, :])
            pool.wait_ge(built, done)
            for v in blocks:
                keep(v, ALU.is_ge, 0, [[-LSEQ, NSEQ], [0, LSEQ]], 1)
            pool.wait_ge(built, done)
            for v in blocks:
                keep(v, ALU.is_ge, LSEQ - 1, [[LSEQ, NSEQ], [0, LSEQ]], -1)
            m.n_built = done

        @block.vector
        def _(dve):
            dve.wait_ge(built, m.n_built)
            dve.tensor_scalar(m.hide[:, :, :], m.seen[:, :, :], -1.0, -FAR, ALU.add, ALU.mult).then_inc(hidden, 1)
            dve.tensor_scalar(m.hide_ssd[:, :, :], m.upto[:, :, :], -1.0, -FAR, ALU.add, ALU.mult).then_inc(hidden, 1)


def modulate(nc, m, T, sem, sb, ps):
    NCH = ADA // 512
    cT = sb("cT", [P, KD, NCOND])
    sT = sb("sT", [P, KD, NCOND])
    wa = sb("wa", [P, 2, KD, 512])
    ba = sb("ba", [NCOND, ADA])
    row = sb("mod_row", [NCOND, ADA])
    gcol = sb("gcol", [P, 2, KD])
    colp = ps("mod_col_ps", [P, 2, 512])
    acc = ps("mod_ps", [P, 2, 512])
    small_in, wa_in = sem("mod_small_in"), [sem(f"wa_in{s}") for s in range(2)]
    silu_done, chunk_done, row_done = sem("mod_silu"), sem("mod_chunk"), sem("mod_row")
    col_done, scaled, gates_out = sem("mod_cols"), sem("mod_scaled"), sem("gates_out")
    w = T["w_ada"].rearrange("(k p) n -> p k n", p=P)

    with nc.Block() as block:
        @block.sync
        def _(sp):
            sp.dma_start(cT[:, :, :], T["cT"]).then_inc(small_in, 16)
            sp.dma_start(ba[:, :], T["b_ada"].partition_broadcast(NCOND)).then_inc(small_in, 16)
            sp.dma_start(gcol[:, 0, :], T["g_pre_mix"]).then_inc(small_in, 16)
            sp.dma_start(gcol[:, 1, :], T["g_pre_ffn"]).then_inc(small_in, 16)
            for s in range(2):
                sp.dma_start(wa[:, s, :, :], w[:, :, s * 512:(s + 1) * 512]).then_inc(wa_in[s], 16)
            with sp.Fori(1, NCH // 2) as i:
                for s in range(2):
                    sp.wait_ge(chunk_done, i * 2 + (s - 1))
                    sp.dma_start(wa[:, s, :, :], w[:, :, ds(i * 1024 + s * 512, 512)]).then_inc(wa_in[s], 16)
            sp.wait_ge(row_done, NCH)
            for g, c in enumerate((2, 5)):
                sp.dma_start(T["gates"][g], row[:, c * D:(c + 1) * D]).then_inc(gates_out, 16)
            sp.wait_ge(gates_out, 32)

        @block.scalar
        def _(act):
            act.wait_ge(small_in, 64)
            act.activation(sT[:, :, :], cT[:, :, :], ACT.Silu).then_inc(silu_done, 1)

        @block.tensor
        def _(pe):
            pe.wait_ge(silu_done, 1)

            def chunk(s, i, n):
                pe.wait_ge(wa_in[s], i * 16 + 16)
                if n is None or n >= 2:
                    pe.wait_ge(row_done, i * 2 + (s - 1))
                for k in range(KD):
                    mm = pe.matmul(acc[0:NCOND, s, :], sT[:, k, :], wa[:, s, k, :], start=(k == 0), stop=(k == KD - 1))
                mm.then_inc(chunk_done, 1)

            for s in range(2):
                chunk(s, 0, s)
            with pe.Fori(1, NCH // 2) as i:
                for s in range(2):
                    chunk(s, i, None)
            pe.wait_ge(row_done, NCH)
            for j, c in enumerate((0, 1, 3, 4)):
                for k in range(KD):
                    at = (j % 2) * KD * NCOND + k * NCOND
                    mm = pe.transpose(colp[:, j // 2, at:at + NCOND],
                                      row[:, c * D + k * P:c * D + (k + 1) * P], m.ident[0:NCOND, 0:NCOND])
            mm.then_inc(col_done, 1)

        @block.vector
        def _(dve):
            dve.wait_ge(small_in, 64)
            with dve.Fori(0, NCH // 2) as i:
                for s in range(2):
                    dve.wait_ge(chunk_done, i * 2 + (s + 1))
                    at = ds(i * 1024 + s * 512, 512)
                    dve.tensor_tensor(row[:, at], acc[0:NCOND, s, :], ba[:, at], ALU.add).then_inc(row_done, 1)
            dve.wait_ge(col_done, 1)
            n = KD * NCOND
            for half in range(2):
                v = colp[:, half, 0:2 * n].rearrange("p (a k c) -> p a k c", a=2, k=KD)
                dve.tensor_copy(m.shift[:, half, :, :], v[:, 0]).then_inc(scaled, 1)
                dve.scalar_tensor_tensor(m.scale[:, half, :, :], v[:, 1], 1.0, spread(gcol[:, half, :], 2, NCOND),
                                         ALU.add, ALU.mult).then_inc(scaled, 1)


def norm_to_columns(nc, m, sem, ps, name, load, src, dst, which, extra=None):
    ss = m.stat
    pr = ps(name + "_ps", [P, 2, 512])
    sa = ps(name + "_ps_s", [P, 2, 512])
    squared, mean, rstd, normed = (sem(name + x) for x in ("_sq", "_mean", "_rstd", "_normed"))
    turned, turned_s, out_p, out_s = (sem(name + x) for x in ("_tp", "_ts", "_op", "_os"))
    loaded = [sem(f"{name}_in{t}") for t in range(NT)]
    with nc.Block() as block:
        if load is not None:
            @block.sync
            def _(sp):
                for t in range(NT):
                    sp.dma_start(src[:, t, :], load[t * P:(t + 1) * P, :]).then_inc(loaded[t], 16)

        @block.scalar
        def _(act):
            for t in range(NT):
                if load is not None:
                    act.wait_ge(loaded[t], 16)
                if t >= 2:
                    act.wait_ge(squared, t - 1)
                act.activation(m.junk[:, t % 2, :], src[:, t, :], ACT.Square, accum_out=ss[:, t:t + 1]).then_inc(squared, 1)

        @block.gpsimd
        def _(pool):
            pool.wait_ge(mean, 1)
            pool.tensor_tensor(m.rstd[:, :], ss[:, :], m.mhalf[:, 0:NT], ALU.pow).then_inc(rstd, 1)

        @block.vector
        def _(dve):
            dve.wait_ge(squared, NT)
            dve.tensor_scalar(ss[:, :], ss[:, :], 1.0 / D, EPS, ALU.mult, ALU.add).then_inc(mean, 1)
            dve.wait_ge(rstd, 1)
            for t in range(NT):
                dve.tensor_scalar(src[:, t, :], src[:, t, :], m.rstd[:, t:t + 1], None, ALU.mult).then_inc(normed, 1)
            for k in range(KD):
                dve.wait_ge(turned, k + 1)
                dve.tensor_scalar(dst[:, k, 0:SEQ], pr[:, k % 2, :], m.scale[:, which, k, 0:1],
                                  m.shift[:, which, k, 0:1], ALU.mult, ALU.add).then_inc(out_p, 1)
                if k % 4 == 3:
                    q = k // 4
                    dve.wait_ge(turned_s, q + 1)
                    d4 = dst[:, 4 * q:4 * q + 4, SEQ:TOK].rearrange("p k (b i) -> p k b i", b=NSEQ)
                    s4 = sa[:, q, :].rearrange("p (k b i) -> p k b i", k=4, b=NSEQ)
                    for kk in range(4):
                        dve.tensor_tensor(d4[:, kk], s4[:, kk],
                                          spread(m.scale[:, which, 4 * q + kk, 1:NCOND], 2, LSEQ),
                                          ALU.mult).then_inc(out_s, 1)
                    dve.wait_ge(out_s, 8 * q + 4)
                    for kk in range(4):
                        dve.tensor_tensor(d4[:, kk], d4[:, kk],
                                          spread(m.shift[:, which, 4 * q + kk, 1:NCOND], 2, LSEQ),
                                          ALU.add).then_inc(out_s, 1)

        @block.tensor
        def _(pe):
            pe.wait_ge(normed, NT)
            for k in range(KD):
                if k >= 2:
                    pe.wait_ge(out_p, k - 1)
                for t in range(NT - 1):
                    mm = pe.transpose(pr[:, k % 2, t * P:(t + 1) * P], src[:, t, k * P:(k + 1) * P], m.ident[:, :])
                mm.then_inc(turned, 1)
                mm = pe.transpose(sa[:, k // 4, (k % 4) * P:(k % 4 + 1) * P], src[:, NT - 1, k * P:(k + 1) * P],
                                  m.ident[:, :])
                if k % 4 == 3:
                    mm.then_inc(turned_s, 1)


def column_products(nc, m, sem, sb, ps, name, w_blocks, n_blocks, src, sink):
    ring = sb(name + "_w", [P, 2, KD, P])
    acc = ps(name + "_acc", [P, 2, 2, 512])
    w_in, made, taken = [sem(f"{name}_in{s}") for s in range(2)], sem(name + "_made"), sem(name + "_taken")
    with nc.Block() as block:
        @block.sync
        def _(sp):
            for s in range(2):
                sp.dma_start(ring[:, s, :, :], w_blocks[s]).then_inc(w_in[s], 16)
            with sp.Fori(1, n_blocks // 2) as i:
                for s in range(2):
                    sp.wait_ge(made, i * 2 + (s - 1))
                    sp.dma_start(ring[:, s, :, :], w_blocks[ds(i * 2 + s, 1)].rearrange("a p k c -> (a p) k c")
                                 ).then_inc(w_in[s], 16)

        @block.tensor
        def _(pe):
            def blk(i, s, first):
                pe.wait_ge(w_in[s], i * 16 + 16)
                if not first:
                    pe.wait_ge(taken, i * 2 + (s - 1))
                for k in range(KD):
                    for h in range(2):
                        mm = pe.matmul(acc[:, s, h, 0:HALF], ring[:, s, k, :], src[:, k, h * HALF:(h + 1) * HALF],
                                       start=(k == 0), stop=(k == KD - 1))
                mm.then_inc(made, 1)
            for s in range(2):
                blk(0, s, True)
            with pe.Fori(1, n_blocks // 2) as i:
                for s in range(2):
                    blk(i, s, False)

        @block.scalar
        def _(act):
            sink(act, acc, made, taken)


def project(nc, m, T, sem, sb, ps, psctx):
    def sink(act, acc, made, taken):
        with act.Fori(0, 4) as i:
            for s in range(2):
                act.wait_ge(made, i * 2 + (s + 1))
                act.copy(m.qkT[:, ds(i * 2 + s, 1), :].rearrange("p a (h n) -> p (a h) n", h=2),
                         acc[:, s, :, 0:HALF]).then_inc(taken, 1)
        for n in range(8, 14):
            s, j = n % 2, n - 8
            act.wait_ge(made, n + 1)
            act.copy(m.xpad[:, j, CW - 1:CW - 1 + HALF], acc[:, s, 0, 0:HALF])
            act.copy(m.xpad[:, j, CW - 1 + HALF:SEGP], acc[:, s, 1, 0:SEQ - HALF])
            act.copy(m.xpad[:, j, SEGP:].rearrange("p (b i) -> p b i", b=NSEQ)[:, :, CW - 1:],
                     acc[:, s, 1, SEQ - HALF:HALF].rearrange("p (b i) -> p b i", b=NSEQ)).then_inc(taken, 1)

    with psctx() as pp:
        column_products(nc, m, sem, sb, pp, "proj", T["w_cols"], 14, m.hT, sink)

    wv = sb("w_rows", [P, KD, 1024 + H])
    rows_in, pads_in = sem("rows_in"), sem("pads_in")
    vz_made, vz_taken, dt_made, dt_taken = sem("vz_made"), sem("vz_taken"), sem("dt_made"), sem("dt_taken")
    conv, conv_ready, out_done = sem("conv_step"), sem("conv_sum"), sem("proj_out")
    zeroed, silu_done = sem("pad_zero"), sem("conv_silu")
    with psctx() as pp, nc.Block() as block:
        acc = pp("vz_ps", [P, 2, 2, 512])
        dtp = pp("dt_ps", [P, 512])

        @block.sync
        def _(sp):
            for c in range(2):
                sp.dma_start(wv[:, :, c * 512:(c + 1) * 512], T["w_vz"][:, :, c * 512:(c + 1) * 512]).then_inc(rows_in, 16)
            sp.dma_start(wv[:, :, 1024:], T["w_vz"][:, :, 1024:]).then_inc(rows_in, 16)
            for j in range(6):
                sp.dma_start(m.xpad[:, j, SEGP:].rearrange("p (b i) -> p b i", b=NSEQ)[:, :, 0:CW - 1],
                             T["state_conv"][:, j]).then_inc(pads_in, 16)
            sp.dma_start(m.conv_w[:, :, :], T["conv_w"]).then_inc(pads_in, 16)
            sp.dma_start(m.conv_b[:, :], T["conv_b"]).then_inc(pads_in, 16)
            sp.dma_start(m.dt_bias[:, :], T["dt_bias"].partition_broadcast(P)).then_inc(pads_in, 16)
            sp.dma_start(m.a_log[:, :], T["a_log"].partition_broadcast(P)).then_inc(pads_in, 16)
            sp.dma_start(m.d_skip[:, :], T["d_skip"].partition_broadcast(P)).then_inc(pads_in, 16)
            sp.dma_start(T["kT_out"], m.qkT[:, 4:8, :]).then_inc(out_done, 16)
            for j in range(6):
                sp.dma_start(T["conv_out"][:, j, 0, :], m.xpad[:, j, SEGP - (CW - 1):SEGP]).then_inc(out_done, 16)
                sp.dma_start(T["conv_out"][:, j, 1:NCOND, :],
                             m.xpad[:, j, SEGP:].rearrange("p (b i) -> p b i", b=NSEQ)[:, :, SEGS - (CW - 1):]
                             ).then_inc(out_done, 16)
            sp.wait_ge(vz_taken, NT)
            for t in range(NT):
                sp.dma_start(T["v_out"][t * P:(t + 1) * P, :], m.vN[:, t, :]).then_inc(out_done, 16)
            sp.wait_ge(out_done, 16 * (13 + NT))

        @block.tensor
        def _(pe):
            for t in range(NT):
                if t == 0:
                    pe.wait_ge(rows_in, 48)
                if t >= 2:
                    pe.wait_ge(vz_taken, t - 1)
                for k in range(KD):
                    lhs = m.hT[:, k, t * P:(t + 1) * P]
                    pe.matmul(acc[:, t % 2, 0, :], lhs, wv[:, k, 0:512], start=(k == 0), stop=(k == KD - 1))
                    mm = pe.matmul(acc[:, t % 2, 1, :], lhs, wv[:, k, 512:1024], start=(k == 0), stop=(k == KD - 1))
                mm.then_inc(vz_made, 1)
                for k in range(KD):
                    mm = pe.matmul(dtp[:, t * H:(t + 1) * H], m.hT[:, k, t * P:(t + 1) * P], wv[:, k, 1024:],
                                   start=(k == 0), stop=(k == KD - 1))
            mm.then_inc(dt_made, 1)

        @block.vector
        def _(dve):
            dve.memset(m.xpad[:, :, 0:CW - 1], 0.0).then_inc(zeroed, 1)
            dve.wait_ge(pads_in, 16 * 11)
            dve.wait_ge(zeroed, 1)
            for w in range(CW):
                for j in range(6):
                    src = m.xpad[:, j, w:w + CONVO]
                    if w:
                        dve.wait_ge(conv, (w - 1) * 6 + j + 1)
                        dve.scalar_tensor_tensor(m.xc[:, j, 0:CONVO], src, m.conv_w[:, j, w:w + 1], m.xc[:, j, 0:CONVO],
                                                 ALU.mult, ALU.add).then_inc(conv, 1)
                    else:
                        dve.tensor_scalar(m.xc[:, j, 0:CONVO], src, m.conv_w[:, j, 0:1], m.conv_b[:, j:j + 1],
                                          ALU.mult, ALU.add).then_inc(conv, 1)
            dve.wait_ge(dt_made, 1)
            dve.tensor_tensor(m.dt[:, :, :], dtp[:, 0:NT * H].rearrange("p (t h) -> p t h", t=NT),
                              spread(m.dt_bias[:, :], 1, NT), ALU.add).then_inc(dt_taken, 1)

        @block.scalar
        def _(act):
            for t in range(NT):
                act.wait_ge(vz_made, t + 1)
                act.copy(m.vN[:, t, :], acc[:, t % 2, 0, :])
                act.copy(m.zN[:, t, :], acc[:, t % 2, 1, :]).then_inc(vz_taken, 1)
            for j in range(6):
                act.wait_ge(conv, 18 + j + 1)
                act.activation(m.xc[:, j, 0:CONVO], m.xc[:, j, 0:CONVO], ACT.Silu).then_inc(silu_done, 1)


def scan(nc, m, T, sem, sb, ps):
    E = LSEQ * NSEQ
    xt = sb("xt", [P, 6, P])
    dts, das = sb("dts", [P, H]), sb("das", [P, H])
    a8, dtA = sb("a8", [P, H]), sb("dtA", [P, NT, H])
    sp = sb("sp_tmp", [P, NT * H])
    cum, grow = sb("cum", [P, 2 * H]), sb("grow", [P, 2, H])
    lastc = sb("lastc", [P, H, NSEQ])
    seg, dec, W = sb("seg", [P, H, P]), sb("dec", [P, H, P]), sb("W", [P, H, P])
    Bn = sb("Bn", [P, P])
    xdt, xdte, xD = sb("xdt", [P, H, HD]), sb("xdte", [P, H, HD]), sb("xD", [P, H, HD])
    state = sb("state", [P, 512])
    CTg = sb("CTg", [P, 2, P])
    cdec = sb("cdec", [P, H, NSEQ])
    CTm = sb("CTm", [P, NSEQ * (P + LSEQ)])
    Bm = sb("Bm", [P, NSEQ, P])
    sst = sb("sst", [P, NSEQ, 512])
    misc, csb = ps("scan_misc", [P, 512]), ps("scan_cs", [P, 512])
    rows = ps("scan_rows", [P, H, P])
    xsP, yd, yo, S = (ps(n, [P, 512]) for n in ("scan_xs", "scan_yd", "scan_yo", "scan_S"))
    cs, cb, bP = csb[:, 0:16], misc[:, 16:272].rearrange("p (g t) -> p g t", g=2), misc[:, 272:400]
    Spair = (S, xsP)

    ready, dt_step, dt_act = sem("scan_ready"), sem("dt_step"), sem("dt_act")
    staged = sem("scan_staged")
    cum_made, rows_made, cb_made, y_made = sem("cum_made"), sem("rows_made"), sem("cb_made"), sem("y_made")
    act_done, seg_step, w_ready, x_ready = sem("scan_exp"), sem("seg_step"), sem("w_ready"), sem("x_ready")
    state_step, y_step = sem("state_step"), sem("y_step")
    st_in, st_out, masked = sem("ssm_in"), sem("ssm_out_sem"), sem("scan_masked")
    bm_ready = sem("bm_ready")
    s_made, s_taken, aged = sem("S_made"), sem("S_taken"), sem("sst_aged")
    gate_silu, gated = sem("gate_silu"), sem("gated")
    flat = lambda v: v[:, :, :].rearrange("p t h -> p (t h)")
    NP = NT - 1

    def own(v, g):
        return v[64 * g:64 * g + 64, :, g * 256:(g + 1) * 256]

    with nc.Block() as block:
        @block.sync
        def _(eng):
            eng.wait_ge(masked, 2)
            for g in range(2):
                eng.dma_start(own(sst, g), T["state_ssm"][64 * g:64 * g + 64]).then_inc(st_in, 16)
            eng.wait_ge(state_step, 1 + 4 * NP)
            for g in range(2):
                r = slice(64 * g, 64 * g + 64)
                eng.dma_start(T["ssm_out"][r, 0, :], state[r, g * 256:(g + 1) * 256]).then_inc(st_out, 16)
            eng.wait_ge(s_taken, 2 * NSEQ)
            for g in range(2):
                eng.dma_start(T["ssm_out"][64 * g:64 * g + 64, 1:NCOND, :], own(sst, g)).then_inc(st_out, 16)
            eng.wait_ge(st_out, 64)

        @block.gpsimd
        def _(pool):
            pool.memset(state[:, :], 0.0).then_inc(state_step, 1)
            pool.memset(CTm[:, :], 0.0).then_inc(masked, 1)
            pool.memset(sst[:, :, :], 0.0).then_inc(masked, 1)
            pool.memset(CTg[:, :, :], 0.0).then_inc(staged, 1)
            pool.wait_ge(staged, 1)
            pool.wait_ge(ready, 1)

            def stage(i, sampled):
                for dst, src in ((dts, m.dt), (das, dtA)):
                    pool.tensor_copy(dst[:, :], src[:, ds(i, 1), :].rearrange("p a h -> p (a h)")
                                     if not sampled else src[:, NP, :]).then_inc(staged, 1)
                if sampled:
                    pool.tensor_copy(xt[:, :, :].rearrange("p j (b i) -> p j b i", b=NSEQ),
                                     m.xc[:, :, SEGP:].rearrange("p j (b i) -> p j b i", b=NSEQ)[:, :, :, 0:LSEQ]
                                     ).then_inc(staged, 1)
                else:
                    pool.tensor_copy(xt[:, :, :], m.xc[:, :, ds(i * P, P)]).then_inc(staged, 1)
                copied = i * 5 + 4 if sampled or isinstance(i, int) else pool.to_reg(i * 5 + 4)
                pool.wait_ge(ready, 1)
                pool.wait_ge(staged, copied)
                for g in range(2):
                    r = slice(64 * g, 64 * g + 64)
                    pool.tensor_copy(CTg[r, g, :], xt[r, 5, :]).then_inc(staged, 1)

            stage(0, False)
            with pool.Fori(1, NP) as i:
                pool.wait_ge(ready, 1)
                pool.wait_ge(y_made, i)
                pool.wait_ge(x_ready, i * 4)
                stage(i, False)
            pool.wait_ge(y_made, NP)
            pool.wait_ge(x_ready, NP * 4)
            stage(NP, True)
            pool.wait_ge(staged, 5 * NT + 1)
            pool.wait_ge(masked, 2)
            diagonal = CTm[:, :].rearrange("p (b x) -> p b x", b=NSEQ)[:, :, 0:LSEQ]
            pool.tensor_copy(diagonal, xt[:, 5, :].rearrange("p (b i) -> p b i", b=NSEQ)).then_inc(masked, 1)

        @block.tensor
        def _(pe):
            def tile(i, sampled, first):
                w = 1 if sampled else 0
                pe.wait_ge(staged, i * 5 + 6)
                if not first:
                    pe.wait_ge(y_step, i * 3)
                pe.matmul(cs[:, 0:H], m.upto[:, w, :], das[:, :], start=True, stop=True)
                pe.matmul(cs[:, H:], m.later[:, w, :], das[:, :], start=True, stop=True).then_inc(cum_made, 1)
                for h in range(H):
                    mm = pe.matmul(rows[:, h, :], das[:, h:h + 1].broadcast_to([P, P]), m.upto[:, w, :],
                                   start=True, stop=True)
                mm.then_inc(rows_made, 1)
                pe.matmul(cb, xt[:, 4, :], CTg[:, :, :], start=True, stop=True)
                for j in range(4):
                    pe.transpose(xsP[:, j * P:(j + 1) * P], xt[:, j, :], m.ident[:, :])
                pe.transpose(bP, xt[:, 4, :], m.ident[:, :]).then_inc(cb_made, 1)
                pe.wait_ge(w_ready, i + 1)
                pe.wait_ge(x_ready, i * 4 + 3)
                for h in range(H):
                    pe.matmul(yd[:, h * HD:(h + 1) * HD], W[:, h, :], xdt[:, h, :], start=True, stop=True)
                if sampled:
                    pe.wait_ge(masked, 3)
                    pe.wait_ge(st_in, 32)
                    for b in range(NSEQ):
                        mm = pe.matmul(yo[:, :], CTm[:, b * P:(b + 1) * P], sst[:, b, :],
                                       start=(b == 0), stop=(b == NSEQ - 1))
                    mm.then_inc(y_made, 1)
                    pe.wait_ge(bm_ready, 1)
                    pe.wait_ge(x_ready, 4 * NT)
                    for b in range(NSEQ):
                        if b >= 2:
                            pe.wait_ge(s_taken, 2 * (b - 1))
                        pe.matmul(Spair[b % 2][:, :], Bm[:, b, :], xdte[:, :, :].rearrange("p h d -> p (h d)"),
                                  start=True, stop=True).then_inc(s_made, 1)
                else:
                    pe.wait_ge(state_step, i * 4 + 1)
                    pe.matmul(yo[:, :], xt[:, 5, :], state[:, :], start=True, stop=True)
                    pe.matmul(S[:, :], Bn[:, :], xdte[:, :, :].rearrange("p h d -> p (h d)"),
                              start=True, stop=True).then_inc(y_made, 1)

            tile(0, False, True)
            with pe.Fori(1, NP) as i:
                tile(i, False, False)
            tile(NP, True, False)

        @block.scalar
        def _(act):
            act.activation(a8[:, :], m.a_log[:, :], ACT.Exp).then_inc(dt_act, 1)
            act.activation(sp[:, :], flat(m.dt), ACT.Abs).then_inc(dt_act, 1)
            act.wait_ge(dt_act, 2)
            act.activation(sp[:, :], sp[:, :], ACT.Exp, scale=-1.0).then_inc(dt_act, 1)
            act.wait_ge(dt_act, 3)
            act.activation(sp[:, :], sp[:, :], ACT.Ln, bias=1.0).then_inc(dt_act, 1)

            def tile(i, sampled, first):
                act.wait_ge(seg_step, i * 4 + 1)
                if not first:
                    act.wait_ge(y_step, i * 3)
                    act.wait_ge(x_ready, i * 4)
                    act.wait_ge(state_step, i * 4 + 1)
                act.activation(grow[:, :, :].rearrange("p a h -> p (a h)"), cum[:, :], ACT.Exp).then_inc(act_done, 1)
                act.wait_ge(seg_step, i * 4 + 3)
                n = NSEQ if sampled else 1
                act.activation(cdec[:, :, 0:n], lastc[:, :, 0:n], ACT.Exp).then_inc(act_done, 1)
                act.wait_ge(seg_step, i * 4 + 4)
                if not first:
                    act.wait_ge(w_ready, i)
                act.activation(dec[:, :, :], seg[:, :, :], ACT.Exp).then_inc(act_done, 1)

            tile(0, False, True)
            with act.Fori(1, NP) as i:
                tile(i, False, False)
            tile(NP, True, False)
            act.activation(m.zN[:, :, :], m.zN[:, :, :], ACT.Silu).then_inc(gate_silu, 1)

        @block.vector
        def _(dve):
            dve.wait_ge(dt_act, 4)
            dve.scalar_tensor_tensor(flat(m.dt), flat(m.dt), 0.0, sp[:, :], ALU.max, ALU.add).then_inc(dt_step, 1)
            dve.wait_ge(dt_step, 1)
            dve.scalar_tensor_tensor(dtA[:, :, :], m.dt[:, :, :], -1.0, spread(a8[:, :], 1, NT), ALU.mult,
                                     ALU.mult).then_inc(ready, 1)

            def tile(i, sampled, first):
                w = 1 if sampled else 0
                dve.wait_ge(cum_made, i + 1)
                if not first:
                    dve.wait_ge(act_done, i * 3)
                dve.tensor_copy(cum[:, :], cs).then_inc(seg_step, 1)
                dve.wait_ge(rows_made, i + 1)
                dve.wait_ge(seg_step, i * 4 + 1)
                dve.tensor_tensor(seg[:, :, :], rows[:, :, :], spread(cum[:, 0:H], 2, P), ALU.subtract
                                  ).then_inc(seg_step, 1)
                if sampled:
                    dve.tensor_copy(lastc[:, :, :], rows[:, :, LSEQ - 1:P:LSEQ]).then_inc(seg_step, 1)
                else:
                    dve.tensor_copy(lastc[:, :, 0], rows[:, :, P - 1]).then_inc(seg_step, 1)
                dve.wait_ge(seg_step, i * 4 + 2)
                dve.tensor_tensor(seg[:, :, :], seg[:, :, :], spread(m.hide_ssd[:, w, :], 1, H), ALU.min
                                  ).then_inc(seg_step, 1)
                dve.wait_ge(cb_made, i + 1)
                dve.wait_ge(staged, i * 5 + 6)
                xs = xsP[:, :].rearrange("p (h d) -> p h d", h=H)
                dve.tensor_tensor(xdt[:, :, :], xs, spread(dts[:, :], 2, HD), ALU.mult).then_inc(x_ready, 1)
                dve.tensor_copy(Bn[:, :], bP).then_inc(x_ready, 1)
                dve.wait_ge(act_done, i * 3 + 1)
                dve.wait_ge(x_ready, i * 4 + 1)
                dve.tensor_tensor(xdte[:, :, :], xdt[:, :, :], spread(grow[:, 1, :], 2, HD), ALU.mult
                                  ).then_inc(x_ready, 1)
                if not first:
                    dve.wait_ge(y_step, i * 3)
                dve.tensor_tensor(xD[:, :, :], xs, spread(m.d_skip[:, :], 2, HD), ALU.mult).then_inc(x_ready, 1)
                dve.wait_ge(act_done, i * 3 + 3)
                for g in range(2):
                    hs = slice(4 * g, 4 * g + 4)
                    op = dve.tensor_tensor(W[:, hs, :], dec[:, hs, :], spread(cb[:, g, :], 1, 4), ALU.mult)
                op.then_inc(w_ready, 1)
                if sampled:
                    dve.wait_ge(x_ready, 4 * NP + 2)
                    dve.tensor_tensor(Bm[:, :, :], spread(Bn[:, :], 1, NSEQ), spread(m.same[:, 0:P:LSEQ], 2, P),
                                      ALU.mult).then_inc(bm_ready, 1)
                dve.wait_ge(y_made, i + 1)
                out = (m.oN[:, NP, 512:] if sampled else
                       m.oN[:, ds(i, 1), 512:].rearrange("p a n -> p (a n)")).rearrange("p (h d) -> p h d", h=H)
                by_head = lambda v: v[:, :].rearrange("p (h d) -> p h d", h=H)
                dve.tensor_tensor(out, by_head(yo), spread(grow[:, 0, :], 2, HD), ALU.mult).then_inc(y_step, 1)
                dve.wait_ge(y_step, i * 3 + 1)
                dve.tensor_tensor(out, out, by_head(yd), ALU.add).then_inc(y_step, 1)
                dve.wait_ge(y_step, i * 3 + 2)
                dve.wait_ge(x_ready, i * 4 + 4)
                dve.tensor_tensor(out, out, xD[:, :, :], ALU.add).then_inc(y_step, 1)
                if not sampled:
                    for step in range(2):
                        for g in range(2):
                            r = slice(64 * g, 64 * g + 64)
                            cols = slice(g * 256, (g + 1) * 256)
                            st = state[r, cols].rearrange("p (k d) -> p k d", k=4)
                            if step == 0:
                                dve.tensor_tensor(st, st, spread(cdec[r, 4 * g:4 * g + 4, 0], 2, HD), ALU.mult
                                                  ).then_inc(state_step, 1)
                            else:
                                dve.wait_ge(state_step, i * 4 + (2 + g))
                                dve.tensor_tensor(state[r, cols], state[r, cols], S[r, cols], ALU.add
                                                  ).then_inc(state_step, 1)

            dve.wait_ge(state_step, 1)
            tile(0, False, True)
            with dve.Fori(1, NP) as i:
                tile(i, False, False)
            tile(NP, True, False)
            for g in range(2):
                r = slice(64 * g, 64 * g + 64)
                st = own(sst, g).rearrange("p b (k d) -> p b k d", k=4)
                by_seq = cdec[r, 4 * g:4 * g + 4, :].rearrange("p k b -> p b k")
                dve.tensor_tensor(st, st, spread(by_seq, 3, HD), ALU.mult).then_inc(aged, 1)
            dve.wait_ge(aged, 2)
            for b in range(NSEQ):
                dve.wait_ge(s_made, b + 1)
                for g in range(2):
                    r, cols = slice(64 * g, 64 * g + 64), slice(g * 256, (g + 1) * 256)
                    dve.tensor_tensor(sst[r, b, cols], sst[r, b, cols], Spair[b % 2][r, cols], ALU.add
                                      ).then_inc(s_taken, 1)
            dve.wait_ge(gate_silu, 1)
            dve.wait_ge(y_step, 3 * NT)
            dve.tensor_tensor(m.oN[:, :, 512:], m.oN[:, :, 512:], m.zN[:, :, :], ALU.mult).then_inc(gated, 1)


def attend(nc, m, T, sem, sb, psctx):
    m.sp_new = sb("sp_new", [P, H, P])
    attend_own(nc, m, sem, sb, psctx)
    attend_past(nc, m, T, sem, sb, psctx)


def attend_own(nc, m, sem, sb, psctx):
    ND = NT * P
    OFF = {0: (ND, 3), 1: (ND + 3 * P, 2), 2: (ND + 5 * P, 1)}
    NW = ND + 6 * P
    SC = HD ** -0.5
    kS = sb("kS", [P, TOK])
    qB = sb("qB", [P, 2, TOK])
    with scope(nc.sbuf_tensor) as tmp, psctx() as ps:
        z, a, w = (tmp(n, [P, 2, NW]) for n in ("own_z", "own_a", "own_w"))
        zP, SP = ps("own_zP", [P, 1536]), ps("own_SP", [P, 1536])
        oP = ps("own_oP", [P, 2, 512])
        zeroed, staged = sem("own_zeroed"), sem("own_staged")
        z_made, z_taken, ln_step, sp_step = (sem("own_" + n) for n in ("zmade", "ztaken", "lnstep", "spstep"))
        s_made, arg_step, w_done, o_made, o_taken = (sem("own_" + n) for n in ("smade", "argstep", "wdone", "omade", "otaken"))
        with nc.Block() as block:
            @block.gpsimd
            def _(pool):
                pool.memset(qB[:, :, :], 0.0).then_inc(zeroed, 1)
                pool.wait_ge(zeroed, 1)

                def stage(i):
                    pool.tensor_copy(kS[:, :], m.qkT[:, ds(i + 4, 1), :].rearrange("p a n -> p (a n)")).then_inc(staged, 1)
                    for g in range(2):
                        r = slice(64 * g, 64 * g + 64)
                        pool.wait_ge(zeroed, 1)
                        pool.wait_ge(staged, i * 3 + (g + 1))
                        pool.tensor_copy(qB[r, g, :], m.qkT[r, ds(i, 1), :].rearrange("p a n -> p (a n)")).then_inc(staged, 1)

                stage(0)
                with pool.Fori(1, 4) as i:
                    pool.wait_ge(zeroed, 1)
                    pool.wait_ge(z_made, i * 2)
                    stage(i)

            @block.tensor
            def _(pe):
                def pair(i, first):
                    pe.wait_ge(staged, i * 3 + 3)
                    for s in range(2):
                        if s or not first:
                            pe.wait_ge(z_taken, i * 2 + s)
                        for j in range(NT):
                            c = slice(j * P, (j + 1) * P)
                            mm = pe.matmul(zP[:, c], kS[:, c], qB[:, s, c], start=True, stop=True)
                            if j in OFF:
                                at, n = OFF[j]
                                mm = pe.matmul(zP[:, at:at + n * P], kS[:, c], qB[:, s, (j + 1) * P:(j + 1 + n) * P],
                                               start=True, stop=True)
                        mm.then_inc(z_made, 1)
                    for s in range(2):
                        pe.wait_ge(sp_step, i * 4 + (2 * s + 2))
                        if s or not first:
                            pe.wait_ge(arg_step, i * 4 + 2 * s)
                        sp = a[:, s, :]
                        pe.matmul(SP[:, 0:512], m.from_[:, :], sp[:, 0:512], start=True, stop=True)
                        pe.matmul(SP[:, 512:ND], m.from_[:, :], sp[:, 512:ND], start=True, stop=True)
                        for j, (at, n) in OFF.items():
                            pe.matmul(SP[:, at:at + n * P], m.from_[:, :], sp[:, at:at + n * P], start=True, stop=False)
                            for jj in range(j + 1, 4):
                                o = at + (jj - j - 1) * P
                                mm = pe.matmul(SP[:, o:o + P], m.ones[:, :], sp[:, jj * P:(jj + 1) * P],
                                               start=False, stop=(jj == 3))
                                if jj in OFF:
                                    a2, n2 = OFF[jj]
                                    mm = pe.matmul(SP[:, o + P:o + P + n2 * P], m.ones[:, :], sp[:, a2:a2 + n2 * P],
                                                   start=False, stop=False)
                        mm.then_inc(s_made, 1)
                    for s in range(2):
                        pe.wait_ge(w_done, i * 2 + (s + 1))
                        if not first:
                            pe.wait_ge(o_taken, i * 2 - (1 - s))
                        for q in range(NT):
                            keys = range(q + 1) if q < 4 else [4]
                            for j in keys:
                                c = j * P if j == q else OFF[j][0] + (q - j - 1) * P
                                mm = pe.matmul(oP[:, s, q * HD:(q + 1) * HD], w[:, s, c:c + P],
                                               m.vN[:, j, ds(i * 128 + s * HD, HD)], start=(j == keys[0]), stop=(j == q))
                        mm.then_inc(o_made, 1)
                pair(0, True)
                with pe.Fori(1, 4) as i:
                    pair(i, False)

            @block.scalar
            def _(act):
                def pair(i, first):
                    for s in range(2):
                        act.wait_ge(z_taken, i * 2 + (s + 1))
                        if not first:
                            act.wait_ge(s_made, i * 2 - (1 - s))
                            act.wait_ge(arg_step, i * 4 + (2 * s - 2))
                        act.activation(a[:, s, :], z[:, s, :], ACT.Abs).then_inc(ln_step, 1)
                        act.wait_ge(ln_step, i * 6 + (3 * s + 1))
                        act.activation(a[:, s, :], a[:, s, :], ACT.Exp, scale=-1.0).then_inc(ln_step, 1)
                        act.wait_ge(ln_step, i * 6 + (3 * s + 2))
                        act.activation(a[:, s, :], a[:, s, :], ACT.Ln, bias=1.0).then_inc(ln_step, 1)
                    for s in range(2):
                        act.wait_ge(arg_step, i * 4 + (2 * s + 2))
                        if not first:
                            act.wait_ge(o_made, i * 2 - (1 - s))
                        act.activation(w[:, s, :], z[:, s, :], ACT.Exp).then_inc(w_done, 1)
                pair(0, True)
                with act.Fori(1, 4) as i:
                    pair(i, False)

            @block.vector
            def _(dve):
                def pair(i, first):
                    for s in range(2):
                        dve.wait_ge(z_made, i * 2 + (s + 1))
                        if not first:
                            dve.wait_ge(w_done, i * 2 - (1 - s))
                        dve.tensor_scalar(z[:, s, :], zP[:, 0:NW], SC, None, ALU.mult).then_inc(z_taken, 1)
                    for s in range(2):
                        dve.wait_ge(ln_step, i * 6 + (3 * s + 3))
                        dve.scalar_tensor_tensor(a[:, s, :], z[:, s, :], 0.0, a[:, s, :], ALU.max, ALU.add
                                                 ).then_inc(sp_step, 1)
                        dve.wait_ge(sp_step, i * 4 + (2 * s + 1))
                        seen = m.seen[:, :, :].rearrange("p t q -> p (t q)")
                        dve.tensor_tensor(a[:, s, 0:ND], a[:, s, 0:ND], seen, ALU.mult).then_inc(sp_step, 1)
                        dve.wait_ge(sp_step, i * 4 + (2 * s + 2))
                        dve.tensor_copy(m.sp_new[:, ds(i * 2 + s, 1), :].rearrange("p a n -> p (a n)"),
                                        a[:, s, ND - P:ND])
                    for s in range(2):
                        dve.wait_ge(s_made, i * 2 + (s + 1))
                        dve.tensor_tensor(z[:, s, :], z[:, s, :], SP[:, 0:NW], ALU.subtract).then_inc(arg_step, 1)
                        dve.wait_ge(arg_step, i * 4 + (2 * s + 1))
                        hide = m.hide[:, :, :].rearrange("p t q -> p (t q)")
                        dve.tensor_tensor(z[:, s, 0:ND], z[:, s, 0:ND], hide, ALU.min).then_inc(arg_step, 1)
                    for s in range(2):
                        dve.wait_ge(o_made, i * 2 + (s + 1))
                        dve.tensor_copy(m.oN[:, :, ds(i * 128 + s * HD, HD)],
                                        oP[:, s, 0:NT * HD].rearrange("p (t d) -> p t d", t=NT)).then_inc(o_taken, 1)
                pair(0, True)
                with dve.Fori(1, 4) as i:
                    pair(i, False)


def attend_past(nc, m, T, sem, sb, psctx):
    NJ = PAST // P
    SC = HD ** -0.5
    with scope(nc.sbuf_tensor) as tmp, psctx() as ps:
        kT, vb = tmp("past_k", [P, 2, 4, PAST]), tmp("past_v", [P, 2, NJ, 512])
        qB = tmp("past_q", [P, 4, 2, P])
        z, a, w = (tmp(n, [P, 2, NJ, P]) for n in ("past_z", "past_a", "past_w"))
        oTs = tmp("past_oT", [HD, H, P])
        zP, SP, oP = (ps(n, [P, 2, 512]) for n in ("past_zP", "past_SP", "past_oP"))
        back = ps("past_back", [P, 512])
        zeroed, q_ready = sem("past_zeroed"), sem("past_q_ready")
        kv_in = [sem(f"past_in{s}") for s in range(2)]
        z_made, z_taken, ln_step, sp_done = (sem("past_" + n) for n in ("zmade", "ztaken", "lnstep", "spdone"))
        s_made, arg_done, w_done, o_made, o_taken = (sem("past_" + n) for n in ("smade", "argdone", "wdone", "omade", "otaken"))
        back_made, added = sem("past_back_made"), sem("past_added")
        with nc.Block() as block:
            @block.sync
            def _(sp):
                def load(i, s):
                    one = lambda t: t[ds(i * 2 + s, 1)] if not isinstance(i, int) else t[2 * i + s:2 * i + s + 1]
                    sp.dma_start(kT[:, s, :, :], one(T["cache_kT"]).rearrange("a p k n -> (a p) k n")).then_inc(kv_in[s], 16)
                    sp.dma_start(vb[:, s, :, :], one(T["cache_v"]).rearrange("a (j p) n -> p (a j) n", p=P)
                                 ).then_inc(kv_in[s], 16)
                for s in range(2):
                    load(0, s)
                with sp.Fori(1, NSEQ // 2) as i:
                    for s in range(2):
                        sp.wait_ge(o_made, i * 2 - (1 - s))
                        load(i, s)

            @block.gpsimd
            def _(pool):
                pool.memset(qB[:, :, :, :], 0.0).then_inc(zeroed, 1)
                pool.wait_ge(zeroed, 1)
                for g in range(2):
                    r = slice(64 * g, 64 * g + 64)
                    if g:
                        pool.wait_ge(q_ready, g)
                    pool.tensor_copy(qB[r, :, g, :], m.qkT[r, 0:4, SEQ:TOK]).then_inc(q_ready, 1)

            @block.tensor
            def _(pe):
                pe.wait_ge(q_ready, 2)

                def pair(i, first):
                    for s in range(2):
                        pe.wait_ge(kv_in[s], i * 32 + 32)
                        if not first:
                            pe.wait_ge(z_taken, i * 2 - (1 - s))
                        for j in range(NJ):
                            for k in range(4):
                                mm = pe.matmul(zP[:, s, j * P + k * 32:j * P + k * 32 + 32], kT[:, s, k, j * P:(j + 1) * P],
                                               qB[:, k, :, ds(i * 32 + s * LSEQ, LSEQ)], start=True, stop=True)
                        mm.then_inc(z_made, 1)
                    for s in range(2):
                        pe.wait_ge(sp_done, i * 2 + (s + 1))
                        if not first:
                            pe.wait_ge(arg_done, i * 2 - (1 - s))
                        out = SP[:, s, :].rearrange("p (j c) -> p j c", j=NJ)
                        pe.matmul(out, m.from_[:, :], a[:, s, :, :], start=True, stop=False)
                        for j in range(1, NJ):
                            pe.matmul(out[:, 0:j, :], m.ones[:, :], spread(a[:, s, j, :], 1, j), start=False, stop=False)
                        for j in range(NJ):
                            mm = pe.matmul(out[:, j, :], m.ones[:, :], m.sp_new[:, :, ds(i * 32 + s * LSEQ, LSEQ)],
                                           start=False, stop=(j == NJ - 1))
                        mm.then_inc(s_made, 1)
                    for s in range(2):
                        pe.wait_ge(w_done, i * 2 + (s + 1))
                        if not first:
                            pe.wait_ge(o_taken, i * 2 - (1 - s))
                        for h in range(H):
                            for j in range(NJ):
                                mm = pe.matmul(oP[0:HD, s, h * LSEQ:(h + 1) * LSEQ], vb[:, s, j, h * HD:(h + 1) * HD],
                                               w[:, s, j, h * LSEQ:(h + 1) * LSEQ], start=(j == 0), stop=(j == NJ - 1))
                        mm.then_inc(o_made, 1)
                pair(0, True)
                with pe.Fori(1, NSEQ // 2) as i:
                    pair(i, False)
                pe.wait_ge(o_taken, NSEQ)
                for h in range(H):
                    mm = pe.transpose(back[:, h * HD:(h + 1) * HD], oTs[:, h, :], m.ident[0:HD, 0:HD])
                mm.then_inc(back_made, 1)

            @block.scalar
            def _(act):
                def pair(i, first):
                    for s in range(2):
                        act.wait_ge(z_taken, i * 2 + (s + 1))
                        if not first:
                            act.wait_ge(s_made, i * 2 - (1 - s))
                        act.activation(a[:, s, :, :], z[:, s, :, :], ACT.Abs).then_inc(ln_step, 1)
                        act.wait_ge(ln_step, i * 6 + (3 * s + 1))
                        act.activation(a[:, s, :, :], a[:, s, :, :], ACT.Exp, scale=-1.0).then_inc(ln_step, 1)
                        act.wait_ge(ln_step, i * 6 + (3 * s + 2))
                        act.activation(a[:, s, :, :], a[:, s, :, :], ACT.Ln, bias=1.0).then_inc(ln_step, 1)
                    for s in range(2):
                        act.wait_ge(arg_done, i * 2 + (s + 1))
                        if not first:
                            act.wait_ge(o_made, i * 2 - (1 - s))
                        act.activation(w[:, s, :, :], z[:, s, :, :], ACT.Exp).then_inc(w_done, 1)
                pair(0, True)
                with act.Fori(1, NSEQ // 2) as i:
                    pair(i, False)

            @block.vector
            def _(dve):
                def pair(i, first):
                    flat = lambda t, s: t[:, s, :, :].rearrange("p j c -> p (j c)")
                    for s in range(2):
                        dve.wait_ge(z_made, i * 2 + (s + 1))
                        if not first:
                            dve.wait_ge(w_done, i * 2 - (1 - s))
                        dve.tensor_scalar(flat(z, s), zP[:, s, :], SC, None, ALU.mult).then_inc(z_taken, 1)
                    for s in range(2):
                        dve.wait_ge(ln_step, i * 6 + (3 * s + 3))
                        dve.scalar_tensor_tensor(flat(a, s), flat(z, s), 0.0, flat(a, s), ALU.max, ALU.add
                                                 ).then_inc(sp_done, 1)
                    for s in range(2):
                        dve.wait_ge(s_made, i * 2 + (s + 1))
                        dve.tensor_tensor(flat(z, s), flat(z, s), SP[:, s, :], ALU.subtract).then_inc(arg_done, 1)
                    for s in range(2):
                        dve.wait_ge(o_made, i * 2 + (s + 1))
                        dve.tensor_copy(oTs[:, :, ds(i * 32 + s * LSEQ, LSEQ)],
                                        oP[0:HD, s, 0:P].rearrange("p (h q) -> p h q", h=H)).then_inc(o_taken, 1)
                pair(0, True)
                with dve.Fori(1, NSEQ // 2) as i:
                    pair(i, False)
                dve.wait_ge(back_made, 1)
                dve.tensor_tensor(m.oN[:, NT - 1, 0:512], m.oN[:, NT - 1, 0:512], back[:, :], ALU.add).then_inc(added, 1)


def add_residual(nc, m, T, sem, sb, name, src, base, g_post, gate, store, keep):
    gates = sb(name + "_gates", [P, 2, D])
    post = sb(name + "_post", [P, D])
    junk = sb(name + "_junk", [P, 2, D])
    ld, gate_ready, squared, mean, rstd, step, stored = (
        sem(f"{name}_{n}") for n in ("ld", "gate", "sq", "mean", "rstd", "step", "stored"))
    base_in = [sem(f"{name}_base{t}") for t in range(NT)]
    with nc.Block() as block:
        @block.sync
        def _(sp):
            sp.dma_start(post[:, :], g_post.partition_broadcast(P)).then_inc(ld, 16)
            sp.dma_start(gates[:, 0, :], T["gates"][gate, 0].partition_broadcast(P)).then_inc(ld, 16)
            for b in range(NSEQ):
                sp.dma_start(gates[b * LSEQ:(b + 1) * LSEQ, 1, :],
                             T["gates"][gate, b + 1].partition_broadcast(LSEQ)).then_inc(ld, 16)
            for t in range(NT):
                sp.dma_start(keep[:, t, :], base[t * P:(t + 1) * P, :]).then_inc(base_in[t], 16)
            for t in range(NT):
                sp.wait_ge(step, 2 * t + 2)
                sp.dma_start(store[t * P:(t + 1) * P, :], keep[:, t, :]).then_inc(stored, 16)
            sp.wait_ge(stored, 16 * NT)

        @block.scalar
        def _(act):
            for t in range(NT):
                if t >= 2:
                    act.wait_ge(squared, t - 1)
                act.activation(junk[:, t % 2, :], src[:, t, :], ACT.Square,
                               accum_out=m.stat[:, t:t + 1]).then_inc(squared, 1)

        @block.gpsimd
        def _(pool):
            pool.wait_ge(mean, 1)
            pool.tensor_tensor(m.rstd[:, :], m.stat[:, :], m.mhalf[:, 0:NT], ALU.pow).then_inc(rstd, 1)

        @block.vector
        def _(dve):
            dve.wait_ge(ld, 16 * (2 + NSEQ))
            dve.tensor_tensor(gates[:, :, :], gates[:, :, :], spread(post[:, :], 1, 2), ALU.mult).then_inc(gate_ready, 1)
            dve.wait_ge(squared, NT)
            dve.tensor_scalar(m.stat[:, :], m.stat[:, :], 1.0 / D, EPS, ALU.mult, ALU.add).then_inc(mean, 1)
            dve.wait_ge(rstd, 1)
            dve.wait_ge(gate_ready, 1)
            for t in range(NT):
                dve.scalar_tensor_tensor(src[:, t, :], src[:, t, :], m.rstd[:, t:t + 1], gates[:, t // (NT - 1), :],
                                         ALU.mult, ALU.mult).then_inc(step, 1)
                dve.wait_ge(step, 2 * t + 1)
                dve.wait_ge(base_in[t], 16)
                dve.tensor_tensor(keep[:, t, :], keep[:, t, :], src[:, t, :], ALU.add).then_inc(step, 1)


def mixer_columns(nc, m, T, sem, sb, ps, oT):
    NH = 2 * NT
    g = sb("g_mix", [P, KD])
    junk = sb("mix_junk", [P, 2, 512])
    stat, rstd = sb("mix_stat", [P, NH]), sb("mix_rstd", [P, NH])
    pr, sa = ps("mixc_p", [P, 2, 512]), ps("mixc_s", [P, 2, 512])
    ld, squared, mean, rooted, normed, turned, taken = (
        sem("mixc_" + n) for n in ("ld", "sq", "mean", "rstd", "normed", "turned", "taken"))
    with nc.Block() as block:
        @block.sync
        def _(sp):
            sp.dma_start(g[:, :], T["g_mix"]).then_inc(ld, 16)

        @block.scalar
        def _(act):
            for n in range(NH):
                t, half = n // 2, n % 2
                if n >= 2:
                    act.wait_ge(squared, n - 1)
                act.activation(junk[:, n % 2, :], m.oN[:, t, half * 512:(half + 1) * 512], ACT.Square,
                               accum_out=stat[:, n:n + 1]).then_inc(squared, 1)

        @block.gpsimd
        def _(pool):
            pool.wait_ge(mean, 1)
            pool.tensor_tensor(rstd[:, :], stat[:, :], m.mhalf[:, :], ALU.pow).then_inc(rooted, 1)

        @block.vector
        def _(dve):
            dve.wait_ge(squared, NH)
            dve.tensor_scalar(stat[:, :], stat[:, :], 1.0 / 512, EPS, ALU.mult, ALU.add).then_inc(mean, 1)
            dve.wait_ge(rooted, 1)
            for n in range(NH):
                v = m.oN[:, n // 2, (n % 2) * 512:(n % 2 + 1) * 512]
                dve.tensor_scalar(v, v, rstd[:, n:n + 1], None, ALU.mult).then_inc(normed, 1)
            dve.wait_ge(ld, 16)
            for k in range(KD):
                dve.wait_ge(turned, k + 1)
                dve.tensor_scalar(oT[:, k, 0:SEQ], pr[:, k % 2, :], g[:, k:k + 1], None, ALU.mult).then_inc(taken, 1)
                dve.tensor_scalar(oT[:, k, SEQ:], sa[:, k % 2, 0:P], g[:, k:k + 1], None, ALU.mult).then_inc(taken, 1)

        @block.tensor
        def _(pe):
            pe.wait_ge(normed, NH)
            for k in range(KD):
                if k >= 2:
                    pe.wait_ge(taken, 2 * (k - 1))
                for t in range(NT):
                    out = pr[:, k % 2, t * P:(t + 1) * P] if t < NT - 1 else sa[:, k % 2, 0:P]
                    mm = pe.transpose(out, m.oN[:, t, k * P:(k + 1) * P], m.ident[:, :])
                mm.then_inc(turned, 1)


def mix(nc, m, T, sem, sb, psctx):
    with scope(nc.sbuf_tensor) as tmp:
        x1 = tmp("x1", [P, NT, D])
        mx = tmp("mx", [P, NT, D])
        with scope(nc.sbuf_tensor) as tmp2:
            oT = tmp2("oT", [P, KD, TOK])
            w = tmp2("w_out", [P, KD, D])
            with psctx() as ps:
                mixer_columns(nc, m, T, sem, tmp2, ps, oT)
            w_in, made, taken = [sem(f"w_out{k}") for k in range(KD)], sem("mix_made"), sem("mix_taken")
            with psctx() as ps, nc.Block() as block:
                acc = ps("mix_ps", [P, 2, 2, 512])

                @block.sync
                def _(sp):
                    for k in range(KD):
                        sp.dma_start(w[:, k, :], T["w_out"][k * P:(k + 1) * P, :]).then_inc(w_in[k], 16)

                @block.tensor
                def _(pe):
                    for t in range(NT):
                        if t >= 2:
                            pe.wait_ge(taken, t - 1)
                        for k in range(KD):
                            if t == 0:
                                pe.wait_ge(w_in[k], 16)
                            for h in range(2):
                                mm = pe.matmul(acc[:, t % 2, h, :], oT[:, k, t * P:(t + 1) * P],
                                               w[:, k, h * 512:(h + 1) * 512], start=(k == 0), stop=(k == KD - 1))
                        mm.then_inc(made, 1)

                @block.scalar
                def _(act):
                    for t in range(NT):
                        act.wait_ge(made, t + 1)
                        act.copy(mx[:, t, :].rearrange("p (h n) -> p h n", h=2), acc[:, t % 2, :, :]).then_inc(taken, 1)
        with scope(nc.sbuf_tensor) as tmp2:
            add_residual(nc, m, T, sem, tmp2, "res1", mx, T["x"], T["g_post_mix"], 0, T["x1"], x1)
        m.junk = mx
        with scope(nc.sbuf_tensor) as tmp2:
            h2T = tmp2("h2T", [P, KD, TOK])
            with psctx() as ps:
                norm_to_columns(nc, m, sem, ps, "n2", None, x1, h2T, 1)
            split, low = sem("h2_split"), sem("h2_low")
            with nc.Block() as block:
                @block.vector
                def _(dve):
                    for k in range(KD):
                        dve.tensor_copy(m.h2h[:, k, :], h2T[:, k, :]).then_inc(split, 1)
                    for k in range(KD):
                        dve.wait_ge(split, k + 1)
                        dve.tensor_tensor(m.h2l[:, k, :], h2T[:, k, :], m.h2h[:, k, :].bitcast(F32), ALU.subtract
                                          ).then_inc(low, 1)

            def sink(act, acc, made, taken):
                with act.Fori(0, 4) as i:
                    for s in range(2):
                        act.wait_ge(made, i * 2 + (s + 1))
                        act.copy(m.qhT[:, ds(i * 2 + s, 1), :].rearrange("p a (h n) -> p (a h) n", h=2),
                                 acc[:, s, :, 0:HALF]).then_inc(taken, 1)
            with psctx() as ps:
                column_products(nc, m, sem, tmp2, ps, "pq", T["w_pq"], 8, h2T, sink)


def route(nc, m, T, sem, sb, psctx):
    NG = 2 * H
    NC = TOPK * TOPK
    skb = sb("skb", [P, 2, NKEY])
    qs = sb("qs", [P, H, P])
    s = sb("s", [P, NG, NKEY])
    top, itop, itopf = sb("top", [P, NG, TOPK]), sb("itop", [P, NG, TOPK], U32), sb("itopf", [P, NG, TOPK])
    cand = sb("cand", [P, H, NC])
    best, ci = sb("best", [P, H, TOPK]), sb("ci", [P, H, TOPK], U32)
    cab, cabf = sb("cab", [P, 2, H, TOPK], U32), sb("cabf", [P, 2, H, TOPK])
    hit = sb("hit", [P, H, TOPK, TOPK])
    picks = sb("picks", [P, 3, H, TOPK])
    zs, rz = sb("zs", [P, H]), sb("rz", [P, H])
    picksT = sb("picksT", [P, 3, P])
    iota16, iota = sb("iota16", [P, TOPK]), sb("iota", [P, NKEY])
    UN = 8
    hot1, hot2 = sb("hot1", [P, UN, NKEY]), sb("hot2", [P, UN, NKEY])
    Gs = sb("Gs", [P, NKEY, P])
    setup, zeroed, keys_in = sem("route_setup"), sem("route_zeroed"), sem("keys_in")
    q_in, s_made, s_taken = sem("rq_in"), sem("rs_made"), sem("rs_taken")
    stepA, stepB, stepC = sem("routeA"), sem("routeB"), sem("routeC")
    exp_done, t_made, t_taken = sem("r_exp"), sem("rt_made"), sem("rt_taken")
    hots, g_made, g_taken, g_out = sem("hots"), sem("g_made"), sem("g_taken"), sem("g_out")
    NA, NB, NCC = 5 * NG + 1, 5 * H + 2, 12
    EV = UN // 4
    STEPS = P // UN
    with psctx() as ps, nc.Block() as block:
        sP = ps("route_s", [P, NG, NKEY])
        tP = ps("route_t", [P, 512])
        gP = ps("route_g", [P, 2, 4, NKEY])

        @block.gpsimd
        def _(pool):
            pool.iota(iota[:, :], pattern=[[1, NKEY]], base=0, channel_multiplier=0,
                      allow_small_or_imprecise_dtypes=True).then_inc(setup, 1)
            pool.iota(iota16[:, :], pattern=[[1, TOPK]], base=0, channel_multiplier=0,
                      allow_small_or_imprecise_dtypes=True).then_inc(setup, 1)
            pool.memset(skb[:, :, :], 0.0).then_inc(zeroed, 1)

        @block.sync
        def _(sp):
            sp.wait_ge(zeroed, 1)
            for c in range(2):
                sp.dma_start(skb[64 * c:64 * c + 64, c, :], T["sub_keys"][64 * c:64 * c + 64, :]).then_inc(keys_in, 16)
            sp.dma_start(qs[:, :, :], m.qhT[:, :, 0:P]).then_inc(q_in, 16)
            with sp.Fori(1, NT) as i:
                sp.wait_ge(s_made, i)
                sp.dma_start(qs[:, :, :], m.qhT[:, :, ds(i * P, P)]).then_inc(q_in, 16)
                sp.wait_ge(g_taken, i * (EV * STEPS) + EV)
                sp.dma_start(T["G"][ds(i - 1, 1)].rearrange("a p j t -> (a p) j t"), Gs[:, :, :]).then_inc(g_out, 16)
            sp.wait_ge(g_taken, NT * EV * STEPS + EV)
            sp.dma_start(T["G"][NT - 1], Gs[:, :, :]).then_inc(g_out, 16)
            sp.wait_ge(g_out, 16 * NT)

        @block.tensor
        def _(pe):
            def scores(i, first):
                pe.wait_ge(q_in, i * 16 + 16)
                if first:
                    pe.wait_ge(keys_in, 32)
                else:
                    pe.wait_ge(s_taken, i)
                for h in range(H):
                    mm = pe.matmul(sP[:, 2 * h:2 * h + 2, :], qs[:, h, :], skb[:, :, :], start=True, stop=True)
                mm.then_inc(s_made, 1)

            def weights(i, first, next_scores):
                pe.wait_ge(stepC, i * NCC + NCC)
                for c in range(3):
                    mm = pe.transpose(tP[:, c * P:(c + 1) * P], picks[:, c, :, :].rearrange("p h r -> p (h r)"), m.ident[:, :])
                mm.then_inc(t_made, 1)
                if next_scores:
                    scores(i + 1, False)
                with pe.Fori(0, STEPS) as q:
                    for u in range(UN):
                        pe.wait_ge(hots, (i * STEPS + q) * UN + (u + 1))
                        if u % 4 == 0:
                            pe.wait_ge(g_taken, (i * STEPS + q) * EV + (u // 4 + 1))
                        mm = pe.matmul(gP[:, u // 4, u % 4, :], hot1[:, u, :], hot2[:, u, :], start=True, stop=True)
                        mm.then_inc(g_made, 1)

            pe.sem_inc(g_made, UN)
            scores(0, True)
            with pe.Fori(0, NT - 1) as i:
                weights(i, False, True)
            weights(NT - 1, False, False)

        @block.scalar
        def _(act):
            def take(i, first):
                act.wait_ge(s_made, i + 1)
                if not first:
                    act.wait_ge(stepA, i * NA)
                act.copy(s[:, :, :], sP[:, :, :]).then_inc(s_taken, 1)

            def weights(i, more):
                act.wait_ge(stepB, i * (NB + 1) + (NB + 1))
                act.activation(best[:, :, :], best[:, :, :], ACT.Exp).then_inc(exp_done, 1)
                act.wait_ge(t_made, i + 1)
                act.copy(picksT[:, :, :].rearrange("p c t -> p (c t)"), tP[:, 0:3 * P]).then_inc(t_taken, 1)
                if more:
                    take(i + 1, False)
                with act.Fori(0, STEPS) as q:
                    for e in range(EV):
                        act.wait_ge(g_made, (i * STEPS + q) * UN + (UN + 4 * (e + 1)))
                        act.copy(Gs[:, :, ds(q * UN + 4 * e, 4)].rearrange("p j t -> p t j"), gP[:, e, :, :]
                                 ).then_inc(g_taken, 1)
            act.sem_inc(g_taken, EV)
            take(0, True)
            weights(0, True)
            with act.Fori(1, NT - 1) as i:
                act.wait_ge(g_out, i * 16)
                weights(i, True)
            act.wait_ge(g_out, (NT - 1) * 16)
            weights(NT - 1, False)

        @block.vector
        def _(dve):
            def after(what, value):
                value = value if isinstance(value, int) else dve.to_reg(value)
                dve.wait_ge(setup, 2)
                dve.wait_ge(what, value)

            def tile(i, first):
                a0, b0, c0 = i * NA, i * (NB + 1), i * NCC
                after(s_taken, i + 1)
                for g in range(NG):
                    dve.max(top[:, g, 0:8], s[:, g, :]).then_inc(stepA, 1)
                after(stepA, a0 + NG)
                for g in range(NG):
                    dve.max_index(itop[:, g, 0:8], top[:, g, 0:8], s[:, g, :]).then_inc(stepA, 1)
                after(stepA, a0 + 2 * NG)
                for g in range(NG):
                    dve.match_replace(s[:, g, :], top[:, g, 0:8], s[:, g, :], -3e38).then_inc(stepA, 1)
                after(stepA, a0 + 3 * NG)
                for g in range(NG):
                    dve.max(top[:, g, 8:16], s[:, g, :]).then_inc(stepA, 1)
                after(stepA, a0 + 4 * NG)
                for g in range(NG):
                    dve.max_index(itop[:, g, 8:16], top[:, g, 8:16], s[:, g, :]).then_inc(stepA, 1)
                dve.wait_ge(stepA, a0 + 5 * NG)
                dve.tensor_copy(itopf[:, :, :], itop[:, :, :]).then_inc(stepA, 1)
                dve.tensor_tensor(cand[:, :, :].rearrange("p h (a b) -> p h a b", a=TOPK),
                                  spread(top[:, 0:NG:2, :], 3, TOPK), spread(top[:, 1:NG:2, :], 2, TOPK), ALU.add
                                  ).then_inc(stepB, 1)
                after(stepB, b0 + 1)
                for h in range(H):
                    dve.max(best[:, h, 0:8], cand[:, h, :]).then_inc(stepB, 1)
                after(stepB, b0 + (1 + H))
                for h in range(H):
                    dve.max_index(ci[:, h, 0:8], best[:, h, 0:8], cand[:, h, :]).then_inc(stepB, 1)
                after(stepB, b0 + (1 + 2 * H))
                for h in range(H):
                    dve.match_replace(cand[:, h, :], best[:, h, 0:8], cand[:, h, :], -3e38).then_inc(stepB, 1)
                after(stepB, b0 + (1 + 3 * H))
                for h in range(H):
                    dve.max(best[:, h, 8:16], cand[:, h, :]).then_inc(stepB, 1)
                after(stepB, b0 + (1 + 4 * H))
                for h in range(H):
                    dve.max_index(ci[:, h, 8:16], best[:, h, 8:16], cand[:, h, :]).then_inc(stepB, 1)
                dve.tensor_copy(zs[:, :], best[:, :, 0]).then_inc(stepB, 1)
                dve.wait_ge(stepB, b0 + NB)
                dve.tensor_tensor(best[:, :, :], best[:, :, :], spread(zs[:, :], 2, TOPK), ALU.subtract
                                  ).then_inc(stepB, 1)
                dve.tensor_scalar(cab[:, 0, :, :], ci[:, :, :], 4, None, ALU.logical_shift_right).then_inc(stepC, 1)
                dve.tensor_scalar(cab[:, 1, :, :], ci[:, :, :], 15, None, ALU.bitwise_and).then_inc(stepC, 1)
                dve.wait_ge(stepC, c0 + 2)
                dve.tensor_copy(cabf[:, :, :, :], cab[:, :, :, :]).then_inc(stepC, 1)
                dve.wait_ge(stepA, a0 + NA)
                if not first:
                    dve.wait_ge(t_made, i)
                for c in range(2):
                    dve.wait_ge(stepC, c0 + (3 + 3 * c))
                    dve.tensor_tensor(hit[:, :, :, :], spread(cabf[:, c, :, :], 3, TOPK),
                                      spread(spread(iota16[:, :], 1, TOPK), 1, H), ALU.is_equal).then_inc(stepC, 1)
                    dve.wait_ge(stepC, c0 + (4 + 3 * c))
                    dve.tensor_tensor(hit[:, :, :, :], hit[:, :, :, :], spread(itopf[:, c:NG:2, :], 2, TOPK), ALU.mult
                                      ).then_inc(stepC, 1)
                    dve.wait_ge(stepC, c0 + (5 + 3 * c))
                    dve.tensor_reduce(picks[:, c, :, :], hit[:, :, :, :], AX, ALU.add).then_inc(stepC, 1)
                dve.wait_ge(exp_done, i + 1)
                dve.tensor_reduce(zs[:, :], best[:, :, :], AX, ALU.add).then_inc(stepC, 1)
                dve.wait_ge(stepC, c0 + 10)
                dve.reciprocal(rz[:, :], zs[:, :]).then_inc(stepC, 1)
                dve.wait_ge(stepC, c0 + 11)
                dve.tensor_tensor(picks[:, 2, :, :], best[:, :, :], spread(rz[:, :], 2, TOPK), ALU.mult
                                  ).then_inc(stepC, 1)
                after(t_taken, i + 1)
                with dve.Fori(0, STEPS) as q:
                    for u in range(UN):
                        dve.wait_ge(g_made, (i * STEPS + q) * UN + (u + 1))
                        t = ds(q * UN + u, 1)
                        dve.tensor_scalar(hot1[:, u, :], iota[:, :], picksT[:, 0, t], None, ALU.is_equal)
                        dve.tensor_scalar(hot2[:, u, :], iota[:, :], picksT[:, 1, t], picksT[:, 2, t],
                                          ALU.is_equal, ALU.mult).then_inc(hots, 1)

            tile(0, True)
            with dve.Fori(1, NT) as i:
                tile(i, False)


def experts(nc, m, T, sem, sb, psctx):
    GB = 4
    NGR = NKEY // GB
    Y = m.oN
    with scope(nc.sbuf_tensor) as tmp, psctx() as ps, nc.Block() as block:
        ur, uh, ul = tmp("ur", [P, 2, KD, P]), tmp("uh", [P, 2, KD, P], F32R), tmp("ul", [P, 2, KD, P], F32R)
        vr, vh, vl = tmp("vr", [P, 2, D]), tmp("vh", [P, GB, D], F32R), tmp("vl", [P, GB, D], F32R)
        gr = tmp("gr", [P, NT, GB, P])
        ga = tmp("ga", [P, 2, TOK])
        ah, al = tmp("ah", [P, GB, TOK], F32R), tmp("al", [P, GB, TOK], F32R)
        hP = ps("ex_h", [P, 2, 2, 512])
        yP = ps("ex_y", [P, 4, 512])
        u_in, v_in = [sem(f"u_in{n}") for n in range(2)], [sem(f"v_in{n}") for n in range(2)]
        g_in = sem("G_in")
        uh_done, ul_done, vh_done, vl_done = sem("uh_done"), sem("ul_done"), sem("vh_done"), sem("vl_done")
        h_made, gelu_done, weighted, ah_done, al_done = (sem("ex_" + n) for n in ("hmade", "gelu", "weighted", "ah", "al"))
        y_made, y_taken, y_zero = sem("ex_ymade"), sem("ex_ytaken"), sem("ex_yzero")
        NY = 2 * NT
        YB = [max(y for y in range(NY) if y % 4 == a) for a in range(4)]
        Glayout = T["G"].rearrange("t p j n -> p t j n")

        @block.sync
        def _(sp):
            def load_u(n, s, first=False):
                if not first:
                    sp.wait_ge(ul_done, n - 1)
                    sp.wait_ge(uh_done, n - 1)
                src = T["uT"][n] if isinstance(n, int) else T["uT"][ds(n, 1)].rearrange("a p k c -> (a p) k c")
                sp.dma_start(ur[:, s, :, :], src).then_inc(u_in[s], 16)

            def load_g(g, first=False):
                if not first:
                    sp.wait_ge(weighted, g * GB)
                for t in range(NT):
                    sp.dma_start(gr[:, t, :, :], Glayout[:, t, ds(g * GB, GB), :]).then_inc(g_in, 16)

            for n in range(2):
                load_u(n, n, True)
            load_g(0, True)
            with sp.Fori(0, NGR - 1) as g:
                for s in range(GB):
                    load_u(g * GB + (s + 2), s % 2)
                load_g(g + 1)
            for s in range(GB - 2):
                load_u(NKEY - 2 + s, s % 2)

        @block.gpsimd
        def _(pool):
            def load_v(n, s, first=False):
                if not first:
                    pool.wait_ge(vl_done, n - 1)
                    pool.wait_ge(vh_done, n - 1)
                src = T["v_tab"][n] if isinstance(n, int) else T["v_tab"][ds(n, 1)].rearrange("a p n -> (a p) n")
                pool.dma_start(vr[:, s, :], src).then_inc(v_in[s], 16)

            for n in range(2):
                load_v(n, n, True)
            with pool.Fori(1, NKEY // 2) as i:
                for s in range(2):
                    load_v(i * 2 + s, s)

        @block.tensor
        def _(pe):
            def hidden(n, s, first=False):
                pe.wait_ge(ul_done, n + 1)
                pe.wait_ge(uh_done, n + 1)
                if not first:
                    pe.wait_ge(gelu_done, n - 1)
                for k in range(KD):
                    for u, h in ((uh, m.h2h), (uh, m.h2l), (ul, m.h2h)):
                        for half in range(2):
                            mm = pe.matmul(hP[:, s, half, 0:HALF], u[:, s, k, :], h[:, k, half * HALF:(half + 1) * HALF],
                                           start=(k == 0 and u is uh and h is m.h2h), stop=(k == KD - 1 and u is ul))
                mm.then_inc(h_made, 1)

            def outputs(g, first=False):
                pe.wait_ge(al_done, g * GB + GB)
                pe.wait_ge(vl_done, g * GB + GB)
                pe.wait_ge(vh_done, g * GB + GB)
                for y in range(NY):
                    t, d = y // 2, slice((y % 2) * 512, (y % 2 + 1) * 512)
                    if y >= 4 or not first:
                        before = y - 4 if y >= 4 else (YB[y] - NY)
                        pe.wait_ge(y_taken, g * NY + (before + 1))
                    for b in range(GB):
                        for a, v in ((ah, vh), (al, vh), (ah, vl)):
                            mm = pe.matmul(yP[:, y % 4, :], a[:, b, t * P:(t + 1) * P], v[:, b, d],
                                           start=(b == 0 and a is ah and v is vh), stop=(b == GB - 1 and v is vl))
                    mm.then_inc(y_made, 1)

            hidden(0, 0, True)
            hidden(1, 1, True)
            for s in range(2, GB + 1):
                hidden(s, s % 2)
            outputs(0, True)
            with pe.Fori(1, NGR - 1) as g:
                for s in range(1, GB + 1):
                    hidden(g * GB + s, s % 2)
                outputs(g)
            for s in range(1, GB):
                hidden(NKEY - GB + s, s % 2)
            outputs(NGR - 1)

        @block.scalar
        def _(act):
            def split_u(g, b, first=False):
                s = b % 2
                act.wait_ge(u_in[s], g * (8 * GB) + (16 * (b // 2) + 16))
                if not first:
                    act.wait_ge(h_made, g * GB + (b - 1))
                act.copy(uh[:, s, :, :], ur[:, s, :, :]).then_inc(uh_done, 1)

            def body(g, first, last):
                for s in range(GB):
                    n = g * GB + s
                    act.wait_ge(h_made, n + 1)
                    if not (first and s < 2):
                        act.wait_ge(al_done, n - 1)
                    act.activation(ga[:, s % 2, :].rearrange("p (h n) -> p h n", h=2), hP[:, s % 2, :, 0:HALF],
                                   ACT.Gelu_apprx_tanh).then_inc(gelu_done, 1)
                    if not (last and s >= GB - 2):
                        split_u(g, s + 2)
                    act.wait_ge(v_in[s % 2], g * (8 * GB) + (16 * (s // 2) + 16))
                    if not first and s == 0:
                        act.wait_ge(y_made, g * NY)
                    act.copy(vh[:, s, :], vr[:, s % 2, :]).then_inc(vh_done, 1)

            split_u(0, 0, True)
            split_u(0, 1, True)
            body(0, True, False)
            with act.Fori(1, NGR - 1) as g:
                body(g, False, False)
            body(NGR - 1, False, True)

        @block.vector
        def _(dve):
            dve.memset(Y[:, :, :], 0.0).then_inc(y_zero, 1)

            def split_u(n, s):
                dve.wait_ge(uh_done, n + 1)
                dve.tensor_tensor(ul[:, s, :, :], ur[:, s, :, :], uh[:, s, :, :].bitcast(F32), ALU.subtract
                                  ).then_inc(ul_done, 1)

            def body(g, first, last):
                dve.wait_ge(g_in, g * (16 * NT) + 16 * NT)
                for s in range(GB):
                    n = g * GB + s
                    ga_s = ga[:, s % 2, :]
                    dve.wait_ge(gelu_done, n + 1)
                    dve.tensor_tensor(ga_s.rearrange("p (t n) -> p t n", t=NT), ga_s.rearrange("p (t n) -> p t n", t=NT),
                                      gr[:, :, s, :], ALU.mult).then_inc(weighted, 1)
                    if not first and s == 0:
                        dve.wait_ge(y_made, g * NY)
                    dve.wait_ge(weighted, n + 1)
                    dve.tensor_copy(ah[:, s, :], ga_s).then_inc(ah_done, 1)
                    dve.wait_ge(ah_done, n + 1)
                    dve.tensor_tensor(al[:, s, :], ga_s, ah[:, s, :].bitcast(F32), ALU.subtract).then_inc(al_done, 1)
                    if not (last and s >= GB - 2):
                        split_u(n + 2, s % 2)
                    dve.wait_ge(vh_done, n + 1)
                    dve.tensor_tensor(vl[:, s, :], vr[:, s % 2, :], vh[:, s, :].bitcast(F32), ALU.subtract
                                      ).then_inc(vl_done, 1)
                for y in range(NY):
                    out = Y[:, y // 2, (y % 2) * 512:(y % 2 + 1) * 512]
                    dve.wait_ge(y_made, g * NY + (y + 1))
                    dve.tensor_tensor(out, out, yP[:, y % 4, :], ALU.add).then_inc(y_taken, 1)

            split_u(0, 0)
            split_u(1, 1)
            dve.wait_ge(y_zero, 1)
            body(0, True, False)
            with dve.Fori(1, NGR - 1) as g:
                body(g, False, False)
            body(NGR - 1, False, True)
    with scope(nc.sbuf_tensor) as tmp:
        y = tmp("y", [P, NT, D])
        add_residual(nc, m, T, sem, tmp, "res2", Y, T["x1"], T["g_post_ffn"], 1, T["y_out"], y)


@contextmanager
def scope(alloc):
    with ExitStack() as stack:
        yield lambda name, shape, dt=F32: stack.enter_context(alloc(name, shape, dt))


def program(nc, T):
    with ExitStack() as whole:
        def sem(name):
            return nc.alloc_semaphore(name=name)

        def recycle(since):
            nc.clear_and_free_semaphores(nc.allocated_since(since))
            nc.all_engine_barrier()

        def sb(name, shape, dt=F32):
            return whole.enter_context(nc.sbuf_tensor(name, shape, dt))

        def sbctx():
            return scope(nc.sbuf_tensor)

        def psctx():
            return scope(nc.psum_tensor)

        m = Memory()
        none_yet = nc.snapshot_sems()
        build_constants(nc, m, sem, sb)
        m.scale, m.shift = sb("scale", [P, 2, KD, NCOND]), sb("shift", [P, 2, KD, NCOND])
        m.stat, m.rstd = sb("stat", [P, NT]), sb("rstd", [P, NT])
        m.oN = sb("oN", [P, NT, D])
        with sbctx() as s2:
            m.qkT = s2("qkT", [P, 8, TOK])
            m.xc = s2("xc", [P, 6, CONVW])
            m.vN, m.zN = s2("vN", [P, NT, 512]), s2("zN", [P, NT, 512])
            m.dt = s2("dt", [P, NT, H])
            m.a_log, m.d_skip = s2("a_log", [P, H]), s2("d_skip", [P, H])
            with sbctx() as s3:
                m.hT = s3("hT", [P, KD, TOK])
                with sbctx() as s4, psctx() as pp:
                    modulate(nc, m, T, sem, s4, pp)
                with sbctx() as s4, psctx() as pp:
                    x = s4("x_in", [P, NT, D])
                    m.junk = s4("junk1", [P, 2, D])
                    norm_to_columns(nc, m, sem, pp, "n1", T["x"], x, m.hT, 0)
                m.xpad = s3("xpad", [P, 6, CONVW])
                m.conv_w, m.conv_b = s3("conv_w", [P, 6, CW]), s3("conv_b", [P, 6])
                m.dt_bias = s3("dt_bias", [P, H])
                project(nc, m, T, sem, s3, None, psctx)
            with sbctx() as s3, psctx() as pp:
                scan(nc, m, T, sem, s3, pp)
            with sbctx() as s3:
                attend(nc, m, T, sem, s3, psctx)
        recycle(none_yet)
        m.h2h, m.h2l = sb("h2h", [P, KD, TOK], F32R), sb("h2l", [P, KD, TOK], F32R)
        with sbctx() as s1:
            m.qhT = s1("qhT", [P, KD, TOK])
            with sbctx() as s2:
                mix(nc, m, T, sem, s2, psctx)
            with sbctx() as s2:
                route(nc, m, T, sem, s2, psctx)
        recycle(none_yet)
        with sbctx() as s2:
            experts(nc, m, T, sem, s2, psctx)


INS = dict(x=[TOK, D], cT=[P, KD, NCOND], w_ada=[D, ADA], b_ada=[ADA], g_pre_mix=[P, KD], g_pre_ffn=[P, KD],
           w_cols=[14, P, KD, P], w_vz=[P, KD, 1024 + H], state_conv=[P, 6, NSEQ, CW - 1], conv_w=[P, 6, CW],
           conv_b=[P, 6], dt_bias=[H], a_log=[H], d_skip=[H],
           state_ssm=[P, NSEQ, 256], g_mix=[P, KD], cache_kT=[NSEQ, P, 4, PAST], cache_v=[NSEQ, PAST, 512],
           w_out=[D, D], g_post_mix=[D], g_post_ffn=[D], w_pq=[8, P, KD, P], sub_keys=[P, NKEY],
           uT=[NKEY, P, KD, P], v_tab=[NKEY, P, D])
OUTS = dict(kT_out=[P, 4, TOK], v_out=[TOK, 512], conv_out=[P, 6, NCOND, CW - 1], ssm_out=[P, NCOND, 256], y_out=[TOK, D])
SCRATCH = dict(gates=[2, NCOND, D], G=[NT, P, NKEY, P], x1=[TOK, D])


def layout(x_prompt, x_sample, c_prompt, c_sample, cache_k, cache_v, state_ssm, state_conv, w_ada, b_ada, g_pre_mix,
           g_post_mix, g_pre_ffn, g_post_ffn, w_in, conv_w, conv_b, dt_bias, a_log, d_skip, g_attn_norm, g_ssd_norm,
           w_out, w_pq, sub_keys, u_tab, v_tab):
    def col_blocks(w):
        return w.reshape(KD, P, -1, P).transpose(2, 1, 0, 3)

    def by_column(g):
        return g.reshape(-1, P).T

    w = w_in[0]
    att, ssd = 3 * 512, 3 * 512 + 512
    return dict(
        x=np.concatenate([x_prompt.reshape(SEQ, D), x_sample.reshape(P, D)]),
        cT=np.concatenate([c_prompt, c_sample]).reshape(NCOND, KD, P).transpose(2, 1, 0),
        w_ada=w_ada[0], b_ada=b_ada[0], g_pre_mix=by_column(g_pre_mix), g_pre_ffn=by_column(g_pre_ffn),
        w_cols=col_blocks(np.concatenate([w[:, :1024], w[:, ssd:ssd + 768]], 1)),
        w_vz=np.concatenate([w[:, 1024:ssd], w[:, ssd + 768:]], 1).reshape(KD, P, -1).transpose(1, 0, 2),
        state_conv=state_conv[0].reshape(NSEQ, CW - 1, 6, P).transpose(3, 2, 0, 1),
        conv_w=conv_w[0].reshape(CW, 6, P).transpose(2, 1, 0), conv_b=by_column(conv_b),
        dt_bias=dt_bias[0], a_log=a_log[0], d_skip=d_skip[0],
        state_ssm=state_ssm[0].reshape(NSEQ, 2, 4, HD, 64).transpose(1, 4, 0, 2, 3).reshape(P, NSEQ, 256),
        g_mix=by_column(np.concatenate([g_attn_norm, g_ssd_norm], 1)),
        cache_kT=cache_k[0].reshape(NSEQ, PAST, 4, P).transpose(0, 3, 2, 1),
        cache_v=cache_v[0].reshape(NSEQ, PAST, 512),
        w_out=w_out[0], g_post_mix=g_post_mix[0], g_post_ffn=g_post_ffn[0], w_pq=col_blocks(w_pq[0]),
        sub_keys=sub_keys[0].transpose(0, 2, 1).reshape(P, NKEY),
        uT=u_tab[0].reshape(P, NKEY, KD, P).transpose(1, 3, 2, 0),
        v_tab=v_tab[0].reshape(P, NKEY, D).transpose(1, 0, 2))


def unlayout(r):
    y, v = r["y_out"], r["v_out"]
    k = r["kT_out"].transpose(2, 1, 0).reshape(TOK, 512)
    conv = r["conv_out"].transpose(2, 3, 1, 0).reshape(NCOND, CW - 1, 768)
    ssm = r["ssm_out"].reshape(2, 64, NCOND, 4, HD).transpose(2, 0, 3, 4, 1).reshape(NCOND, H, HD, 64)
    c = np.ascontiguousarray
    return (c(y[:SEQ]).reshape(1, SEQ, D), c(y[SEQ:]).reshape(NSEQ, LSEQ, D),
            c(k[:SEQ]).reshape(1, 1, SEQ, H, HD), c(v[:SEQ]).reshape(1, 1, SEQ, H, HD), c(ssm[None, :1]), c(conv[None, :1]),
            c(k[SEQ:]).reshape(1, NSEQ, LSEQ, H, HD), c(v[SEQ:]).reshape(1, NSEQ, LSEQ, H, HD), c(ssm[None, 1:]),
            c(conv[None, 1:]))


def build(nc):
    T = {}
    for name, shape in INS.items():
        T[name] = nc.dram_tensor("in_" + name, shape, F32, kind="ExternalInput").ap()
    for name, shape in OUTS.items():
        T[name] = nc.dram_tensor("out_" + name, shape, F32, kind="ExternalOutput").ap()
    for name, shape in SCRATCH.items():
        T[name] = nc.dram_tensor("scratch_" + name, shape, F32).ap()
    program(nc, T)


def kernel(**inputs):
    import concourse.bacc as bacc
    from concourse.bass_utils import run_bass_kernel_spmd

    nc = bacc.Bacc("TRN2", target_bir_lowering=False, num_devices=1)
    build(nc)
    arrays = {"in_" + k: np.ascontiguousarray(a) for k, a in layout(**inputs).items()}
    r = run_bass_kernel_spmd(nc, [arrays], core_ids=[0]).results[0]
    return unlayout({k: r["out_" + k] for k in OUTS})
```

```python
from contextlib import ExitStack, contextmanager

import numpy as np

import concourse.bass as bass
from concourse import mybir

F32 = mybir.dt.float32
F32R = mybir.dt.float32r
U32 = mybir.dt.uint32
ALU = mybir.AluOpType
ACT = mybir.ActivationFunctionType
AX = mybir.AxisListType.X
ds = bass.ds

P = 128
D = 1024
KD = D // P
SEQ = 512
NSEQ, LSEQ = 8, 16
NT = 5
TOK = NT * P
HALF = TOK // 2
PAST = 512
H, HD = 8, 64
NCOND = 1 + NSEQ
ADA = 6 * D
CW = 4
SEGP = CW - 1 + SEQ
SEGS = CW - 1 + LSEQ
CONVW = SEGP + NSEQ * SEGS
CONVO = CONVW - (CW - 1)
NKEY = 128
TOPK = 16
EPS = 1e-6
FAR = -1e30


class Memory:
    pass


def spread(ap, axis, n):
    shape = list(ap.shape)
    shape.insert(axis, n)
    return ap.unsqueeze(axis).broadcast_to(shape)


def build_constants(nc, m, sem, sb):
    m.ident = sb("ident", [P, P])
    m.ones = sb("ones", [P, P])
    m.upto = sb("upto", [P, 2, P])
    m.later = sb("later", [P, 2, P])
    m.from_ = sb("from_", [P, P])
    m.seen = sb("seen", [P, NT, P])
    m.same = sb("same", [P, P])
    m.hide = sb("hide", [P, NT, P])
    m.hide_ssd = sb("hide_ssd", [P, 2, P])
    m.mhalf = sb("mhalf", [P, 2 * NT])
    filled, built = sem("const_filled"), sem("const_built")
    hidden = sem("const_hidden")
    with nc.Block() as block:
        @block.gpsimd
        def _(pool):
            pool.memset(m.ident[:, :], 0.0).then_inc(filled, 1)
            pool.memset(m.mhalf[:, :], -0.5).then_inc(filled, 1)
            for t in (m.ones, m.from_, m.same):
                pool.memset(t[:, :], 1.0).then_inc(filled, 1)
            for t in (m.upto, m.later, m.seen):
                pool.memset(t[:, :, :], 1.0).then_inc(filled, 1)
            pool.wait_ge(filled, 8)

            done = 0

            def keep(view, compare, base, pattern, by_row, fill=0.0):
                nonlocal done
                pool.affine_select(out=view, in_=view, compare_op=compare, fill=fill, base=base,
                                   pattern=pattern, channel_multiplier=by_row).then_inc(built, 1)
                done += 1

            keep(m.ident[:, :], ALU.not_equal, 0, [[-1, P]], 1, 1.0)
            keep(m.from_[:, :], ALU.is_ge, 0, [[-1, P]], 1)
            keep(m.upto[:, :, :], ALU.is_ge, 0, [[0, 2], [1, P]], -1)
            keep(m.later[:, :, :], ALU.is_gt, 0, [[0, 2], [-1, P]], 1)
            keep(m.seen[:, :, :], ALU.is_gt, 0, [[0, NT], [1, P]], -1)
            blocks = (m.same[:, :], m.upto[:, 1, :], m.later[:, 1, :], m.seen[:, NT - 1, :])
            pool.wait_ge(built, done)
            for v in blocks:
                keep(v, ALU.is_ge, 0, [[-LSEQ, NSEQ], [0, LSEQ]], 1)
            pool.wait_ge(built, done)
            for v in blocks:
                keep(v, ALU.is_ge, LSEQ - 1, [[LSEQ, NSEQ], [0, LSEQ]], -1)
            m.n_built = done

        @block.vector
        def _(dve):
            dve.wait_ge(built, m.n_built)
            dve.tensor_scalar(m.hide[:, :, :], m.seen[:, :, :], -1.0, -FAR, ALU.add, ALU.mult).then_inc(hidden, 1)
            dve.tensor_scalar(m.hide_ssd[:, :, :], m.upto[:, :, :], -1.0, -FAR, ALU.add, ALU.mult).then_inc(hidden, 1)


def modulate(nc, m, T, sem, sb, ps):
    NCH = ADA // 512
    cT = sb("cT", [P, KD, NCOND])
    sT = sb("sT", [P, KD, NCOND])
    wa = sb("wa", [P, 2, KD, 512])
    ba = sb("ba", [NCOND, ADA])
    row = sb("mod_row", [NCOND, ADA])
    gcol = sb("gcol", [P, 2, KD])
    colp = ps("mod_col_ps", [P, 2, 512])
    acc = ps("mod_ps", [P, 2, 512])
    small_in, wa_in = sem("mod_small_in"), [sem(f"wa_in{s}") for s in range(2)]
    silu_done, chunk_done, row_done = sem("mod_silu"), sem("mod_chunk"), sem("mod_row")
    col_done, scaled, gates_out = sem("mod_cols"), sem("mod_scaled"), sem("gates_out")
    w = T["w_ada"].rearrange("(k p) n -> p k n", p=P)

    with nc.Block() as block:
        @block.sync
        def _(sp):
            sp.dma_start(cT[:, :, :], T["cT"]).then_inc(small_in, 16)
            sp.dma_start(ba[:, :], T["b_ada"].partition_broadcast(NCOND)).then_inc(small_in, 16)
            sp.dma_start(gcol[:, 0, :], T["g_pre_mix"]).then_inc(small_in, 16)
            sp.dma_start(gcol[:, 1, :], T["g_pre_ffn"]).then_inc(small_in, 16)
            for s in range(2):
                sp.dma_start(wa[:, s, :, :], w[:, :, s * 512:(s + 1) * 512]).then_inc(wa_in[s], 16)
            with sp.Fori(1, NCH // 2) as i:
                for s in range(2):
                    sp.wait_ge(chunk_done, i * 2 + (s - 1))
                    sp.dma_start(wa[:, s, :, :], w[:, :, ds(i * 1024 + s * 512, 512)]).then_inc(wa_in[s], 16)
            sp.wait_ge(row_done, NCH)
            for g, c in enumerate((2, 5)):
                sp.dma_start(T["gates"][g], row[:, c * D:(c + 1) * D]).then_inc(gates_out, 16)
            sp.wait_ge(gates_out, 32)

        @block.scalar
        def _(act):
            act.wait_ge(small_in, 64)
            act.activation(sT[:, :, :], cT[:, :, :], ACT.Silu).then_inc(silu_done, 1)

        @block.tensor
        def _(pe):
            pe.wait_ge(silu_done, 1)

            def chunk(s, i, n):
                pe.wait_ge(wa_in[s], i * 16 + 16)
                if n is None or n >= 2:
                    pe.wait_ge(row_done, i * 2 + (s - 1))
                for k in range(KD):
                    mm = pe.matmul(acc[0:NCOND, s, :], sT[:, k, :], wa[:, s, k, :], start=(k == 0), stop=(k == KD - 1))
                mm.then_inc(chunk_done, 1)

            for s in range(2):
                chunk(s, 0, s)
            with pe.Fori(1, NCH // 2) as i:
                for s in range(2):
                    chunk(s, i, None)
            pe.wait_ge(row_done, NCH)
            for j, c in enumerate((0, 1, 3, 4)):
                for k in range(KD):
                    at = (j % 2) * KD * NCOND + k * NCOND
                    mm = pe.transpose(colp[:, j // 2, at:at + NCOND],
                                      row[:, c * D + k * P:c * D + (k + 1) * P], m.ident[0:NCOND, 0:NCOND])
            mm.then_inc(col_done, 1)

        @block.vector
        def _(dve):
            dve.wait_ge(small_in, 64)
            with dve.Fori(0, NCH // 2) as i:
                for s in range(2):
                    dve.wait_ge(chunk_done, i * 2 + (s + 1))
                    at = ds(i * 1024 + s * 512, 512)
                    dve.tensor_tensor(row[:, at], acc[0:NCOND, s, :], ba[:, at], ALU.add).then_inc(row_done, 1)
            dve.wait_ge(col_done, 1)
            n = KD * NCOND
            for half in range(2):
                v = colp[:, half, 0:2 * n].rearrange("p (a k c) -> p a k c", a=2, k=KD)
                dve.tensor_copy(m.shift[:, half, :, :], v[:, 0]).then_inc(scaled, 1)
                dve.scalar_tensor_tensor(m.scale[:, half, :, :], v[:, 1], 1.0, spread(gcol[:, half, :], 2, NCOND),
                                         ALU.add, ALU.mult).then_inc(scaled, 1)


def norm_to_columns(nc, m, sem, ps, name, load, src, dst, which, extra=None):
    ss = m.stat
    pr = ps(name + "_ps", [P, 2, 512])
    sa = ps(name + "_ps_s", [P, 2, 512])
    squared, mean, rstd, normed = (sem(name + x) for x in ("_sq", "_mean", "_rstd", "_normed"))
    turned, turned_s, out_p, out_s = (sem(name + x) for x in ("_tp", "_ts", "_op", "_os"))
    loaded = [sem(f"{name}_in{t}") for t in range(NT)]
    with nc.Block() as block:
        if load is not None:
            @block.sync
            def _(sp):
                for t in range(NT):
                    sp.dma_start(src[:, t, :], load[t * P:(t + 1) * P, :]).then_inc(loaded[t], 16)

        @block.scalar
        def _(act):
            for t in range(NT):
                if load is not None:
                    act.wait_ge(loaded[t], 16)
                if t >= 2:
                    act.wait_ge(squared, t - 1)
                act.activation(m.junk[:, t % 2, :], src[:, t, :], ACT.Square, accum_out=ss[:, t:t + 1]).then_inc(squared, 1)

        @block.gpsimd
        def _(pool):
            pool.wait_ge(mean, 1)
            pool.tensor_tensor(m.rstd[:, :], ss[:, :], m.mhalf[:, 0:NT], ALU.pow).then_inc(rstd, 1)

        @block.vector
        def _(dve):
            dve.wait_ge(squared, NT)
            dve.tensor_scalar(ss[:, :], ss[:, :], 1.0 / D, EPS, ALU.mult, ALU.add).then_inc(mean, 1)
            dve.wait_ge(rstd, 1)
            for t in range(NT):
                dve.tensor_scalar(src[:, t, :], src[:, t, :], m.rstd[:, t:t + 1], None, ALU.mult).then_inc(normed, 1)
            for k in range(KD):
                dve.wait_ge(turned, k + 1)
                dve.tensor_scalar(dst[:, k, 0:SEQ], pr[:, k % 2, :], m.scale[:, which, k, 0:1],
                                  m.shift[:, which, k, 0:1], ALU.mult, ALU.add).then_inc(out_p, 1)
                if k % 4 == 3:
                    q = k // 4
                    dve.wait_ge(turned_s, q + 1)
                    d4 = dst[:, 4 * q:4 * q + 4, SEQ:TOK].rearrange("p k (b i) -> p k b i", b=NSEQ)
                    s4 = sa[:, q, :].rearrange("p (k b i) -> p k b i", k=4, b=NSEQ)
                    for kk in range(4):
                        dve.tensor_tensor(d4[:, kk], s4[:, kk],
                                          spread(m.scale[:, which, 4 * q + kk, 1:NCOND], 2, LSEQ),
                                          ALU.mult).then_inc(out_s, 1)
                    dve.wait_ge(out_s, 8 * q + 4)
                    for kk in range(4):
                        dve.tensor_tensor(d4[:, kk], d4[:, kk],
                                          spread(m.shift[:, which, 4 * q + kk, 1:NCOND], 2, LSEQ),
                                          ALU.add).then_inc(out_s, 1)

        @block.tensor
        def _(pe):
            pe.wait_ge(normed, NT)
            for k in range(KD):
                if k >= 2:
                    pe.wait_ge(out_p, k - 1)
                for t in range(NT - 1):
                    mm = pe.transpose(pr[:, k % 2, t * P:(t + 1) * P], src[:, t, k * P:(k + 1) * P], m.ident[:, :])
                mm.then_inc(turned, 1)
                mm = pe.transpose(sa[:, k // 4, (k % 4) * P:(k % 4 + 1) * P], src[:, NT - 1, k * P:(k + 1) * P],
                                  m.ident[:, :])
                if k % 4 == 3:
                    mm.then_inc(turned_s, 1)


def column_products(nc, m, sem, sb, ps, name, w_blocks, n_blocks, src, sink):
    ring = sb(name + "_w", [P, 2, KD, P])
    acc = ps(name + "_acc", [P, 2, 2, 512])
    w_in, made, taken = [sem(f"{name}_in{s}") for s in range(2)], sem(name + "_made"), sem(name + "_taken")
    with nc.Block() as block:
        @block.sync
        def _(sp):
            for s in range(2):
                sp.dma_start(ring[:, s, :, :], w_blocks[s]).then_inc(w_in[s], 16)
            with sp.Fori(1, n_blocks // 2) as i:
                for s in range(2):
                    sp.wait_ge(made, i * 2 + (s - 1))
                    sp.dma_start(ring[:, s, :, :], w_blocks[ds(i * 2 + s, 1)].rearrange("a p k c -> (a p) k c")
                                 ).then_inc(w_in[s], 16)

        @block.tensor
        def _(pe):
            def blk(i, s, first):
                pe.wait_ge(w_in[s], i * 16 + 16)
                if not first:
                    pe.wait_ge(taken, i * 2 + (s - 1))
                for k in range(KD):
                    for h in range(2):
                        mm = pe.matmul(acc[:, s, h, 0:HALF], ring[:, s, k, :], src[:, k, h * HALF:(h + 1) * HALF],
                                       start=(k == 0), stop=(k == KD - 1))
                mm.then_inc(made, 1)
            for s in range(2):
                blk(0, s, True)
            with pe.Fori(1, n_blocks // 2) as i:
                for s in range(2):
                    blk(i, s, False)

        @block.scalar
        def _(act):
            sink(act, acc, made, taken)


def project(nc, m, T, sem, sb, ps, psctx):
    def sink(act, acc, made, taken):
        with act.Fori(0, 4) as i:
            for s in range(2):
                act.wait_ge(made, i * 2 + (s + 1))
                act.copy(m.qkT[:, ds(i * 2 + s, 1), :].rearrange("p a (h n) -> p (a h) n", h=2),
                         acc[:, s, :, 0:HALF]).then_inc(taken, 1)
        for n in range(8, 14):
            s, j = n % 2, n - 8
            act.wait_ge(made, n + 1)
            act.copy(m.xpad[:, j, CW - 1:CW - 1 + HALF], acc[:, s, 0, 0:HALF])
            act.copy(m.xpad[:, j, CW - 1 + HALF:SEGP], acc[:, s, 1, 0:SEQ - HALF])
            act.copy(m.xpad[:, j, SEGP:].rearrange("p (b i) -> p b i", b=NSEQ)[:, :, CW - 1:],
                     acc[:, s, 1, SEQ - HALF:HALF].rearrange("p (b i) -> p b i", b=NSEQ)).then_inc(taken, 1)

    with psctx() as pp:
        column_products(nc, m, sem, sb, pp, "proj", T["w_cols"], 14, m.hT, sink)

    wv = sb("w_rows", [P, KD, 1024 + H])
    rows_in, pads_in = sem("rows_in"), sem("pads_in")
    vz_made, vz_taken, dt_made, dt_taken = sem("vz_made"), sem("vz_taken"), sem("dt_made"), sem("dt_taken")
    conv, conv_ready, out_done = sem("conv_step"), sem("conv_sum"), sem("proj_out")
    zeroed, silu_done = sem("pad_zero"), sem("conv_silu")
    with psctx() as pp, nc.Block() as block:
        acc = pp("vz_ps", [P, 2, 2, 512])
        dtp = pp("dt_ps", [P, 512])

        @block.sync
        def _(sp):
            for c in range(2):
                sp.dma_start(wv[:, :, c * 512:(c + 1) * 512], T["w_vz"][:, :, c * 512:(c + 1) * 512]).then_inc(rows_in, 16)
            sp.dma_start(wv[:, :, 1024:], T["w_vz"][:, :, 1024:]).then_inc(rows_in, 16)
            for j in range(6):
                sp.dma_start(m.xpad[:, j, SEGP:].rearrange("p (b i) -> p b i", b=NSEQ)[:, :, 0:CW - 1],
                             T["state_conv"][:, j]).then_inc(pads_in, 16)
            sp.dma_start(m.conv_w[:, :, :], T["conv_w"]).then_inc(pads_in, 16)
            sp.dma_start(m.conv_b[:, :], T["conv_b"]).then_inc(pads_in, 16)
            sp.dma_start(m.dt_bias[:, :], T["dt_bias"].partition_broadcast(P)).then_inc(pads_in, 16)
            sp.dma_start(m.a_log[:, :], T["a_log"].partition_broadcast(P)).then_inc(pads_in, 16)
            sp.dma_start(m.d_skip[:, :], T["d_skip"].partition_broadcast(P)).then_inc(pads_in, 16)
            sp.dma_start(T["kT_out"], m.qkT[:, 4:8, :]).then_inc(out_done, 16)
            for j in range(6):
                sp.dma_start(T["conv_out"][:, j, 0, :], m.xpad[:, j, SEGP - (CW - 1):SEGP]).then_inc(out_done, 16)
                sp.dma_start(T["conv_out"][:, j, 1:NCOND, :],
                             m.xpad[:, j, SEGP:].rearrange("p (b i) -> p b i", b=NSEQ)[:, :, SEGS - (CW - 1):]
                             ).then_inc(out_done, 16)
            sp.wait_ge(vz_taken, NT)
            for t in range(NT):
                sp.dma_start(T["v_out"][t * P:(t + 1) * P, :], m.vN[:, t, :]).then_inc(out_done, 16)
            sp.wait_ge(out_done, 16 * (13 + NT))

        @block.tensor
        def _(pe):
            for t in range(NT):
                if t == 0:
                    pe.wait_ge(rows_in, 48)
                if t >= 2:
                    pe.wait_ge(vz_taken, t - 1)
                for k in range(KD):
                    lhs = m.hT[:, k, t * P:(t + 1) * P]
                    pe.matmul(acc[:, t % 2, 0, :], lhs, wv[:, k, 0:512], start=(k == 0), stop=(k == KD - 1))
                    mm = pe.matmul(acc[:, t % 2, 1, :], lhs, wv[:, k, 512:1024], start=(k == 0), stop=(k == KD - 1))
                mm.then_inc(vz_made, 1)
                for k in range(KD):
                    mm = pe.matmul(dtp[:, t * H:(t + 1) * H], m.hT[:, k, t * P:(t + 1) * P], wv[:, k, 1024:],
                                   start=(k == 0), stop=(k == KD - 1))
            mm.then_inc(dt_made, 1)

        @block.vector
        def _(dve):
            dve.memset(m.xpad[:, :, 0:CW - 1], 0.0).then_inc(zeroed, 1)
            dve.wait_ge(pads_in, 16 * 11)
            dve.wait_ge(zeroed, 1)
            for w in range(CW):
                for j in range(6):
                    src = m.xpad[:, j, w:w + CONVO]
                    if w:
                        dve.wait_ge(conv, (w - 1) * 6 + j + 1)
                        dve.scalar_tensor_tensor(m.xc[:, j, 0:CONVO], src, m.conv_w[:, j, w:w + 1], m.xc[:, j, 0:CONVO],
                                                 ALU.mult, ALU.add).then_inc(conv, 1)
                    else:
                        dve.tensor_scalar(m.xc[:, j, 0:CONVO], src, m.conv_w[:, j, 0:1], m.conv_b[:, j:j + 1],
                                          ALU.mult, ALU.add).then_inc(conv, 1)
            dve.wait_ge(dt_made, 1)
            dve.tensor_tensor(m.dt[:, :, :], dtp[:, 0:NT * H].rearrange("p (t h) -> p t h", t=NT),
                              spread(m.dt_bias[:, :], 1, NT), ALU.add).then_inc(dt_taken, 1)

        @block.scalar
        def _(act):
            for t in range(NT):
                act.wait_ge(vz_made, t + 1)
                act.copy(m.vN[:, t, :], acc[:, t % 2, 0, :])
                act.copy(m.zN[:, t, :], acc[:, t % 2, 1, :]).then_inc(vz_taken, 1)
            for j in range(6):
                act.wait_ge(conv, 18 + j + 1)
                act.activation(m.xc[:, j, 0:CONVO], m.xc[:, j, 0:CONVO], ACT.Silu).then_inc(silu_done, 1)


def scan(nc, m, T, sem, sb, ps):
    E = LSEQ * NSEQ
    xt = sb("xt", [P, 6, P])
    dts, das = sb("dts", [P, H]), sb("das", [P, H])
    a8, dtA = sb("a8", [P, H]), sb("dtA", [P, NT, H])
    sp = sb("sp_tmp", [P, NT * H])
    cum, grow = sb("cum", [P, 2 * H]), sb("grow", [P, 2, H])
    lastc = sb("lastc", [P, H, NSEQ])
    seg, dec, W = sb("seg", [P, H, P]), sb("dec", [P, H, P]), sb("W", [P, H, P])
    Bn = sb("Bn", [P, P])
    xdt, xdte, xD = sb("xdt", [P, H, HD]), sb("xdte", [P, H, HD]), sb("xD", [P, H, HD])
    state = sb("state", [P, 512])
    CTg = sb("CTg", [P, 2, P])
    cdec = sb("cdec", [P, H, NSEQ])
    CTm = sb("CTm", [P, NSEQ * (P + LSEQ)])
    Bm = sb("Bm", [P, NSEQ, P])
    sst = sb("sst", [P, NSEQ, 512])
    misc, csb = ps("scan_misc", [P, 512]), ps("scan_cs", [P, 512])
    rows = ps("scan_rows", [P, H, P])
    xsP, yd, yo, S = (ps(n, [P, 512]) for n in ("scan_xs", "scan_yd", "scan_yo", "scan_S"))
    cs, cb, bP = csb[:, 0:16], misc[:, 16:272].rearrange("p (g t) -> p g t", g=2), misc[:, 272:400]
    Spair = (S, xsP)

    ready, dt_step, dt_act = sem("scan_ready"), sem("dt_step"), sem("dt_act")
    staged = sem("scan_staged")
    cum_made, rows_made, cb_made, y_made = sem("cum_made"), sem("rows_made"), sem("cb_made"), sem("y_made")
    act_done, seg_step, w_ready, x_ready = sem("scan_exp"), sem("seg_step"), sem("w_ready"), sem("x_ready")
    state_step, y_step = sem("state_step"), sem("y_step")
    st_in, st_out, masked = sem("ssm_in"), sem("ssm_out_sem"), sem("scan_masked")
    bm_ready = sem("bm_ready")
    s_made, s_taken, aged = sem("S_made"), sem("S_taken"), sem("sst_aged")
    gate_silu, gated = sem("gate_silu"), sem("gated")
    flat = lambda v: v[:, :, :].rearrange("p t h -> p (t h)")
    NP = NT - 1

    def own(v, g):
        return v[64 * g:64 * g + 64, :, g * 256:(g + 1) * 256]

    with nc.Block() as block:
        @block.sync
        def _(eng):
            eng.wait_ge(masked, 2)
            for g in range(2):
                eng.dma_start(own(sst, g), T["state_ssm"][64 * g:64 * g + 64]).then_inc(st_in, 16)
            eng.wait_ge(state_step, 1 + 4 * NP)
            for g in range(2):
                r = slice(64 * g, 64 * g + 64)
                eng.dma_start(T["ssm_out"][r, 0, :], state[r, g * 256:(g + 1) * 256]).then_inc(st_out, 16)
            eng.wait_ge(s_taken, 2 * NSEQ)
            for g in range(2):
                eng.dma_start(T["ssm_out"][64 * g:64 * g + 64, 1:NCOND, :], own(sst, g)).then_inc(st_out, 16)
            eng.wait_ge(st_out, 64)

        @block.gpsimd
        def _(pool):
            pool.memset(state[:, :], 0.0).then_inc(state_step, 1)
            pool.memset(CTm[:, :], 0.0).then_inc(masked, 1)
            pool.memset(sst[:, :, :], 0.0).then_inc(masked, 1)
            pool.memset(CTg[:, :, :], 0.0).then_inc(staged, 1)
            pool.wait_ge(staged, 1)
            pool.wait_ge(ready, 1)

            def stage(i, sampled):
                for dst, src in ((dts, m.dt), (das, dtA)):
                    pool.tensor_copy(dst[:, :], src[:, ds(i, 1), :].rearrange("p a h -> p (a h)")
                                     if not sampled else src[:, NP, :]).then_inc(staged, 1)
                if sampled:
                    pool.tensor_copy(xt[:, :, :].rearrange("p j (b i) -> p j b i", b=NSEQ),
                                     m.xc[:, :, SEGP:].rearrange("p j (b i) -> p j b i", b=NSEQ)[:, :, :, 0:LSEQ]
                                     ).then_inc(staged, 1)
                else:
                    pool.tensor_copy(xt[:, :, :], m.xc[:, :, ds(i * P, P)]).then_inc(staged, 1)
                copied = i * 5 + 4 if sampled or isinstance(i, int) else pool.to_reg(i * 5 + 4)
                pool.wait_ge(ready, 1)
                pool.wait_ge(staged, copied)
                for g in range(2):
                    r = slice(64 * g, 64 * g + 64)
                    pool.tensor_copy(CTg[r, g, :], xt[r, 5, :]).then_inc(staged, 1)

            stage(0, False)
            with pool.Fori(1, NP) as i:
                pool.wait_ge(ready, 1)
                pool.wait_ge(y_made, i)
                pool.wait_ge(x_ready, i * 4)
                stage(i, False)
            pool.wait_ge(y_made, NP)
            pool.wait_ge(x_ready, NP * 4)
            stage(NP, True)
            pool.wait_ge(staged, 5 * NT + 1)
            pool.wait_ge(masked, 2)
            diagonal = CTm[:, :].rearrange("p (b x) -> p b x", b=NSEQ)[:, :, 0:LSEQ]
            pool.tensor_copy(diagonal, xt[:, 5, :].rearrange("p (b i) -> p b i", b=NSEQ)).then_inc(masked, 1)

        @block.tensor
        def _(pe):
            def tile(i, sampled, first):
                w = 1 if sampled else 0
                pe.wait_ge(staged, i * 5 + 6)
                if not first:
                    pe.wait_ge(y_step, i * 3)
                pe.matmul(cs[:, 0:H], m.upto[:, w, :], das[:, :], start=True, stop=True)
                pe.matmul(cs[:, H:], m.later[:, w, :], das[:, :], start=True, stop=True).then_inc(cum_made, 1)
                for h in range(H):
                    mm = pe.matmul(rows[:, h, :], das[:, h:h + 1].broadcast_to([P, P]), m.upto[:, w, :],
                                   start=True, stop=True)
                mm.then_inc(rows_made, 1)
                pe.matmul(cb, xt[:, 4, :], CTg[:, :, :], start=True, stop=True)
                for j in range(4):
                    pe.transpose(xsP[:, j * P:(j + 1) * P], xt[:, j, :], m.ident[:, :])
                pe.transpose(bP, xt[:, 4, :], m.ident[:, :]).then_inc(cb_made, 1)
                pe.wait_ge(w_ready, i + 1)
                pe.wait_ge(x_ready, i * 4 + 3)
                for h in range(H):
                    pe.matmul(yd[:, h * HD:(h + 1) * HD], W[:, h, :], xdt[:, h, :], start=True, stop=True)
                if sampled:
                    pe.wait_ge(masked, 3)
                    pe.wait_ge(st_in, 32)
                    for b in range(NSEQ):
                        mm = pe.matmul(yo[:, :], CTm[:, b * P:(b + 1) * P], sst[:, b, :],
                                       start=(b == 0), stop=(b == NSEQ - 1))
                    mm.then_inc(y_made, 1)
                    pe.wait_ge(bm_ready, 1)
                    pe.wait_ge(x_ready, 4 * NT)
                    for b in range(NSEQ):
                        if b >= 2:
                            pe.wait_ge(s_taken, 2 * (b - 1))
                        pe.matmul(Spair[b % 2][:, :], Bm[:, b, :], xdte[:, :, :].rearrange("p h d -> p (h d)"),
                                  start=True, stop=True).then_inc(s_made, 1)
                else:
                    pe.wait_ge(state_step, i * 4 + 1)
                    pe.matmul(yo[:, :], xt[:, 5, :], state[:, :], start=True, stop=True)
                    pe.matmul(S[:, :], Bn[:, :], xdte[:, :, :].rearrange("p h d -> p (h d)"),
                              start=True, stop=True).then_inc(y_made, 1)

            tile(0, False, True)
            with pe.Fori(1, NP) as i:
                tile(i, False, False)
            tile(NP, True, False)

        @block.scalar
        def _(act):
            act.activation(a8[:, :], m.a_log[:, :], ACT.Exp).then_inc(dt_act, 1)
            act.activation(sp[:, :], flat(m.dt), ACT.Abs).then_inc(dt_act, 1)
            act.wait_ge(dt_act, 2)
            act.activation(sp[:, :], sp[:, :], ACT.Exp, scale=-1.0).then_inc(dt_act, 1)
            act.wait_ge(dt_act, 3)
            act.activation(sp[:, :], sp[:, :], ACT.Ln, bias=1.0).then_inc(dt_act, 1)

            def tile(i, sampled, first):
                act.wait_ge(seg_step, i * 4 + 1)
                if not first:
                    act.wait_ge(y_step, i * 3)
                    act.wait_ge(x_ready, i * 4)
                    act.wait_ge(state_step, i * 4 + 1)
                act.activation(grow[:, :, :].rearrange("p a h -> p (a h)"), cum[:, :], ACT.Exp).then_inc(act_done, 1)
                act.wait_ge(seg_step, i * 4 + 3)
                n = NSEQ if sampled else 1
                act.activation(cdec[:, :, 0:n], lastc[:, :, 0:n], ACT.Exp).then_inc(act_done, 1)
                act.wait_ge(seg_step, i * 4 + 4)
                if not first:
                    act.wait_ge(w_ready, i)
                act.activation(dec[:, :, :], seg[:, :, :], ACT.Exp).then_inc(act_done, 1)

            tile(0, False, True)
            with act.Fori(1, NP) as i:
                tile(i, False, False)
            tile(NP, True, False)
            act.activation(m.zN[:, :, :], m.zN[:, :, :], ACT.Silu).then_inc(gate_silu, 1)

        @block.vector
        def _(dve):
            dve.wait_ge(dt_act, 4)
            dve.scalar_tensor_tensor(flat(m.dt), flat(m.dt), 0.0, sp[:, :], ALU.max, ALU.add).then_inc(dt_step, 1)
            dve.wait_ge(dt_step, 1)
            dve.scalar_tensor_tensor(dtA[:, :, :], m.dt[:, :, :], -1.0, spread(a8[:, :], 1, NT), ALU.mult,
                                     ALU.mult).then_inc(ready, 1)

            def tile(i, sampled, first):
                w = 1 if sampled else 0
                dve.wait_ge(cum_made, i + 1)
                if not first:
                    dve.wait_ge(act_done, i * 3)
                dve.tensor_copy(cum[:, :], cs).then_inc(seg_step, 1)
                dve.wait_ge(rows_made, i + 1)
                dve.wait_ge(seg_step, i * 4 + 1)
                dve.tensor_tensor(seg[:, :, :], rows[:, :, :], spread(cum[:, 0:H], 2, P), ALU.subtract
                                  ).then_inc(seg_step, 1)
                if sampled:
                    dve.tensor_copy(lastc[:, :, :], rows[:, :, LSEQ - 1:P:LSEQ]).then_inc(seg_step, 1)
                else:
                    dve.tensor_copy(lastc[:, :, 0], rows[:, :, P - 1]).then_inc(seg_step, 1)
                dve.wait_ge(seg_step, i * 4 + 2)
                dve.tensor_tensor(seg[:, :, :], seg[:, :, :], spread(m.hide_ssd[:, w, :], 1, H), ALU.min
                                  ).then_inc(seg_step, 1)
                dve.wait_ge(cb_made, i + 1)
                dve.wait_ge(staged, i * 5 + 6)
                xs = xsP[:, :].rearrange("p (h d) -> p h d", h=H)
                dve.tensor_tensor(xdt[:, :, :], xs, spread(dts[:, :], 2, HD), ALU.mult).then_inc(x_ready, 1)
                dve.tensor_copy(Bn[:, :], bP).then_inc(x_ready, 1)
                dve.wait_ge(act_done, i * 3 + 1)
                dve.wait_ge(x_ready, i * 4 + 1)
                dve.tensor_tensor(xdte[:, :, :], xdt[:, :, :], spread(grow[:, 1, :], 2, HD), ALU.mult
                                  ).then_inc(x_ready, 1)
                if not first:
                    dve.wait_ge(y_step, i * 3)
                dve.tensor_tensor(xD[:, :, :], xs, spread(m.d_skip[:, :], 2, HD), ALU.mult).then_inc(x_ready, 1)
                dve.wait_ge(act_done, i * 3 + 3)
                for g in range(2):
                    hs = slice(4 * g, 4 * g + 4)
                    op = dve.tensor_tensor(W[:, hs, :], dec[:, hs, :], spread(cb[:, g, :], 1, 4), ALU.mult)
                op.then_inc(w_ready, 1)
                if sampled:
                    dve.wait_ge(x_ready, 4 * NP + 2)
                    dve.tensor_tensor(Bm[:, :, :], spread(Bn[:, :], 1, NSEQ), spread(m.same[:, 0:P:LSEQ], 2, P),
                                      ALU.mult).then_inc(bm_ready, 1)
                dve.wait_ge(y_made, i + 1)
                out = (m.oN[:, NP, 512:] if sampled else
                       m.oN[:, ds(i, 1), 512:].rearrange("p a n -> p (a n)")).rearrange("p (h d) -> p h d", h=H)
                by_head = lambda v: v[:, :].rearrange("p (h d) -> p h d", h=H)
                dve.tensor_tensor(out, by_head(yo), spread(grow[:, 0, :], 2, HD), ALU.mult).then_inc(y_step, 1)
                dve.wait_ge(y_step, i * 3 + 1)
                dve.tensor_tensor(out, out, by_head(yd), ALU.add).then_inc(y_step, 1)
                dve.wait_ge(y_step, i * 3 + 2)
                dve.wait_ge(x_ready, i * 4 + 4)
                dve.tensor_tensor(out, out, xD[:, :, :], ALU.add).then_inc(y_step, 1)
                if not sampled:
                    for step in range(2):
                        for g in range(2):
                            r = slice(64 * g, 64 * g + 64)
                            cols = slice(g * 256, (g + 1) * 256)
                            st = state[r, cols].rearrange("p (k d) -> p k d", k=4)
                            if step == 0:
                                dve.tensor_tensor(st, st, spread(cdec[r, 4 * g:4 * g + 4, 0], 2, HD), ALU.mult
                                                  ).then_inc(state_step, 1)
                            else:
                                dve.wait_ge(state_step, i * 4 + (2 + g))
                                dve.tensor_tensor(state[r, cols], state[r, cols], S[r, cols], ALU.add
                                                  ).then_inc(state_step, 1)

            dve.wait_ge(state_step, 1)
            tile(0, False, True)
            with dve.Fori(1, NP) as i:
                tile(i, False, False)
            tile(NP, True, False)
            for g in range(2):
                r = slice(64 * g, 64 * g + 64)
                st = own(sst, g).rearrange("p b (k d) -> p b k d", k=4)
                by_seq = cdec[r, 4 * g:4 * g + 4, :].rearrange("p k b -> p b k")
                dve.tensor_tensor(st, st, spread(by_seq, 3, HD), ALU.mult).then_inc(aged, 1)
            dve.wait_ge(aged, 2)
            for b in range(NSEQ):
                dve.wait_ge(s_made, b + 1)
                for g in range(2):
                    r, cols = slice(64 * g, 64 * g + 64), slice(g * 256, (g + 1) * 256)
                    dve.tensor_tensor(sst[r, b, cols], sst[r, b, cols], Spair[b % 2][r, cols], ALU.add
                                      ).then_inc(s_taken, 1)
            dve.wait_ge(gate_silu, 1)
            dve.wait_ge(y_step, 3 * NT)
            dve.tensor_tensor(m.oN[:, :, 512:], m.oN[:, :, 512:], m.zN[:, :, :], ALU.mult).then_inc(gated, 1)


def attend(nc, m, T, sem, sb, psctx):
    m.sp_new = sb("sp_new", [P, H, P])
    attend_own(nc, m, sem, sb, psctx)
    attend_past(nc, m, T, sem, sb, psctx)


def attend_own(nc, m, sem, sb, psctx):
    ND = NT * P
    OFF = {0: (ND, 3), 1: (ND + 3 * P, 2), 2: (ND + 5 * P, 1)}
    NW = ND + 6 * P
    SC = HD ** -0.5
    kS = sb("kS", [P, TOK])
    qB = sb("qB", [P, 2, TOK])
    with scope(nc.sbuf_tensor) as tmp, psctx() as ps:
        z, a, w = (tmp(n, [P, 2, NW]) for n in ("own_z", "own_a", "own_w"))
        zP, SP = ps("own_zP", [P, 1536]), ps("own_SP", [P, 1536])
        oP = ps("own_oP", [P, 2, 512])
        zeroed, staged = sem("own_zeroed"), sem("own_staged")
        z_made, z_taken, ln_step, sp_step = (sem("own_" + n) for n in ("zmade", "ztaken", "lnstep", "spstep"))
        s_made, arg_step, w_done, o_made, o_taken = (sem("own_" + n) for n in ("smade", "argstep", "wdone", "omade", "otaken"))
        with nc.Block() as block:
            @block.gpsimd
            def _(pool):
                pool.memset(qB[:, :, :], 0.0).then_inc(zeroed, 1)
                pool.wait_ge(zeroed, 1)

                def stage(i):
                    pool.tensor_copy(kS[:, :], m.qkT[:, ds(i + 4, 1), :].rearrange("p a n -> p (a n)")).then_inc(staged, 1)
                    for g in range(2):
                        r = slice(64 * g, 64 * g + 64)
                        pool.wait_ge(zeroed, 1)
                        pool.wait_ge(staged, i * 3 + (g + 1))
                        pool.tensor_copy(qB[r, g, :], m.qkT[r, ds(i, 1), :].rearrange("p a n -> p (a n)")).then_inc(staged, 1)

                stage(0)
                with pool.Fori(1, 4) as i:
                    pool.wait_ge(zeroed, 1)
                    pool.wait_ge(z_made, i * 2)
                    stage(i)

            @block.tensor
            def _(pe):
                def pair(i, first):
                    pe.wait_ge(staged, i * 3 + 3)
                    for s in range(2):
                        if s or not first:
                            pe.wait_ge(z_taken, i * 2 + s)
                        for j in range(NT):
                            c = slice(j * P, (j + 1) * P)
                            mm = pe.matmul(zP[:, c], kS[:, c], qB[:, s, c], start=True, stop=True)
                            if j in OFF:
                                at, n = OFF[j]
                                mm = pe.matmul(zP[:, at:at + n * P], kS[:, c], qB[:, s, (j + 1) * P:(j + 1 + n) * P],
                                               start=True, stop=True)
                        mm.then_inc(z_made, 1)
                    for s in range(2):
                        pe.wait_ge(sp_step, i * 4 + (2 * s + 2))
                        if s or not first:
                            pe.wait_ge(arg_step, i * 4 + 2 * s)
                        sp = a[:, s, :]
                        pe.matmul(SP[:, 0:512], m.from_[:, :], sp[:, 0:512], start=True, stop=True)
                        pe.matmul(SP[:, 512:ND], m.from_[:, :], sp[:, 512:ND], start=True, stop=True)
                        for j, (at, n) in OFF.items():
                            pe.matmul(SP[:, at:at + n * P], m.from_[:, :], sp[:, at:at + n * P], start=True, stop=False)
                            for jj in range(j + 1, 4):
                                o = at + (jj - j - 1) * P
                                mm = pe.matmul(SP[:, o:o + P], m.ones[:, :], sp[:, jj * P:(jj + 1) * P],
                                               start=False, stop=(jj == 3))
                                if jj in OFF:
                                    a2, n2 = OFF[jj]
                                    mm = pe.matmul(SP[:, o + P:o + P + n2 * P], m.ones[:, :], sp[:, a2:a2 + n2 * P],
                                                   start=False, stop=False)
                        mm.then_inc(s_made, 1)
                    for s in range(2):
                        pe.wait_ge(w_done, i * 2 + (s + 1))
                        if not first:
                            pe.wait_ge(o_taken, i * 2 - (1 - s))
                        for q in range(NT):
                            keys = range(q + 1) if q < 4 else [4]
                            for j in keys:
                                c = j * P if j == q else OFF[j][0] + (q - j - 1) * P
                                mm = pe.matmul(oP[:, s, q * HD:(q + 1) * HD], w[:, s, c:c + P],
                                               m.vN[:, j, ds(i * 128 + s * HD, HD)], start=(j == keys[0]), stop=(j == q))
                        mm.then_inc(o_made, 1)
                pair(0, True)
                with pe.Fori(1, 4) as i:
                    pair(i, False)

            @block.scalar
            def _(act):
                def pair(i, first):
                    for s in range(2):
                        act.wait_ge(z_taken, i * 2 + (s + 1))
                        if not first:
                            act.wait_ge(s_made, i * 2 - (1 - s))
                            act.wait_ge(arg_step, i * 4 + (2 * s - 2))
                        act.activation(a[:, s, :], z[:, s, :], ACT.Abs).then_inc(ln_step, 1)
                        act.wait_ge(ln_step, i * 6 + (3 * s + 1))
                        act.activation(a[:, s, :], a[:, s, :], ACT.Exp, scale=-1.0).then_inc(ln_step, 1)
                        act.wait_ge(ln_step, i * 6 + (3 * s + 2))
                        act.activation(a[:, s, :], a[:, s, :], ACT.Ln, bias=1.0).then_inc(ln_step, 1)
                    for s in range(2):
                        act.wait_ge(arg_step, i * 4 + (2 * s + 2))
                        if not first:
                            act.wait_ge(o_made, i * 2 - (1 - s))
                        act.activation(w[:, s, :], z[:, s, :], ACT.Exp).then_inc(w_done, 1)
                pair(0, True)
                with act.Fori(1, 4) as i:
                    pair(i, False)

            @block.vector
            def _(dve):
                def pair(i, first):
                    for s in range(2):
                        dve.wait_ge(z_made, i * 2 + (s + 1))
                        if not first:
                            dve.wait_ge(w_done, i * 2 - (1 - s))
                        dve.tensor_scalar(z[:, s, :], zP[:, 0:NW], SC, None, ALU.mult).then_inc(z_taken, 1)
                    for s in range(2):
                        dve.wait_ge(ln_step, i * 6 + (3 * s + 3))
                        dve.scalar_tensor_tensor(a[:, s, :], z[:, s, :], 0.0, a[:, s, :], ALU.max, ALU.add
                                                 ).then_inc(sp_step, 1)
                        dve.wait_ge(sp_step, i * 4 + (2 * s + 1))
                        seen = m.seen[:, :, :].rearrange("p t q -> p (t q)")
                        dve.tensor_tensor(a[:, s, 0:ND], a[:, s, 0:ND], seen, ALU.mult).then_inc(sp_step, 1)
                        dve.wait_ge(sp_step, i * 4 + (2 * s + 2))
                        dve.tensor_copy(m.sp_new[:, ds(i * 2 + s, 1), :].rearrange("p a n -> p (a n)"),
                                        a[:, s, ND - P:ND])
                    for s in range(2):
                        dve.wait_ge(s_made, i * 2 + (s + 1))
                        dve.tensor_tensor(z[:, s, :], z[:, s, :], SP[:, 0:NW], ALU.subtract).then_inc(arg_step, 1)
                        dve.wait_ge(arg_step, i * 4 + (2 * s + 1))
                        hide = m.hide[:, :, :].rearrange("p t q -> p (t q)")
                        dve.tensor_tensor(z[:, s, 0:ND], z[:, s, 0:ND], hide, ALU.min).then_inc(arg_step, 1)
                    for s in range(2):
                        dve.wait_ge(o_made, i * 2 + (s + 1))
                        dve.tensor_copy(m.oN[:, :, ds(i * 128 + s * HD, HD)],
                                        oP[:, s, 0:NT * HD].rearrange("p (t d) -> p t d", t=NT)).then_inc(o_taken, 1)
                pair(0, True)
                with dve.Fori(1, 4) as i:
                    pair(i, False)


def attend_past(nc, m, T, sem, sb, psctx):
    NJ = PAST // P
    SC = HD ** -0.5
    with scope(nc.sbuf_tensor) as tmp, psctx() as ps:
        kT, vb = tmp("past_k", [P, 2, 4, PAST]), tmp("past_v", [P, 2, NJ, 512])
        qB = tmp("past_q", [P, 4, 2, P])
        z, a, w = (tmp(n, [P, 2, NJ, P]) for n in ("past_z", "past_a", "past_w"))
        oTs = tmp("past_oT", [HD, H, P])
        zP, SP, oP = (ps(n, [P, 2, 512]) for n in ("past_zP", "past_SP", "past_oP"))
        back = ps("past_back", [P, 512])
        zeroed, q_ready = sem("past_zeroed"), sem("past_q_ready")
        kv_in = [sem(f"past_in{s}") for s in range(2)]
        z_made, z_taken, ln_step, sp_done = (sem("past_" + n) for n in ("zmade", "ztaken", "lnstep", "spdone"))
        s_made, arg_done, w_done, o_made, o_taken = (sem("past_" + n) for n in ("smade", "argdone", "wdone", "omade", "otaken"))
        back_made, added = sem("past_back_made"), sem("past_added")
        with nc.Block() as block:
            @block.sync
            def _(sp):
                def load(i, s):
                    one = lambda t: t[ds(i * 2 + s, 1)] if not isinstance(i, int) else t[2 * i + s:2 * i + s + 1]
                    sp.dma_start(kT[:, s, :, :], one(T["cache_kT"]).rearrange("a p k n -> (a p) k n")).then_inc(kv_in[s], 16)
                    sp.dma_start(vb[:, s, :, :], one(T["cache_v"]).rearrange("a (j p) n -> p (a j) n", p=P)
                                 ).then_inc(kv_in[s], 16)
                for s in range(2):
                    load(0, s)
                with sp.Fori(1, NSEQ // 2) as i:
                    for s in range(2):
                        sp.wait_ge(o_made, i * 2 - (1 - s))
                        load(i, s)

            @block.gpsimd
            def _(pool):
                pool.memset(qB[:, :, :, :], 0.0).then_inc(zeroed, 1)
                pool.wait_ge(zeroed, 1)
                for g in range(2):
                    r = slice(64 * g, 64 * g + 64)
                    if g:
                        pool.wait_ge(q_ready, g)
                    pool.tensor_copy(qB[r, :, g, :], m.qkT[r, 0:4, SEQ:TOK]).then_inc(q_ready, 1)

            @block.tensor
            def _(pe):
                pe.wait_ge(q_ready, 2)

                def pair(i, first):
                    for s in range(2):
                        pe.wait_ge(kv_in[s], i * 32 + 32)
                        if not first:
                            pe.wait_ge(z_taken, i * 2 - (1 - s))
                        for j in range(NJ):
                            for k in range(4):
                                mm = pe.matmul(zP[:, s, j * P + k * 32:j * P + k * 32 + 32], kT[:, s, k, j * P:(j + 1) * P],
                                               qB[:, k, :, ds(i * 32 + s * LSEQ, LSEQ)], start=True, stop=True)
                        mm.then_inc(z_made, 1)
                    for s in range(2):
                        pe.wait_ge(sp_done, i * 2 + (s + 1))
                        if not first:
                            pe.wait_ge(arg_done, i * 2 - (1 - s))
                        out = SP[:, s, :].rearrange("p (j c) -> p j c", j=NJ)
                        pe.matmul(out, m.from_[:, :], a[:, s, :, :], start=True, stop=False)
                        for j in range(1, NJ):
                            pe.matmul(out[:, 0:j, :], m.ones[:, :], spread(a[:, s, j, :], 1, j), start=False, stop=False)
                        for j in range(NJ):
                            mm = pe.matmul(out[:, j, :], m.ones[:, :], m.sp_new[:, :, ds(i * 32 + s * LSEQ, LSEQ)],
                                           start=False, stop=(j == NJ - 1))
                        mm.then_inc(s_made, 1)
                    for s in range(2):
                        pe.wait_ge(w_done, i * 2 + (s + 1))
                        if not first:
                            pe.wait_ge(o_taken, i * 2 - (1 - s))
                        for h in range(H):
                            for j in range(NJ):
                                mm = pe.matmul(oP[0:HD, s, h * LSEQ:(h + 1) * LSEQ], vb[:, s, j, h * HD:(h + 1) * HD],
                                               w[:, s, j, h * LSEQ:(h + 1) * LSEQ], start=(j == 0), stop=(j == NJ - 1))
                        mm.then_inc(o_made, 1)
                pair(0, True)
                with pe.Fori(1, NSEQ // 2) as i:
                    pair(i, False)
                pe.wait_ge(o_taken, NSEQ)
                for h in range(H):
                    mm = pe.transpose(back[:, h * HD:(h + 1) * HD], oTs[:, h, :], m.ident[0:HD, 0:HD])
                mm.then_inc(back_made, 1)

            @block.scalar
            def _(act):
                def pair(i, first):
                    for s in range(2):
                        act.wait_ge(z_taken, i * 2 + (s + 1))
                        if not first:
                            act.wait_ge(s_made, i * 2 - (1 - s))
                        act.activation(a[:, s, :, :], z[:, s, :, :], ACT.Abs).then_inc(ln_step, 1)
                        act.wait_ge(ln_step, i * 6 + (3 * s + 1))
                        act.activation(a[:, s, :, :], a[:, s, :, :], ACT.Exp, scale=-1.0).then_inc(ln_step, 1)
                        act.wait_ge(ln_step, i * 6 + (3 * s + 2))
                        act.activation(a[:, s, :, :], a[:, s, :, :], ACT.Ln, bias=1.0).then_inc(ln_step, 1)
                    for s in range(2):
                        act.wait_ge(arg_done, i * 2 + (s + 1))
                        if not first:
                            act.wait_ge(o_made, i * 2 - (1 - s))
                        act.activation(w[:, s, :, :], z[:, s, :, :], ACT.Exp).then_inc(w_done, 1)
                pair(0, True)
                with act.Fori(1, NSEQ // 2) as i:
                    pair(i, False)

            @block.vector
            def _(dve):
                def pair(i, first):
                    flat = lambda t, s: t[:, s, :, :].rearrange("p j c -> p (j c)")
                    for s in range(2):
                        dve.wait_ge(z_made, i * 2 + (s + 1))
                        if not first:
                            dve.wait_ge(w_done, i * 2 - (1 - s))
                        dve.tensor_scalar(flat(z, s), zP[:, s, :], SC, None, ALU.mult).then_inc(z_taken, 1)
                    for s in range(2):
                        dve.wait_ge(ln_step, i * 6 + (3 * s + 3))
                        dve.scalar_tensor_tensor(flat(a, s), flat(z, s), 0.0, flat(a, s), ALU.max, ALU.add
                                                 ).then_inc(sp_done, 1)
                    for s in range(2):
                        dve.wait_ge(s_made, i * 2 + (s + 1))
                        dve.tensor_tensor(flat(z, s), flat(z, s), SP[:, s, :], ALU.subtract).then_inc(arg_done, 1)
                    for s in range(2):
                        dve.wait_ge(o_made, i * 2 + (s + 1))
                        dve.tensor_copy(oTs[:, :, ds(i * 32 + s * LSEQ, LSEQ)],
                                        oP[0:HD, s, 0:P].rearrange("p (h q) -> p h q", h=H)).then_inc(o_taken, 1)
                pair(0, True)
                with dve.Fori(1, NSEQ // 2) as i:
                    pair(i, False)
                dve.wait_ge(back_made, 1)
                dve.tensor_tensor(m.oN[:, NT - 1, 0:512], m.oN[:, NT - 1, 0:512], back[:, :], ALU.add).then_inc(added, 1)


def add_residual(nc, m, T, sem, sb, name, src, base, g_post, gate, store, keep):
    gates = sb(name + "_gates", [P, 2, D])
    post = sb(name + "_post", [P, D])
    junk = sb(name + "_junk", [P, 2, D])
    ld, gate_ready, squared, mean, rstd, step, stored = (
        sem(f"{name}_{n}") for n in ("ld", "gate", "sq", "mean", "rstd", "step", "stored"))
    base_in = [sem(f"{name}_base{t}") for t in range(NT)]
    with nc.Block() as block:
        @block.sync
        def _(sp):
            sp.dma_start(post[:, :], g_post.partition_broadcast(P)).then_inc(ld, 16)
            sp.dma_start(gates[:, 0, :], T["gates"][gate, 0].partition_broadcast(P)).then_inc(ld, 16)
            for b in range(NSEQ):
                sp.dma_start(gates[b * LSEQ:(b + 1) * LSEQ, 1, :],
                             T["gates"][gate, b + 1].partition_broadcast(LSEQ)).then_inc(ld, 16)
            for t in range(NT):
                sp.dma_start(keep[:, t, :], base[t * P:(t + 1) * P, :]).then_inc(base_in[t], 16)
            for t in range(NT):
                sp.wait_ge(step, 2 * t + 2)
                sp.dma_start(store[t * P:(t + 1) * P, :], keep[:, t, :]).then_inc(stored, 16)
            sp.wait_ge(stored, 16 * NT)

        @block.scalar
        def _(act):
            for t in range(NT):
                if t >= 2:
                    act.wait_ge(squared, t - 1)
                act.activation(junk[:, t % 2, :], src[:, t, :], ACT.Square,
                               accum_out=m.stat[:, t:t + 1]).then_inc(squared, 1)

        @block.gpsimd
        def _(pool):
            pool.wait_ge(mean, 1)
            pool.tensor_tensor(m.rstd[:, :], m.stat[:, :], m.mhalf[:, 0:NT], ALU.pow).then_inc(rstd, 1)

        @block.vector
        def _(dve):
            dve.wait_ge(ld, 16 * (2 + NSEQ))
            dve.tensor_tensor(gates[:, :, :], gates[:, :, :], spread(post[:, :], 1, 2), ALU.mult).then_inc(gate_ready, 1)
            dve.wait_ge(squared, NT)
            dve.tensor_scalar(m.stat[:, :], m.stat[:, :], 1.0 / D, EPS, ALU.mult, ALU.add).then_inc(mean, 1)
            dve.wait_ge(rstd, 1)
            dve.wait_ge(gate_ready, 1)
            for t in range(NT):
                dve.scalar_tensor_tensor(src[:, t, :], src[:, t, :], m.rstd[:, t:t + 1], gates[:, t // (NT - 1), :],
                                         ALU.mult, ALU.mult).then_inc(step, 1)
                dve.wait_ge(step, 2 * t + 1)
                dve.wait_ge(base_in[t], 16)
                dve.tensor_tensor(keep[:, t, :], keep[:, t, :], src[:, t, :], ALU.add).then_inc(step, 1)


def mixer_columns(nc, m, T, sem, sb, ps, oT, junk):
    NH = 2 * NT
    g = sb("g_mix", [P, KD])
    stat, rstd = sb("mix_stat", [P, NH]), sb("mix_rstd", [P, NH])
    pr, sa = ps("mixc_p", [P, 2, 512]), ps("mixc_s", [P, 2, 512])
    ld, squared, mean, rooted, normed, turned, taken = (
        sem("mixc_" + n) for n in ("ld", "sq", "mean", "rstd", "normed", "turned", "taken"))
    with nc.Block() as block:
        @block.sync
        def _(sp):
            sp.dma_start(g[:, :], T["g_mix"]).then_inc(ld, 16)

        @block.scalar
        def _(act):
            for n in range(NH):
                t, half = n // 2, n % 2
                if n >= 2:
                    act.wait_ge(squared, n - 1)
                act.activation(junk[:, n % 2, :], m.oN[:, t, half * 512:(half + 1) * 512], ACT.Square,
                               accum_out=stat[:, n:n + 1]).then_inc(squared, 1)

        @block.gpsimd
        def _(pool):
            pool.wait_ge(mean, 1)
            pool.tensor_tensor(rstd[:, :], stat[:, :], m.mhalf[:, :], ALU.pow).then_inc(rooted, 1)

        @block.vector
        def _(dve):
            dve.wait_ge(squared, NH)
            dve.tensor_scalar(stat[:, :], stat[:, :], 1.0 / 512, EPS, ALU.mult, ALU.add).then_inc(mean, 1)
            dve.wait_ge(rooted, 1)
            for n in range(NH):
                v = m.oN[:, n // 2, (n % 2) * 512:(n % 2 + 1) * 512]
                dve.tensor_scalar(v, v, rstd[:, n:n + 1], None, ALU.mult).then_inc(normed, 1)
            dve.wait_ge(ld, 16)
            for k in range(KD):
                dve.wait_ge(turned, k + 1)
                dve.tensor_scalar(oT[:, k, 0:SEQ], pr[:, k % 2, :], g[:, k:k + 1], None, ALU.mult).then_inc(taken, 1)
                dve.tensor_scalar(oT[:, k, SEQ:], sa[:, k % 2, 0:P], g[:, k:k + 1], None, ALU.mult).then_inc(taken, 1)

        @block.tensor
        def _(pe):
            pe.wait_ge(normed, NH)
            for k in range(KD):
                if k >= 2:
                    pe.wait_ge(taken, 2 * (k - 1))
                for t in range(NT):
                    out = pr[:, k % 2, t * P:(t + 1) * P] if t < NT - 1 else sa[:, k % 2, 0:P]
                    mm = pe.transpose(out, m.oN[:, t, k * P:(k + 1) * P], m.ident[:, :])
                mm.then_inc(turned, 1)


def mix(nc, m, T, sem, sb, psctx):
    with scope(nc.sbuf_tensor) as tmp:
        x1 = tmp("x1", [P, NT, D])
        mx = tmp("mx", [P, NT, D])
        with scope(nc.sbuf_tensor) as tmp2:
            oT = tmp2("oT", [P, KD, TOK])
            w = tmp2("w_out", [P, KD, D])
            with psctx() as ps:
                mixer_columns(nc, m, T, sem, tmp2, ps, oT, mx[:, 0, :].rearrange("p (a n) -> p a n", a=2))
            w_in, made, taken = [sem(f"w_out{k}") for k in range(KD)], sem("mix_made"), sem("mix_taken")
            with psctx() as ps, nc.Block() as block:
                acc = ps("mix_ps", [P, 2, 2, 512])

                @block.sync
                def _(sp):
                    for k in range(KD):
                        sp.dma_start(w[:, k, :], T["w_out"][k * P:(k + 1) * P, :]).then_inc(w_in[k], 16)

                @block.tensor
                def _(pe):
                    for t in range(NT):
                        if t >= 2:
                            pe.wait_ge(taken, t - 1)
                        for k in range(KD):
                            if t == 0:
                                pe.wait_ge(w_in[k], 16)
                            for h in range(2):
                                mm = pe.matmul(acc[:, t % 2, h, :], oT[:, k, t * P:(t + 1) * P],
                                               w[:, k, h * 512:(h + 1) * 512], start=(k == 0), stop=(k == KD - 1))
                        mm.then_inc(made, 1)

                @block.scalar
                def _(act):
                    for t in range(NT):
                        act.wait_ge(made, t + 1)
                        act.copy(mx[:, t, :].rearrange("p (h n) -> p h n", h=2), acc[:, t % 2, :, :]).then_inc(taken, 1)
        with scope(nc.sbuf_tensor) as tmp2:
            add_residual(nc, m, T, sem, tmp2, "res1", mx, T["x"], T["g_post_mix"], 0, T["x1"], x1)
        m.junk = mx
        with scope(nc.sbuf_tensor) as tmp2:
            h2T = tmp2("h2T", [P, KD, TOK])
            with psctx() as ps:
                norm_to_columns(nc, m, sem, ps, "n2", None, x1, h2T, 1)
            split, low = sem("h2_split"), sem("h2_low")
            with nc.Block() as block:
                @block.vector
                def _(dve):
                    for k in range(KD):
                        dve.tensor_copy(m.h2h[:, k, :], h2T[:, k, :]).then_inc(split, 1)
                    for k in range(KD):
                        dve.wait_ge(split, k + 1)
                        dve.tensor_tensor(m.h2l[:, k, :], h2T[:, k, :], m.h2h[:, k, :].bitcast(F32), ALU.subtract
                                          ).then_inc(low, 1)

            def sink(act, acc, made, taken):
                with act.Fori(0, 4) as i:
                    for s in range(2):
                        act.wait_ge(made, i * 2 + (s + 1))
                        act.copy(m.qhT[:, ds(i * 2 + s, 1), :].rearrange("p a (h n) -> p (a h) n", h=2),
                                 acc[:, s, :, 0:HALF]).then_inc(taken, 1)
            with psctx() as ps:
                column_products(nc, m, sem, tmp2, ps, "pq", T["w_pq"], 8, h2T, sink)


HT = 64
NHT = TOK // HT
GB = 4
FIRSTB, TOPB, STEPB = 2, 6, 8
NPRE = FIRSTB + NT * (TOPB + STEPB)


class ExpertIn:

    def __init__(self, sem, sb):
        self.raw, self.high, self.low = sb("ur", [P, 2, KD, P]), sb("uh", [P, 2, KD, P], F32R), sb("ul", [P, 2, KD, P], F32R)
        self.came = [sem(f"u_in{n}") for n in range(2)]
        self.high_done, self.low_done = sem("uh_done"), sem("ul_done")

    def load(self, eng, T, n, s, first=False):
        if not first:
            eng.wait_ge(self.high_done, n - 1)
            eng.wait_ge(self.low_done, n - 1)
        src = T["uT"][n] if isinstance(n, int) else T["uT"][ds(n, 1)].rearrange("a p k c -> (a p) k c")
        eng.dma_start(self.raw[:, s, :, :], src).then_inc(self.came[s], 16)

    def split_low(self, eng, n, s):
        eng.wait_ge(self.high_done, n + 1)
        eng.tensor_tensor(self.low[:, s, :, :], self.raw[:, s, :, :], self.high[:, s, :, :].bitcast(F32), ALU.subtract
                          ).then_inc(self.low_done, 1)


def route(nc, m, T, sem, sb, psctx):
    NG = 2 * H
    NC = TOPK * TOPK
    skb = sb("skb", [P, 2, NKEY])
    rowv = lambda a, b: m.oN[:, a:b, :].rearrange("p a n -> p (a n)")
    s = rowv(0, 2).rearrange("p (g k) -> p g k", g=NG)
    cand = rowv(2, 4).rearrange("p (h c) -> p h c", h=H)
    qs = m.oN[:, 4, :].rearrange("p (h t) -> p h t", h=H)
    top, itop, itopf = sb("top", [P, NG, TOPK]), sb("itop", [P, NG, TOPK], U32), sb("itopf", [P, NG, TOPK])
    best, ci = sb("best", [P, H, TOPK]), sb("ci", [P, H, TOPK], U32)
    cab, cabf = sb("cab", [P, 2, H, TOPK], U32), sb("cabf", [P, 2, H, TOPK])
    hit = rowv(2, 4).rearrange("p (h r c) -> p h r c", h=H, r=TOPK)
    picks = sb("picks", [P, 3, H, TOPK])
    zs, rz = sb("zs", [P, H]), sb("rz", [P, H])
    picksT = sb("picksT", [P, 3, P])
    iota16, iota = sb("iota16", [P, TOPK]), sb("iota", [P, NKEY])
    UN = 8
    hot1, hot2 = sb("hot1", [P, UN, NKEY]), sb("hot2", [P, UN, NKEY])
    Gs = sb("Gs", [P, 2 * NKEY, HT])
    ga = sb("pre_ga", [P, 2, TOK])
    u = m.u
    setup, zeroed, keys_in = sem("route_setup"), sem("route_zeroed"), sem("keys_in")
    q_in, s_made, s_taken = sem("rq_in"), sem("rs_made"), sem("rs_taken")
    stepA, stepB, stepC = sem("routeA"), sem("routeB"), sem("routeC")
    exp_done, t_made, t_taken = sem("r_exp"), sem("rt_made"), sem("rt_taken")
    hots, g_made, g_taken = sem("hots"), sem("g_made"), sem("g_taken")
    g_out = [sem(f"g_out{n}") for n in range(2)]
    h_made, gelu_done, h_out = sem("pre_hmade"), sem("pre_gelu"), [sem(f"pre_out{n}") for n in range(2)]
    NA, NB, NCC = 5 * NG + 1, 5 * H + 2, 12
    EV = UN // 4
    STEPS = P // UN
    HS = STEPS // 2
    HB = STEPB // 2
    TB = TOPB + STEPB
    slots = lambda n: 8 * n

    def u_free(eng, n):
        eng.wait_ge(h_made, n * 2 - 2)

    with psctx() as ps, nc.Block() as block:
        sP = ps("route_s", [P, H, NKEY])
        tP = ps("route_t", [P, 512])
        gP = ps("route_g", [P, 2, 4, NKEY])
        hP = ps("pre_h", [P, 2, 512])

        @block.gpsimd
        def _(pool):
            pool.iota(iota[:, :], pattern=[[1, NKEY]], base=0, channel_multiplier=0,
                      allow_small_or_imprecise_dtypes=True).then_inc(setup, 1)
            pool.iota(iota16[:, :], pattern=[[1, TOPK]], base=0, channel_multiplier=0,
                      allow_small_or_imprecise_dtypes=True).then_inc(setup, 1)
            pool.memset(skb[:, :, :], 0.0).then_inc(zeroed, 1)
            for n in range(2):
                u.split_low(pool, n, n)
            with pool.Fori(1, NPRE // 2 + 1) as i:
                for n in range(2):
                    u_free(pool, i * 2 + n)
                    u.split_low(pool, i * 2 + n, n)

        @block.sync
        def _(sp):
            def store(n, slot):
                sp.wait_ge(gelu_done, n * 2 + 2)
                dst = T["HG"][n] if isinstance(n, int) else T["HG"][ds(n, 1)].rearrange("a p t -> (a p) t")
                sp.dma_start(dst, ga[:, slot, :]).then_inc(h_out[slot], 16)

            def blocks(base, count):
                for n in range(count):
                    u.load(sp, T, base + (n + 2), n % 2)
                    store(base + n, n % 2)

            for n in range(2):
                u.load(sp, T, n, n, True)
            sp.dma_start(qs, m.qhT[:, :, 0:P]).then_inc(q_in, 16)
            sp.wait_ge(zeroed, 1)
            for c in range(2):
                sp.dma_start(skb[64 * c:64 * c + 64, c, :], T["sub_keys"][64 * c:64 * c + 64, :]).then_inc(keys_in, 16)
            blocks(0, FIRSTB)

            def tile(i, last):
                with sp.Fori(0, TOPB // 2) as j:
                    blocks(i * TB + j * 2 + FIRSTB, 2)
                if not last:
                    sp.wait_ge(s_made, i * 2 + 2)
                    sp.dma_start(qs, m.qhT[:, :, ds(i * P + P, P)]).then_inc(q_in, 16)
                with sp.Fori(0, STEPB // 2) as j:
                    blocks(i * TB + j * 2 + (FIRSTB + TOPB), 2)

            with sp.Fori(0, NT - 1) as i:
                tile(i, False)
            tile(NT - 1, True)
            for n in range(2):
                sp.wait_ge(h_out[n], 16 * (NPRE // 2))
            for hf in range(2):
                sp.wait_ge(g_out[hf], 16 * NT)

        @block.tensor
        def _(pe):
            def scores(i, first):
                pe.wait_ge(q_in, i * 16 + 16)
                if first:
                    pe.wait_ge(keys_in, 32)
                for part in range(2):
                    if part or not first:
                        pe.wait_ge(s_taken, i * 2 + part)
                    for h in range(4):
                        mm = pe.matmul(sP[:, 2 * h:2 * h + 2, :], qs[:, part * 4 + h, :], skb[:, :, :],
                                       start=True, stop=True)
                    mm.then_inc(s_made, 1)

            def hidden(n, slot, half, first=False):
                if half == 0:
                    pe.wait_ge(u.low_done, n + 1)
                    pe.wait_ge(u.high_done, n + 1)
                if not first:
                    pe.wait_ge(gelu_done, n * 2 + (half - 1))
                c = slice(half * HALF, (half + 1) * HALF)
                for k in range(KD):
                    for w, x in ((u.high, m.h2h), (u.high, m.h2l), (u.low, m.h2h)):
                        mm = pe.matmul(hP[:, half, 0:HALF], w[:, slot, k, :], x[:, k, c],
                                       start=(k == 0 and w is u.high and x is m.h2h), stop=(k == KD - 1 and w is u.low))
                mm.then_inc(h_made, 1)

            def token_step(n):
                for v in range(UN):
                    pe.wait_ge(hots, n * UN + (v + 1))
                    if v % 4 == 0:
                        pe.wait_ge(g_taken, n * EV + (v // 4 + 1))
                    pe.matmul(gP[:, v // 4, v % 4, :], hot1[:, v, :], hot2[:, v, :], start=True, stop=True
                              ).then_inc(g_made, 1)

            def tile(i, last):
                with pe.Fori(0, TOPB // 2) as j:
                    for n in range(2):
                        for half in range(2):
                            hidden(i * TB + j * 2 + (FIRSTB + n), n, half)
                pe.wait_ge(stepC, i * NCC + NCC)
                for c in range(3):
                    mm = pe.transpose(tP[:, c * P:(c + 1) * P], picks[:, c, :, :].rearrange("p h r -> p (h r)"), m.ident[:, :])
                mm.then_inc(t_made, 1)
                if not last:
                    scores(i + 1, False)
                for q in range(STEPS):
                    token_step(i * STEPS + q)
                    n = FIRSTB + TOPB + q // 2
                    hidden(i * TB + n, n % 2, q % 2)

            pe.sem_inc(g_made, UN)
            scores(0, True)
            for n in range(FIRSTB):
                for half in range(2):
                    hidden(n, n % 2, half, n == 0)
            with pe.Fori(0, NT - 1) as i:
                tile(i, False)
            tile(NT - 1, True)

        @block.scalar
        def _(act):
            def split(n, slot, arrived, first=False):
                act.wait_ge(u.came[slot], arrived)
                if not first:
                    u_free(act, n)
                act.copy(u.high[:, slot, :, :], u.raw[:, slot, :, :]).then_inc(u.high_done, 1)

            def gelu(n, slot, half, stored=None):
                act.wait_ge(h_made, n * 2 + (half + 1))
                if stored is not None and half == 0:
                    act.wait_ge(h_out[slot], stored)
                act.activation(ga[:, slot, half * HALF:(half + 1) * HALF], hP[:, half, 0:HALF], ACT.Gelu_apprx_tanh
                               ).then_inc(gelu_done, 1)

            def take(i, first):
                for part in range(2):
                    act.wait_ge(s_made, i * 2 + (part + 1))
                    if not first and part == 0:
                        act.wait_ge(stepA, i * NA)
                    act.copy(s[:, 8 * part:8 * part + 8, :], sP[:, :, :]).then_inc(s_taken, 1)

            def gelu_and_split(i, n, half):
                gelu(i * TB + n, n % 2, half, i * slots(TB) + slots(n - n % 2) if half == 0 else None)
                if half:
                    split(i * TB + (n + 2), n % 2, i * slots(TB) + slots(n - n % 2 + 4))

            def tile(i, first, last):
                for n in range(TOPB):
                    for half in range(2):
                        gelu_and_split(i, FIRSTB + n, half)
                act.wait_ge(stepB, i * (NB + 1) + (NB + 1))
                act.activation(best[:, :, :], best[:, :, :], ACT.Exp).then_inc(exp_done, 1)
                act.wait_ge(t_made, i + 1)
                act.copy(picksT[:, :, :].rearrange("p c t -> p (c t)"), tP[:, 0:3 * P]).then_inc(t_taken, 1)
                if not last:
                    take(i + 1, False)
                for q in range(STEPS):
                    hf = q // HS
                    if not first and q % HS == 0:
                        act.wait_ge(g_out[hf], i * 16)
                    for e in range(EV):
                        act.wait_ge(g_made, (i * STEPS + q) * UN + (UN + 4 * (e + 1)))
                        t = q % HS * UN + 4 * e
                        act.copy(Gs[:, hf * NKEY:(hf + 1) * NKEY, t:t + 4].rearrange("p j t -> p t j"), gP[:, e, :, :]
                                 ).then_inc(g_taken, 1)
                    gelu_and_split(i, FIRSTB + TOPB + q // 2, q % 2)
                    if q % HS == HS - 1:
                        act.wait_ge(g_taken, (i * STEPS + q) * EV + 2 * EV)
                        act.dma_start(T["G"][ds(i * 2 + hf, 1)].rearrange("a p j t -> (a p) j t") if not isinstance(i, int)
                                      else T["G"][i * 2 + hf], Gs[:, hf * NKEY:(hf + 1) * NKEY, :]).then_inc(g_out[hf], 16)

            act.sem_inc(g_taken, EV)
            for n in range(2):
                split(n, n, 16, True)
            take(0, True)
            for n in range(FIRSTB):
                gelu(n, n % 2, 0, slots(n - n % 2) if n >= 2 else None)
                gelu(n, n % 2, 1)
                split(n + 2, n % 2, slots(n - n % 2 + 4))
            tile(0, True, False)
            with act.Fori(1, NT - 1) as i:
                tile(i, False, False)
            tile(NT - 1, False, True)

        @block.vector
        def _(dve):
            def after(what, value):
                value = value if isinstance(value, int) else dve.to_reg(value)
                dve.wait_ge(setup, 2)
                dve.wait_ge(what, value)

            def tile(i, first):
                a0, b0, c0 = i * NA, i * (NB + 1), i * NCC
                after(s_taken, i * 2 + 2)
                for g in range(NG):
                    dve.max(top[:, g, 0:8], s[:, g, :]).then_inc(stepA, 1)
                after(stepA, a0 + NG)
                for g in range(NG):
                    dve.max_index(itop[:, g, 0:8], top[:, g, 0:8], s[:, g, :]).then_inc(stepA, 1)
                after(stepA, a0 + 2 * NG)
                for g in range(NG):
                    dve.match_replace(s[:, g, :], top[:, g, 0:8], s[:, g, :], -3e38).then_inc(stepA, 1)
                after(stepA, a0 + 3 * NG)
                for g in range(NG):
                    dve.max(top[:, g, 8:16], s[:, g, :]).then_inc(stepA, 1)
                after(stepA, a0 + 4 * NG)
                for g in range(NG):
                    dve.max_index(itop[:, g, 8:16], top[:, g, 8:16], s[:, g, :]).then_inc(stepA, 1)
                dve.wait_ge(stepA, a0 + 5 * NG)
                dve.tensor_copy(itopf[:, :, :], itop[:, :, :]).then_inc(stepA, 1)
                dve.tensor_tensor(cand[:, :, :].rearrange("p h (a b) -> p h a b", a=TOPK),
                                  spread(top[:, 0:NG:2, :], 3, TOPK), spread(top[:, 1:NG:2, :], 2, TOPK), ALU.add
                                  ).then_inc(stepB, 1)
                after(stepB, b0 + 1)
                for h in range(H):
                    dve.max(best[:, h, 0:8], cand[:, h, :]).then_inc(stepB, 1)
                after(stepB, b0 + (1 + H))
                for h in range(H):
                    dve.max_index(ci[:, h, 0:8], best[:, h, 0:8], cand[:, h, :]).then_inc(stepB, 1)
                after(stepB, b0 + (1 + 2 * H))
                for h in range(H):
                    dve.match_replace(cand[:, h, :], best[:, h, 0:8], cand[:, h, :], -3e38).then_inc(stepB, 1)
                after(stepB, b0 + (1 + 3 * H))
                for h in range(H):
                    dve.max(best[:, h, 8:16], cand[:, h, :]).then_inc(stepB, 1)
                after(stepB, b0 + (1 + 4 * H))
                for h in range(H):
                    dve.max_index(ci[:, h, 8:16], best[:, h, 8:16], cand[:, h, :]).then_inc(stepB, 1)
                dve.tensor_copy(zs[:, :], best[:, :, 0]).then_inc(stepB, 1)
                dve.wait_ge(stepB, b0 + NB)
                dve.tensor_tensor(best[:, :, :], best[:, :, :], spread(zs[:, :], 2, TOPK), ALU.subtract
                                  ).then_inc(stepB, 1)
                dve.tensor_scalar(cab[:, 0, :, :], ci[:, :, :], 4, None, ALU.logical_shift_right).then_inc(stepC, 1)
                dve.tensor_scalar(cab[:, 1, :, :], ci[:, :, :], 15, None, ALU.bitwise_and).then_inc(stepC, 1)
                dve.wait_ge(stepC, c0 + 2)
                dve.tensor_copy(cabf[:, :, :, :], cab[:, :, :, :]).then_inc(stepC, 1)
                dve.wait_ge(stepA, a0 + NA)
                if not first:
                    dve.wait_ge(t_made, i)
                for c in range(2):
                    dve.wait_ge(stepC, c0 + (3 + 3 * c))
                    dve.tensor_tensor(hit[:, :, :, :], spread(cabf[:, c, :, :], 3, TOPK),
                                      spread(spread(iota16[:, :], 1, TOPK), 1, H), ALU.is_equal).then_inc(stepC, 1)
                    dve.wait_ge(stepC, c0 + (4 + 3 * c))
                    dve.tensor_tensor(hit[:, :, :, :], hit[:, :, :, :], spread(itopf[:, c:NG:2, :], 2, TOPK), ALU.mult
                                      ).then_inc(stepC, 1)
                    dve.wait_ge(stepC, c0 + (5 + 3 * c))
                    dve.tensor_reduce(picks[:, c, :, :], hit[:, :, :, :], AX, ALU.add).then_inc(stepC, 1)
                dve.wait_ge(exp_done, i + 1)
                dve.tensor_reduce(zs[:, :], best[:, :, :], AX, ALU.add).then_inc(stepC, 1)
                dve.wait_ge(stepC, c0 + 10)
                dve.reciprocal(rz[:, :], zs[:, :]).then_inc(stepC, 1)
                dve.wait_ge(stepC, c0 + 11)
                dve.tensor_tensor(picks[:, 2, :, :], best[:, :, :], spread(rz[:, :], 2, TOPK), ALU.mult
                                  ).then_inc(stepC, 1)
                after(t_taken, i + 1)
                with dve.Fori(0, STEPS) as q:
                    for u in range(UN):
                        dve.wait_ge(g_made, (i * STEPS + q) * UN + (u + 1))
                        t = ds(q * UN + u, 1)
                        dve.tensor_scalar(hot1[:, u, :], iota[:, :], picksT[:, 0, t], None, ALU.is_equal)
                        dve.tensor_scalar(hot2[:, u, :], iota[:, :], picksT[:, 1, t], picksT[:, 2, t],
                                          ALU.is_equal, ALU.mult).then_inc(hots, 1)

            tile(0, True)
            with dve.Fori(1, NT) as i:
                tile(i, False)


def experts(nc, m, T, sem, sb, psctx):
    NB = NKEY - NPRE
    NGR = NB // GB
    Y = m.oN
    u = m.u
    with scope(nc.sbuf_tensor) as tmp, psctx() as ps, nc.Block() as block:
        vr, vh, vl = tmp("vr", [P, 2, D]), tmp("vh", [P, GB, D], F32R), tmp("vl", [P, GB, D], F32R)
        gr = tmp("gr", [P, NHT, GB * HT])
        ga = tmp("ga", [P, 2, TOK])
        ah, al = tmp("ah", [P, GB, TOK], F32R), tmp("al", [P, GB, TOK], F32R)
        hP = ps("ex_h", [P, 2, 2, 512])
        yP = ps("ex_y", [P, 4, 512])
        v_in = [sem(f"v_in{n}") for n in range(2)]
        g_in = sem("G_in")
        vh_done, vl_done = sem("vh_done"), sem("vl_done")
        h_made, gelu_done, weighted, ah_done, al_done = (sem("ex_" + n) for n in ("hmade", "gelu", "weighted", "ah", "al"))
        y_made, y_taken, y_zero = sem("ex_ymade"), sem("ex_ytaken"), sem("ex_yzero")
        NY = 2 * NT
        YB = [max(y for y in range(NY) if y % 4 == a) for a in range(4)]
        Glayout = T["G"].rearrange("t p j n -> p t (j n)")

        @block.sync
        def _(sp):
            def load_g(g, first=False):
                if not first:
                    sp.wait_ge(weighted, g * GB)
                start = g * (GB * HT) + NPRE * HT
                sp.dma_start(gr[:, :, :], Glayout[:, :, start:start + GB * HT] if first
                             else Glayout[:, :, ds(start, GB * HT)]).then_inc(g_in, 16)

            load_g(0, True)
            with sp.Fori(0, NGR - 1) as g:
                for s in range(GB):
                    u.load(sp, T, g * GB + (NPRE + s + 2), s % 2)
                load_g(g + 1)
            for s in range(GB - 2):
                u.load(sp, T, NKEY - 2 + s, s % 2)

        @block.gpsimd
        def _(pool):
            def load_v(n, s, first=False):
                if not first:
                    pool.wait_ge(vl_done, n - 1)
                    pool.wait_ge(vh_done, n - 1)
                src = (T["v_tab"][NPRE + n] if isinstance(n, int)
                       else T["v_tab"][ds(n + NPRE, 1)].rearrange("a p n -> (a p) n"))
                pool.dma_start(vr[:, s, :], src).then_inc(v_in[s], 16)

            for n in range(2):
                load_v(n, n, True)
            with pool.Fori(1, NB // 2) as i:
                for s in range(2):
                    load_v(i * 2 + s, s)

        @block.tensor
        def _(pe):
            def hidden(n, s, first=False):
                pe.wait_ge(u.low_done, n + (NPRE + 1))
                pe.wait_ge(u.high_done, n + (NPRE + 1))
                if not first:
                    pe.wait_ge(gelu_done, n - 1)
                for k in range(KD):
                    for w, x in ((u.high, m.h2h), (u.high, m.h2l), (u.low, m.h2h)):
                        for half in range(2):
                            mm = pe.matmul(hP[:, s, half, 0:HALF], w[:, s, k, :], x[:, k, half * HALF:(half + 1) * HALF],
                                           start=(k == 0 and w is u.high and x is m.h2h),
                                           stop=(k == KD - 1 and w is u.low))
                mm.then_inc(h_made, 1)

            def outputs(g, first=False):
                pe.wait_ge(al_done, g * GB + GB)
                pe.wait_ge(vl_done, g * GB + GB)
                pe.wait_ge(vh_done, g * GB + GB)
                for y in range(NY):
                    t, d = y // 2, slice((y % 2) * 512, (y % 2 + 1) * 512)
                    if y >= 4 or not first:
                        before = y - 4 if y >= 4 else (YB[y] - NY)
                        pe.wait_ge(y_taken, g * NY + (before + 1))
                    for b in range(GB):
                        for a, v in ((ah, vh), (al, vh), (ah, vl)):
                            mm = pe.matmul(yP[:, y % 4, :], a[:, b, t * P:(t + 1) * P], v[:, b, d],
                                           start=(b == 0 and a is ah and v is vh), stop=(b == GB - 1 and v is vl))
                    mm.then_inc(y_made, 1)

            hidden(0, 0, True)
            hidden(1, 1, True)
            for s in range(2, GB + 1):
                hidden(s, s % 2)
            outputs(0, True)
            with pe.Fori(1, NGR - 1) as g:
                for s in range(1, GB + 1):
                    hidden(g * GB + s, s % 2)
                outputs(g)
            for s in range(1, GB):
                hidden(NB - GB + s, s % 2)
            outputs(NGR - 1)

        @block.scalar
        def _(act):
            def split_u(g, b):
                s = b % 2
                act.wait_ge(u.came[s], g * (8 * GB) + (8 * NPRE + 16 * (b // 2) + 16))
                act.wait_ge(h_made, g * GB + (b - 1))
                act.copy(u.high[:, s, :, :], u.raw[:, s, :, :]).then_inc(u.high_done, 1)

            def body(g, first, last):
                for s in range(GB):
                    n = g * GB + s
                    act.wait_ge(h_made, n + 1)
                    if not (first and s < 2):
                        act.wait_ge(al_done, n - 1)
                    act.activation(ga[:, s % 2, :].rearrange("p (h n) -> p h n", h=2), hP[:, s % 2, :, 0:HALF],
                                   ACT.Gelu_apprx_tanh).then_inc(gelu_done, 1)
                    if not (last and s >= GB - 2):
                        split_u(g, s + 2)
                    act.wait_ge(v_in[s % 2], g * (8 * GB) + (16 * (s // 2) + 16))
                    if not first and s == 0:
                        act.wait_ge(y_made, g * NY)
                    act.copy(vh[:, s, :], vr[:, s % 2, :]).then_inc(vh_done, 1)

            body(0, True, False)
            with act.Fori(1, NGR - 1) as g:
                body(g, False, False)
            body(NGR - 1, False, True)

        @block.vector
        def _(dve):
            dve.memset(Y[:, :, :], 0.0).then_inc(y_zero, 1)

            def split_u(n, s):
                u.split_low(dve, n + NPRE, s)

            def body(g, first, last):
                dve.wait_ge(g_in, g * 16 + 16)
                for s in range(GB):
                    n = g * GB + s
                    ga_s = ga[:, s % 2, :]
                    dve.wait_ge(gelu_done, n + 1)
                    dve.tensor_tensor(ga_s.rearrange("p (t n) -> p t n", t=NHT), ga_s.rearrange("p (t n) -> p t n", t=NHT),
                                      gr[:, :, s * HT:(s + 1) * HT], ALU.mult).then_inc(weighted, 1)
                    if not first and s == 0:
                        dve.wait_ge(y_made, g * NY)
                    dve.wait_ge(weighted, n + 1)
                    dve.tensor_copy(ah[:, s, :], ga_s).then_inc(ah_done, 1)
                    dve.wait_ge(ah_done, n + 1)
                    dve.tensor_tensor(al[:, s, :], ga_s, ah[:, s, :].bitcast(F32), ALU.subtract).then_inc(al_done, 1)
                    if not (last and s >= GB - 2):
                        split_u(n + 2, s % 2)
                    dve.wait_ge(vh_done, n + 1)
                    dve.tensor_tensor(vl[:, s, :], vr[:, s % 2, :], vh[:, s, :].bitcast(F32), ALU.subtract
                                      ).then_inc(vl_done, 1)
                for y in range(NY):
                    out = Y[:, y // 2, (y % 2) * 512:(y % 2 + 1) * 512]
                    dve.wait_ge(y_made, g * NY + (y + 1))
                    dve.tensor_tensor(out, out, yP[:, y % 4, :], ALU.add).then_inc(y_taken, 1)

            dve.wait_ge(y_zero, 1)
            body(0, True, False)
            with dve.Fori(1, NGR - 1) as g:
                body(g, False, False)
            body(NGR - 1, False, True)


def stored_experts(nc, m, T, sem, sb, psctx):
    NGR = NPRE // GB
    NY = 2 * NT
    Y = m.oN
    vr, vh, vl = sb("s_vr", [P, GB, D]), sb("s_vh", [P, 2, GB, D], F32R), sb("s_vl", [P, 2, GB, D], F32R)
    ar, ah, al = sb("s_ar", [P, GB, TOK]), sb("s_ah", [P, 2, GB, TOK], F32R), sb("s_al", [P, 2, GB, TOK], F32R)
    gr = sb("s_gr", [P, NHT, GB * HT])
    v_in, a_in = [sem(f"sv_in{n}") for n in range(GB)], [sem(f"sa_in{n}") for n in range(GB)]
    g_in, weighted = sem("sG_in"), sem("s_weighted")
    vh_done, vl_done, ah_done, al_done = sem("s_vh"), sem("s_vl"), sem("s_ah"), sem("s_al")
    y_made, y_taken = sem("s_ymade"), sem("s_ytaken")
    Glayout = T["G"].rearrange("t p j n -> p t (j n)")
    with psctx() as ps, nc.Block() as block:
        yP = ps("s_y", [P, 4, 512])
        YB = [max(y for y in range(NY) if y % 4 == a) for a in range(4)]

        @block.sync
        def _(sp):
            def load(g, first=False):
                if not first:
                    sp.wait_ge(weighted, g * GB)
                at = g * (GB * HT)
                sp.dma_start(gr[:, :, :], Glayout[:, :, at:at + GB * HT] if first else Glayout[:, :, ds(at, GB * HT)]
                             ).then_inc(g_in, 16)
                for s in range(GB):
                    if not first:
                        sp.wait_ge(al_done, g * GB - (GB - 1 - s))
                    src = T["HG"][g * GB + s] if first else T["HG"][ds(g * GB + s, 1)].rearrange("a p t -> (a p) t")
                    sp.dma_start(ar[:, s, :], src).then_inc(a_in[s], 16)

            load(0, True)
            with sp.Fori(1, NGR) as g:
                load(g)

        @block.gpsimd
        def _(pool):
            def load_v(g, s, first=False):
                if not first:
                    pool.wait_ge(vl_done, g * GB - (GB - 1 - s))
                src = (T["v_tab"][g * GB + s] if first
                       else T["v_tab"][ds(g * GB + s, 1)].rearrange("a p n -> (a p) n"))
                pool.dma_start(vr[:, s, :], src).then_inc(v_in[s], 16)

            for s in range(GB):
                load_v(0, s, True)
            with pool.Fori(1, NGR) as g:
                for s in range(GB):
                    load_v(g, s)

        @block.tensor
        def _(pe):
            def outputs(g, par, first=False):
                pe.wait_ge(al_done, g * GB + GB)
                pe.wait_ge(vl_done, g * GB + GB)
                pe.wait_ge(vh_done, g * GB + GB)
                for y in range(NY):
                    t, d = y // 2, slice((y % 2) * 512, (y % 2 + 1) * 512)
                    if y >= 4 or not first:
                        before = y - 4 if y >= 4 else (YB[y] - NY)
                        pe.wait_ge(y_taken, g * NY + (before + 1))
                    for b in range(GB):
                        for a, v in ((ah, vh), (al, vh), (ah, vl)):
                            mm = pe.matmul(yP[:, y % 4, :], a[:, par, b, t * P:(t + 1) * P], v[:, par, b, d],
                                           start=(b == 0 and a is ah and v is vh), stop=(b == GB - 1 and v is vl))
                    mm.then_inc(y_made, 1)

            outputs(0, 0, True)
            outputs(1, 1)
            with pe.Fori(1, NGR // 2) as i:
                for par in range(2):
                    outputs(i * 2 + par, par)

        @block.scalar
        def _(act):
            def split(g, par, first=False):
                for s in range(GB):
                    act.wait_ge(v_in[s], g * 16 + 16)
                    if not first:
                        act.wait_ge(y_made, g * NY - NY)
                    act.copy(vh[:, par, s, :], vr[:, s, :]).then_inc(vh_done, 1)
                    act.wait_ge(weighted, g * GB + (s + 1))
                    act.copy(ah[:, par, s, :], ar[:, s, :]).then_inc(ah_done, 1)

            split(0, 0, True)
            split(1, 1, True)
            with act.Fori(1, NGR // 2) as i:
                for par in range(2):
                    split(i * 2 + par, par)

        @block.vector
        def _(dve):
            def prepare(g, s, par, first=False):
                dve.wait_ge(g_in, g * 16 + 16)
                dve.wait_ge(a_in[s], g * 16 + 16)
                a = ar[:, s, :].rearrange("p (t n) -> p t n", t=NHT)
                dve.tensor_tensor(a, a, gr[:, :, s * HT:(s + 1) * HT], ALU.mult).then_inc(weighted, 1)
                if not first:
                    dve.wait_ge(y_made, g * NY - NY)
                dve.wait_ge(vh_done, g * GB + (s + 1))
                dve.tensor_tensor(vl[:, par, s, :], vr[:, s, :], vh[:, par, s, :].bitcast(F32), ALU.subtract
                                  ).then_inc(vl_done, 1)
                dve.wait_ge(ah_done, g * GB + (s + 1))
                dve.tensor_tensor(al[:, par, s, :], ar[:, s, :], ah[:, par, s, :].bitcast(F32), ALU.subtract
                                  ).then_inc(al_done, 1)

            def add(g, par, first=False, last=False):
                for y in range(NY):
                    out = Y[:, y // 2, (y % 2) * 512:(y % 2 + 1) * 512]
                    dve.wait_ge(y_made, g * NY + (y + 1))
                    dve.tensor_tensor(out, out, yP[:, y % 4, :], ALU.add).then_inc(y_taken, 1)
                    if not last and y % 2 and y // 2 < GB:
                        prepare(g + 1, y // 2, 1 - par, first)

            for s in range(GB):
                prepare(0, s, 0, True)
            add(0, 0, True)
            with dve.Fori(0, NGR // 2 - 1) as i:
                add(i * 2 + 1, 1)
                add(i * 2 + 2, 0)
            add(NGR - 1, 1, False, True)


@contextmanager
def scope(alloc):
    with ExitStack() as stack:
        yield lambda name, shape, dt=F32: stack.enter_context(alloc(name, shape, dt))


def program(nc, T):
    with ExitStack() as whole:
        def sem(name):
            return nc.alloc_semaphore(name=name)

        def recycle(since):
            nc.clear_and_free_semaphores(nc.allocated_since(since))
            nc.all_engine_barrier()

        def sb(name, shape, dt=F32):
            return whole.enter_context(nc.sbuf_tensor(name, shape, dt))

        def sbctx():
            return scope(nc.sbuf_tensor)

        def psctx():
            return scope(nc.psum_tensor)

        m = Memory()
        none_yet = nc.snapshot_sems()
        build_constants(nc, m, sem, sb)
        m.scale, m.shift = sb("scale", [P, 2, KD, NCOND]), sb("shift", [P, 2, KD, NCOND])
        m.stat, m.rstd = sb("stat", [P, NT]), sb("rstd", [P, NT])
        m.oN = sb("oN", [P, NT, D])
        with sbctx() as s2:
            m.qkT = s2("qkT", [P, 8, TOK])
            m.xc = s2("xc", [P, 6, CONVW])
            m.vN, m.zN = s2("vN", [P, NT, 512]), s2("zN", [P, NT, 512])
            m.dt = s2("dt", [P, NT, H])
            m.a_log, m.d_skip = s2("a_log", [P, H]), s2("d_skip", [P, H])
            with sbctx() as s3:
                m.hT = s3("hT", [P, KD, TOK])
                with sbctx() as s4, psctx() as pp:
                    modulate(nc, m, T, sem, s4, pp)
                with sbctx() as s4, psctx() as pp:
                    x = s4("x_in", [P, NT, D])
                    m.junk = s4("junk1", [P, 2, D])
                    norm_to_columns(nc, m, sem, pp, "n1", T["x"], x, m.hT, 0)
                m.xpad = s3("xpad", [P, 6, CONVW])
                m.conv_w, m.conv_b = s3("conv_w", [P, 6, CW]), s3("conv_b", [P, 6])
                m.dt_bias = s3("dt_bias", [P, H])
                project(nc, m, T, sem, s3, None, psctx)
            with sbctx() as s3, psctx() as pp:
                scan(nc, m, T, sem, s3, pp)
            with sbctx() as s3:
                attend(nc, m, T, sem, s3, psctx)
        recycle(none_yet)
        if True:
            with sbctx() as s1:
                m.u = ExpertIn(sem, s1)
                m.h2h, m.h2l = s1("h2h", [P, KD, TOK], F32R), s1("h2l", [P, KD, TOK], F32R)
                kept = nc.snapshot_sems()
                with sbctx() as s2:
                    m.qhT = s2("qhT", [P, KD, TOK])
                    with sbctx() as s3:
                        mix(nc, m, T, sem, s3, psctx)
                    with sbctx() as s3:
                        route(nc, m, T, sem, s3, psctx)
                recycle(kept)
                with sbctx() as s2:
                    experts(nc, m, T, sem, s2, psctx)
            with sbctx() as s2:
                stored_experts(nc, m, T, sem, s2, psctx)
            with sbctx() as s2:
                y = s2("y", [P, NT, D])
                add_residual(nc, m, T, sem, s2, "res2", m.oN, T["x1"], T["g_post_ffn"], 1, T["y_out"], y)


INS = dict(x=[TOK, D], cT=[P, KD, NCOND], w_ada=[D, ADA], b_ada=[ADA], g_pre_mix=[P, KD], g_pre_ffn=[P, KD],
           w_cols=[14, P, KD, P], w_vz=[P, KD, 1024 + H], state_conv=[P, 6, NSEQ, CW - 1], conv_w=[P, 6, CW],
           conv_b=[P, 6], dt_bias=[H], a_log=[H], d_skip=[H],
           state_ssm=[P, NSEQ, 256], g_mix=[P, KD], cache_kT=[NSEQ, P, 4, PAST], cache_v=[NSEQ, PAST, 512],
           w_out=[D, D], g_post_mix=[D], g_post_ffn=[D], w_pq=[8, P, KD, P], sub_keys=[P, NKEY],
           uT=[NKEY, P, KD, P], v_tab=[NKEY, P, D])
OUTS = dict(kT_out=[P, 4, TOK], v_out=[TOK, 512], conv_out=[P, 6, NCOND, CW - 1], ssm_out=[P, NCOND, 256], y_out=[TOK, D])
SCRATCH = dict(gates=[2, NCOND, D], G=[NHT, P, NKEY, HT], HG=[NPRE, P, TOK], x1=[TOK, D])


def layout(x_prompt, x_sample, c_prompt, c_sample, cache_k, cache_v, state_ssm, state_conv, w_ada, b_ada, g_pre_mix,
           g_post_mix, g_pre_ffn, g_post_ffn, w_in, conv_w, conv_b, dt_bias, a_log, d_skip, g_attn_norm, g_ssd_norm,
           w_out, w_pq, sub_keys, u_tab, v_tab):
    def col_blocks(w):
        return w.reshape(KD, P, -1, P).transpose(2, 1, 0, 3)

    def by_column(g):
        return g.reshape(-1, P).T

    w = w_in[0]
    att, ssd = 3 * 512, 3 * 512 + 512
    return dict(
        x=np.concatenate([x_prompt.reshape(SEQ, D), x_sample.reshape(P, D)]),
        cT=np.concatenate([c_prompt, c_sample]).reshape(NCOND, KD, P).transpose(2, 1, 0),
        w_ada=w_ada[0], b_ada=b_ada[0], g_pre_mix=by_column(g_pre_mix), g_pre_ffn=by_column(g_pre_ffn),
        w_cols=col_blocks(np.concatenate([w[:, :1024], w[:, ssd:ssd + 768]], 1)),
        w_vz=np.concatenate([w[:, 1024:ssd], w[:, ssd + 768:]], 1).reshape(KD, P, -1).transpose(1, 0, 2),
        state_conv=state_conv[0].reshape(NSEQ, CW - 1, 6, P).transpose(3, 2, 0, 1),
        conv_w=conv_w[0].reshape(CW, 6, P).transpose(2, 1, 0), conv_b=by_column(conv_b),
        dt_bias=dt_bias[0], a_log=a_log[0], d_skip=d_skip[0],
        state_ssm=state_ssm[0].reshape(NSEQ, 2, 4, HD, 64).transpose(1, 4, 0, 2, 3).reshape(P, NSEQ, 256),
        g_mix=by_column(np.concatenate([g_attn_norm, g_ssd_norm], 1)),
        cache_kT=cache_k[0].reshape(NSEQ, PAST, 4, P).transpose(0, 3, 2, 1),
        cache_v=cache_v[0].reshape(NSEQ, PAST, 512),
        w_out=w_out[0], g_post_mix=g_post_mix[0], g_post_ffn=g_post_ffn[0], w_pq=col_blocks(w_pq[0]),
        sub_keys=sub_keys[0].transpose(0, 2, 1).reshape(P, NKEY),
        uT=u_tab[0].reshape(P, NKEY, KD, P).transpose(1, 3, 2, 0),
        v_tab=v_tab[0].reshape(P, NKEY, D).transpose(1, 0, 2))


def unlayout(r):
    y, v = r["y_out"], r["v_out"]
    k = r["kT_out"].transpose(2, 1, 0).reshape(TOK, 512)
    conv = r["conv_out"].transpose(2, 3, 1, 0).reshape(NCOND, CW - 1, 768)
    ssm = r["ssm_out"].reshape(2, 64, NCOND, 4, HD).transpose(2, 0, 3, 4, 1).reshape(NCOND, H, HD, 64)
    c = np.ascontiguousarray
    return (c(y[:SEQ]).reshape(1, SEQ, D), c(y[SEQ:]).reshape(NSEQ, LSEQ, D),
            c(k[:SEQ]).reshape(1, 1, SEQ, H, HD), c(v[:SEQ]).reshape(1, 1, SEQ, H, HD), c(ssm[None, :1]), c(conv[None, :1]),
            c(k[SEQ:]).reshape(1, NSEQ, LSEQ, H, HD), c(v[SEQ:]).reshape(1, NSEQ, LSEQ, H, HD), c(ssm[None, 1:]),
            c(conv[None, 1:]))


def build(nc):
    T = {}
    for name, shape in INS.items():
        T[name] = nc.dram_tensor("in_" + name, shape, F32, kind="ExternalInput").ap()
    for name, shape in OUTS.items():
        T[name] = nc.dram_tensor("out_" + name, shape, F32, kind="ExternalOutput").ap()
    for name, shape in SCRATCH.items():
        T[name] = nc.dram_tensor("scratch_" + name, shape, F32).ap()
    program(nc, T)


def kernel(**inputs):
    import concourse.bacc as bacc
    from concourse.bass_utils import run_bass_kernel_spmd

    nc = bacc.Bacc("TRN2", target_bir_lowering=False, num_devices=1)
    build(nc)
    arrays = {"in_" + k: np.ascontiguousarray(a) for k, a in layout(**inputs).items()}
    r = run_bass_kernel_spmd(nc, [arrays], core_ids=[0]).results[0]
    return unlayout({k: r["out_" + k] for k in OUTS})
```

```python
from contextlib import ExitStack, contextmanager

import numpy as np

import concourse.bass as bass
from concourse import mybir

F32 = mybir.dt.float32
F32R = mybir.dt.float32r
BF16 = mybir.dt.bfloat16
U32 = mybir.dt.uint32
ALU = mybir.AluOpType
ACT = mybir.ActivationFunctionType
AX = mybir.AxisListType.X
ds = bass.ds

P = 128
D = 1024
KD = D // P
SEQ = 512
NSEQ, LSEQ = 8, 16
NT = 5
TOK = NT * P
HALF = TOK // 2
PAST = 512
H, HD = 8, 64
NCOND = 1 + NSEQ
ADA = 6 * D
CW = 4
SEGP = CW - 1 + SEQ
SEGS = CW - 1 + LSEQ
CONVW = SEGP + NSEQ * SEGS
CONVO = CONVW - (CW - 1)
NKEY = 128
TOPK = 16
EPS = 1e-6
FAR = -1e30


class Memory:
    pass


def spread(ap, axis, n):
    shape = list(ap.shape)
    shape.insert(axis, n)
    return ap.unsqueeze(axis).broadcast_to(shape)


def build_constants(nc, m, sem, sb):
    m.ident = sb("ident", [P, P])
    m.ones = sb("ones", [P, P])
    m.upto = sb("upto", [P, 2, P])
    m.later = sb("later", [P, 2, P])
    m.from_ = sb("from_", [P, P])
    m.seen = sb("seen", [P, NT, P])
    m.same = sb("same", [P, P])
    m.hide = sb("hide", [P, NT, P])
    m.hide_ssd = sb("hide_ssd", [P, 2, P])
    m.mhalf = sb("mhalf", [P, 2 * NT])
    filled, built = sem("const_filled"), sem("const_built")
    hidden = sem("const_hidden")
    with nc.Block() as block:
        @block.gpsimd
        def _(pool):
            pool.memset(m.ident[:, :], 0.0).then_inc(filled, 1)
            pool.memset(m.mhalf[:, :], -0.5).then_inc(filled, 1)
            for t in (m.ones, m.from_, m.same):
                pool.memset(t[:, :], 1.0).then_inc(filled, 1)
            for t in (m.upto, m.later, m.seen):
                pool.memset(t[:, :, :], 1.0).then_inc(filled, 1)
            pool.wait_ge(filled, 8)

            done = 0

            def keep(view, compare, base, pattern, by_row, fill=0.0):
                nonlocal done
                pool.affine_select(out=view, in_=view, compare_op=compare, fill=fill, base=base,
                                   pattern=pattern, channel_multiplier=by_row).then_inc(built, 1)
                done += 1

            keep(m.ident[:, :], ALU.not_equal, 0, [[-1, P]], 1, 1.0)
            keep(m.from_[:, :], ALU.is_ge, 0, [[-1, P]], 1)
            keep(m.upto[:, :, :], ALU.is_ge, 0, [[0, 2], [1, P]], -1)
            keep(m.later[:, :, :], ALU.is_gt, 0, [[0, 2], [-1, P]], 1)
            keep(m.seen[:, :, :], ALU.is_gt, 0, [[0, NT], [1, P]], -1)
            blocks = (m.same[:, :], m.upto[:, 1, :], m.later[:, 1, :], m.seen[:, NT - 1, :])
            pool.wait_ge(built, done)
            for v in blocks:
                keep(v, ALU.is_ge, 0, [[-LSEQ, NSEQ], [0, LSEQ]], 1)
            pool.wait_ge(built, done)
            for v in blocks:
                keep(v, ALU.is_ge, LSEQ - 1, [[LSEQ, NSEQ], [0, LSEQ]], -1)
            m.n_built = done

        @block.vector
        def _(dve):
            dve.wait_ge(built, m.n_built)
            dve.tensor_scalar(m.hide[:, :, :], m.seen[:, :, :], -1.0, -FAR, ALU.add, ALU.mult).then_inc(hidden, 1)
            dve.tensor_scalar(m.hide_ssd[:, :, :], m.upto[:, :, :], -1.0, -FAR, ALU.add, ALU.mult).then_inc(hidden, 1)


def modulate(nc, m, T, sem, sb, ps, ahead):
    NCH = 2 * D // 512
    cT = sb("cT", [P, KD, NCOND])
    wa = sb("wa", [P, NCH, KD, 512])
    ba = sb("ba", [NCOND, 2 * D])
    row = sb("mod_row", [NCOND, 2 * D])
    gcol = sb("gcol", [P, KD])
    colp = ps("mod_col_ps", [P, 512])
    acc = ps("mod_ps", [P, 2, 512])
    small_in, wa_in = sem("mod_small_in"), [sem(f"wa_in{s}") for s in range(NCH)]
    first_in = [sem(f"wa_first_in{k}") for k in range(KD)]
    silu_done, chunk_done, row_done = sem("mod_silu"), sem("mod_chunk"), sem("mod_row")
    col_done, scaled = sem("mod_cols"), sem("mod_scaled")

    with nc.Block() as block:
        @block.sync
        def _(sp):
            sp.dma_start(cT[:, :, :], T["cT"]).then_inc(small_in, 16)
            sp.dma_start(ba[:, :], T["b_ada"][0:2 * D].partition_broadcast(NCOND)).then_inc(small_in, 16)
            sp.dma_start(gcol[:, :], T["g_pre_mix"]).then_inc(small_in, 16)
            for k in range(KD):
                sp.dma_start(wa[:, 0, k, :], T["w_ada"][k * P:(k + 1) * P, 0:512]).then_inc(first_in[k], 16)
            for n in range(1, NCH):
                sp.dma_start(wa[:, n, :, :], ada_chunk(T, n)).then_inc(wa_in[n], 16)
            ahead(sp)

        @block.scalar
        def _(act):
            act.wait_ge(small_in, 48)
            act.activation(m.silu_c[:, :, :], cT[:, :, :], ACT.Silu).then_inc(silu_done, 1)

        @block.tensor
        def _(pe):
            pe.wait_ge(silu_done, 1)
            for n in range(NCH):
                if n:
                    pe.wait_ge(wa_in[n], 16)
                if n >= 2:
                    pe.wait_ge(row_done, n - 1)
                for k in range(KD):
                    if n == 0:
                        pe.wait_ge(first_in[k], 16)
                    mm = pe.matmul(acc[0:NCOND, n % 2, :], m.silu_c[:, k, :], wa[:, n, k, :], start=(k == 0),
                                   stop=(k == KD - 1))
                mm.then_inc(chunk_done, 1)
            pe.wait_ge(row_done, NCH)
            turn_rows(pe, m, colp, row, 0).then_inc(col_done, 1)

        @block.vector
        def _(dve):
            dve.wait_ge(small_in, 48)
            for n in range(NCH):
                dve.wait_ge(chunk_done, n + 1)
                at = slice(n * 512, (n + 1) * 512)
                dve.tensor_tensor(row[:, at], acc[0:NCOND, n % 2, :], ba[:, at], ALU.add).then_inc(row_done, 1)
            dve.wait_ge(col_done, 1)
            take_columns(dve, m, colp, gcol, 0, scaled)


def ada_chunk(T, n):
    at = slice(n * 512, (n + 1) * 512) if isinstance(n, int) else ds(n * 512, 512)
    return T["w_ada"].rearrange("(k p) n -> p k n", p=P)[:, :, at]


def turn_rows(pe, m, colp, row, start):
    for j in range(2):
        for k in range(KD):
            at = (j * KD + k) * NCOND
            mm = pe.transpose(colp[:, at:at + NCOND], row[:, start + j * D + k * P:start + j * D + (k + 1) * P],
                              m.ident[0:NCOND, 0:NCOND])
    return mm


def take_columns(dve, m, colp, gcol, half, scaled):
    v = colp[:, 0:2 * KD * NCOND].rearrange("p (a k c) -> p a k c", a=2, k=KD)
    dve.tensor_copy(m.shift[:, half, :, :], v[:, 0]).then_inc(scaled, 1)
    dve.scalar_tensor_tensor(m.scale[:, half, :, :], v[:, 1], 1.0, spread(gcol[:, :], 2, NCOND),
                             ALU.add, ALU.mult).then_inc(scaled, 1)


def norm_to_columns(nc, m, sem, ps, name, loaded, src, dst, which, ahead):
    ss = m.stat
    pr = ps(name + "_ps", [P, 2, 512])
    sa = ps(name + "_ps_s", [P, 2, 512])
    squared, mean, rstd, normed = (sem(name + x) for x in ("_sq", "_mean", "_rstd", "_normed"))
    turned, turned_s, out_p, out_s = (sem(name + x) for x in ("_tp", "_ts", "_op", "_os"))
    with nc.Block() as block:
        @block.sync
        def _(sp):
            ahead(sp)

        @block.scalar
        def _(act):
            for t in range(NT):
                if loaded is not None:
                    act.wait_ge(loaded[t], 16)
                if t >= 2:
                    act.wait_ge(squared, t - 1)
                act.activation(m.junk[:, t % 2, :], src[:, t, :], ACT.Square, accum_out=ss[:, t:t + 1]).then_inc(squared, 1)

        @block.gpsimd
        def _(pool):
            pool.wait_ge(mean, 1)
            pool.tensor_tensor(m.rstd[:, :], ss[:, :], m.mhalf[:, 0:NT], ALU.pow).then_inc(rstd, 1)

        @block.vector
        def _(dve):
            dve.wait_ge(squared, NT)
            dve.tensor_scalar(ss[:, :], ss[:, :], 1.0 / D, EPS, ALU.mult, ALU.add).then_inc(mean, 1)
            dve.wait_ge(rstd, 1)
            for t in range(NT):
                dve.tensor_scalar(src[:, t, :], src[:, t, :], m.rstd[:, t:t + 1], None, ALU.mult).then_inc(normed, 1)
            for k in range(KD):
                dve.wait_ge(turned, k + 1)
                dve.tensor_scalar(dst[:, k, 0:SEQ], pr[:, k % 2, :], m.scale[:, which, k, 0:1],
                                  m.shift[:, which, k, 0:1], ALU.mult, ALU.add).then_inc(out_p, 1)
                if k % 4 == 3:
                    q = k // 4
                    dve.wait_ge(turned_s, q + 1)
                    d4 = dst[:, 4 * q:4 * q + 4, SEQ:TOK].rearrange("p k (b i) -> p k b i", b=NSEQ)
                    s4 = sa[:, q, :].rearrange("p (k b i) -> p k b i", k=4, b=NSEQ)
                    for kk in range(4):
                        dve.tensor_tensor(d4[:, kk], s4[:, kk],
                                          spread(m.scale[:, which, 4 * q + kk, 1:NCOND], 2, LSEQ),
                                          ALU.mult).then_inc(out_s, 1)
                    dve.wait_ge(out_s, 8 * q + 4)
                    for kk in range(4):
                        dve.tensor_tensor(d4[:, kk], d4[:, kk],
                                          spread(m.shift[:, which, 4 * q + kk, 1:NCOND], 2, LSEQ),
                                          ALU.add).then_inc(out_s, 1)

        @block.tensor
        def _(pe):
            pe.wait_ge(normed, NT)
            for k in range(KD):
                if k >= 2:
                    pe.wait_ge(out_p, k - 1)
                for t in range(NT - 1):
                    mm = pe.transpose(pr[:, k % 2, t * P:(t + 1) * P], src[:, t, k * P:(k + 1) * P], m.ident[:, :])
                mm.then_inc(turned, 1)
                mm = pe.transpose(sa[:, k // 4, (k % 4) * P:(k % 4 + 1) * P], src[:, NT - 1, k * P:(k + 1) * P],
                                  m.ident[:, :])
                if k % 4 == 3:
                    mm.then_inc(turned_s, 1)


class SplitRing:

    def __init__(self, sem, name, blocks, sb=None, memory=None):
        self.blocks = blocks
        if memory is None:
            self.raw, self.high, self.low = (sb(name + "_raw", [P, 2, KD, P]), sb(name + "_high", [P, 2, KD, P], F32R),
                                             sb(name + "_low", [P, 2, KD, P], F32R))
        else:
            self.raw, self.high, self.low = memory.raw, memory.high, memory.low
        self.came = [sem(f"{name}_in{n}") for n in range(2)]
        self.high_done, self.low_done = sem(name + "_high_done"), sem(name + "_low_done")

    def load(self, eng, n, s, first=False):
        if not first:
            eng.wait_ge(self.high_done, n - 1)
            eng.wait_ge(self.low_done, n - 1)
        src = self.blocks[n] if isinstance(n, int) else self.blocks[ds(n, 1)].rearrange("a p k c -> (a p) k c")
        eng.dma_start(self.raw[:, s, :, :], src).then_inc(self.came[s], 16)

    def split_low(self, eng, n, s):
        eng.wait_ge(self.high_done, n + 1)
        eng.tensor_tensor(self.low[:, s, :, :], self.raw[:, s, :, :], self.high[:, s, :, :].bitcast(F32), ALU.subtract
                          ).then_inc(self.low_done, 1)


def column_products(nc, sem, ps, name, ring, n_blocks, src, high, low, sink, ahead=None):
    acc = ps(name + "_acc", [P, 2, 2, 512])
    made, taken = sem(name + "_made"), sem(name + "_taken")
    src_high, src_low = sem(name + "_src_high"), sem(name + "_src_low")
    with nc.Block() as block:
        @block.sync
        def _(sp):
            if ahead is not None:
                ahead(sp)
            with sp.Fori(1, n_blocks // 2) as i:
                for s in range(2):
                    ring.load(sp, i * 2 + s, s)

        @block.vector
        def _(dve):
            def split(n, s, first=False):
                dve.wait_ge(ring.came[s], 16 if first else n * 8 + (16 - 8 * s))
                if not first:
                    dve.wait_ge(made, n - 1)
                dve.tensor_copy(ring.high[:, s, :, :], ring.raw[:, s, :, :]).then_inc(ring.high_done, 1)
                ring.split_low(dve, n, s)

            split(0, 0, True)
            for k in range(KD):
                dve.tensor_copy(high[:, k, :], src[:, k, :]).then_inc(src_high, 1)
                dve.wait_ge(src_high, k + 1)
                dve.tensor_tensor(low[:, k, :], src[:, k, :], high[:, k, :].bitcast(F32), ALU.subtract
                                  ).then_inc(src_low, 1)
            split(1, 1, True)
            with dve.Fori(1, n_blocks // 2) as i:
                for s in range(2):
                    split(i * 2 + s, s)

        @block.tensor
        def _(pe):
            def blk(n, s, first=False):
                pe.wait_ge(ring.low_done, n + 1)
                if not first:
                    pe.wait_ge(taken, n - 1)
                for k in range(KD):
                    if first and s == 0:
                        pe.wait_ge(src_low, k + 1)
                    for w, x in ((ring.high, high), (ring.high, low), (ring.low, high)):
                        for h in range(2):
                            mm = pe.matmul(acc[:, s, h, 0:HALF], w[:, s, k, :], x[:, k, h * HALF:(h + 1) * HALF],
                                           start=(k == 0 and w is ring.high and x is high),
                                           stop=(k == KD - 1 and w is ring.low))
                mm.then_inc(made, 1)
            for s in range(2):
                blk(s, s, True)
            with pe.Fori(1, n_blocks // 2) as i:
                for s in range(2):
                    blk(i * 2 + s, s)

        @block.scalar
        def _(act):
            sink(act, acc, made, taken)


def project(nc, m, T, sem, sb, ring, psctx):
    def sink(act, acc, made, taken):
        with act.Fori(0, 4) as i:
            for s in range(2):
                act.wait_ge(made, i * 2 + (s + 1))
                act.copy(m.qkT[:, ds(i * 2 + s, 1), :].rearrange("p a (h n) -> p (a h) n", h=2),
                         acc[:, s, :, 0:HALF]).then_inc(taken, 1)
        for n in range(8, 14):
            s, j = n % 2, n - 8
            act.wait_ge(made, n + 1)
            act.copy(m.xpad[:, j, CW - 1:CW - 1 + HALF], acc[:, s, 0, 0:HALF])
            act.copy(m.xpad[:, j, CW - 1 + HALF:SEGP], acc[:, s, 1, 0:SEQ - HALF])
            act.copy(m.xpad[:, j, SEGP:].rearrange("p (b i) -> p b i", b=NSEQ)[:, :, CW - 1:],
                     acc[:, s, 1, SEQ - HALF:HALF].rearrange("p (b i) -> p b i", b=NSEQ)).then_inc(taken, 1)

    wv = m.oN[:, 0:4, :].rearrange("p t d -> p (t d)").rearrange("p (k n) -> p k n", k=KD)
    wz = sb("w_rows", [P, KD, 512 + H])
    rows_in, pads_in = sem("rows_in"), sem("pads_in")

    def load_rows(sp):
        sp.dma_start(wv, T["w_vz"][:, :, 0:512]).then_inc(rows_in, 16)
        sp.dma_start(wz[:, :, :], T["w_vz"][:, :, 512:]).then_inc(rows_in, 16)

    with psctx() as pp, scope(nc.sbuf_tensor) as tmp:
        high, low = tmp("hT_high", [P, KD, TOK], F32R), tmp("hT_low", [P, KD, TOK], F32R)
        column_products(nc, sem, pp, "proj", ring, 14, m.hT, high, low, sink, load_rows)

    vz_made, vz_taken, dt_made, dt_taken = sem("vz_made"), sem("vz_taken"), sem("dt_made"), sem("dt_taken")
    conv, conv_ready, out_done = sem("conv_step"), sem("conv_sum"), sem("proj_out")
    zeroed, silu_done = sem("pad_zero"), sem("conv_silu")
    with psctx() as pp, nc.Block() as block:
        acc = pp("vz_ps", [P, 2, 2, 512])
        dtp = pp("dt_ps", [P, 512])

        @block.sync
        def _(sp):
            for j in range(6):
                sp.dma_start(m.xpad[:, j, SEGP:].rearrange("p (b i) -> p b i", b=NSEQ)[:, :, 0:CW - 1],
                             T["state_conv"][:, j]).then_inc(pads_in, 16)
            sp.dma_start(m.conv_w[:, :, :], T["conv_w"]).then_inc(pads_in, 16)
            sp.dma_start(m.conv_b[:, :], T["conv_b"]).then_inc(pads_in, 16)
            sp.dma_start(m.dt_bias[:, :], T["dt_bias"].partition_broadcast(P)).then_inc(pads_in, 16)
            sp.dma_start(m.a_log[:, :], T["a_log"].partition_broadcast(P)).then_inc(pads_in, 16)
            sp.dma_start(m.d_skip[:, :], T["d_skip"].partition_broadcast(P)).then_inc(pads_in, 16)
            sp.dma_start(T["kT_out"], m.qkT[:, 4:8, :]).then_inc(out_done, 16)
            for j in range(6):
                sp.dma_start(T["conv_out"][:, j, 0, :], m.xpad[:, j, SEGP - (CW - 1):SEGP]).then_inc(out_done, 16)
                sp.dma_start(T["conv_out"][:, j, 1:NCOND, :],
                             m.xpad[:, j, SEGP:].rearrange("p (b i) -> p b i", b=NSEQ)[:, :, SEGS - (CW - 1):]
                             ).then_inc(out_done, 16)
            sp.wait_ge(vz_taken, NT)
            for t in range(NT):
                sp.dma_start(T["v_out"][t * P:(t + 1) * P, :], m.vN[:, t, :]).then_inc(out_done, 16)
            sp.wait_ge(out_done, 16 * (13 + NT))

        @block.tensor
        def _(pe):
            for t in range(NT):
                if t == 0:
                    pe.wait_ge(rows_in, 32)
                if t >= 2:
                    pe.wait_ge(vz_taken, t - 1)
                for k in range(KD):
                    lhs = m.hT[:, k, t * P:(t + 1) * P]
                    pe.matmul(acc[:, t % 2, 0, :], lhs, wv[:, k, :], start=(k == 0), stop=(k == KD - 1))
                    mm = pe.matmul(acc[:, t % 2, 1, :], lhs, wz[:, k, 0:512], start=(k == 0), stop=(k == KD - 1))
                mm.then_inc(vz_made, 1)
                for k in range(KD):
                    mm = pe.matmul(dtp[:, t * H:(t + 1) * H], m.hT[:, k, t * P:(t + 1) * P], wz[:, k, 512:],
                                   start=(k == 0), stop=(k == KD - 1))
            mm.then_inc(dt_made, 1)

        @block.vector
        def _(dve):
            dve.memset(m.xpad[:, :, 0:CW - 1], 0.0).then_inc(zeroed, 1)
            dve.wait_ge(pads_in, 16 * 11)
            dve.wait_ge(zeroed, 1)
            for w in range(CW):
                for j in range(6):
                    src = m.xpad[:, j, w:w + CONVO]
                    if w:
                        dve.wait_ge(conv, (w - 1) * 6 + j + 1)
                        dve.scalar_tensor_tensor(m.xc[:, j, 0:CONVO], src, m.conv_w[:, j, w:w + 1], m.xc[:, j, 0:CONVO],
                                                 ALU.mult, ALU.add).then_inc(conv, 1)
                    else:
                        dve.tensor_scalar(m.xc[:, j, 0:CONVO], src, m.conv_w[:, j, 0:1], m.conv_b[:, j:j + 1],
                                          ALU.mult, ALU.add).then_inc(conv, 1)
            dve.wait_ge(dt_made, 1)
            dve.tensor_tensor(m.dt[:, :, :], dtp[:, 0:NT * H].rearrange("p (t h) -> p t h", t=NT),
                              spread(m.dt_bias[:, :], 1, NT), ALU.add).then_inc(dt_taken, 1)

        @block.scalar
        def _(act):
            for t in range(NT):
                act.wait_ge(vz_made, t + 1)
                act.copy(m.vN[:, t, :], acc[:, t % 2, 0, :])
                act.copy(m.zN[:, t, :], acc[:, t % 2, 1, :]).then_inc(vz_taken, 1)
            for j in range(6):
                act.wait_ge(conv, 18 + j + 1)
                act.activation(m.xc[:, j, 0:CONVO], m.xc[:, j, 0:CONVO], ACT.Silu).then_inc(silu_done, 1)


def scan(nc, m, T, sem, sb, ps):
    NCH = 4 * D // 512
    wa, ba = sb("wa2", [P, 2, KD, 512]), sb("ba2", [NCOND, 4 * D])
    row, gcol = sb("mod_row2", [NCOND, 4 * D]), sb("gcol2", [P, KD])
    small_in, wa_in = sem("mod2_small_in"), [sem(f"wa2_in{s}") for s in range(2)]
    chunk_done, row_done, col_done = sem("mod2_chunk"), sem("mod2_row"), sem("mod2_cols")
    scaled, gates_out = sem("mod2_scaled"), sem("gates_out")
    E = LSEQ * NSEQ
    xt = sb("xt", [P, 6, P])
    dts, das = sb("dts", [P, H]), sb("das", [P, H])
    a8, dtA = sb("a8", [P, H]), sb("dtA", [P, NT, H])
    sp = sb("sp_tmp", [P, NT * H])
    cum, grow = sb("cum", [P, 2 * H]), sb("grow", [P, 2, H])
    lastc = sb("lastc", [P, H, NSEQ])
    seg, dec, W = sb("seg", [P, H, P]), sb("dec", [P, H, P]), sb("W", [P, H, P])
    Bn = sb("Bn", [P, P])
    xdt, xdte, xD = sb("xdt", [P, H, HD]), sb("xdte", [P, H, HD]), sb("xD", [P, H, HD])
    state = sb("state", [P, 512])
    CTg = sb("CTg", [P, 2, P])
    cdec = sb("cdec", [P, H, NSEQ])
    CTm = sb("CTm", [P, NSEQ * (P + LSEQ)])
    Bm = sb("Bm", [P, NSEQ, P])
    sst = sb("sst", [P, NSEQ, 512])
    misc, ada = ps("scan_misc", [P, 512]), ps("mod2_ps", [P, 512])
    rows = ps("scan_rows", [P, H, P])
    xsP, yd, yo, S = (ps(n, [P, 512]) for n in ("scan_xs", "scan_yd", "scan_yo", "scan_S"))
    cs, cb, bP = misc[:, 0:16], misc[:, 16:272].rearrange("p (g t) -> p g t", g=2), misc[:, 272:400]
    Spair = (S, xsP)

    ready, dt_step, dt_act = sem("scan_ready"), sem("dt_step"), sem("dt_act")
    staged = sem("scan_staged")
    cum_made, rows_made, cb_made, y_made = sem("cum_made"), sem("rows_made"), sem("cb_made"), sem("y_made")
    act_done, seg_step, w_ready, x_ready = sem("scan_exp"), sem("seg_step"), sem("w_ready"), sem("x_ready")
    state_step, y_step = sem("state_step"), sem("y_step")
    st_in, st_out, masked = sem("ssm_in"), sem("ssm_out_sem"), sem("scan_masked")
    bm_ready = sem("bm_ready")
    s_made, s_taken, aged = sem("S_made"), sem("S_taken"), sem("sst_aged")
    gate_silu, gated = sem("gate_silu"), sem("gated")
    flat = lambda v: v[:, :, :].rearrange("p t h -> p (t h)")
    NP = NT - 1

    def own(v, g):
        return v[64 * g:64 * g + 64, :, g * 256:(g + 1) * 256]

    with nc.Block() as block:
        @block.sync
        def _(eng):
            eng.dma_start(ba[:, :], T["b_ada"][2 * D:].partition_broadcast(NCOND)).then_inc(small_in, 16)
            eng.dma_start(gcol[:, :], T["g_pre_ffn"]).then_inc(small_in, 16)
            for s in range(2):
                eng.dma_start(wa[:, s, :, :], ada_chunk(T, 4 + s)).then_inc(wa_in[s], 16)
            eng.wait_ge(masked, 2)
            for g in range(2):
                eng.dma_start(own(sst, g), T["state_ssm"][64 * g:64 * g + 64]).then_inc(st_in, 16)
            with eng.Fori(1, NCH // 2) as i:
                for s in range(2):
                    eng.wait_ge(chunk_done, i * 2 + (s - 1))
                    eng.dma_start(wa[:, s, :, :], ada_chunk(T, i * 2 + (4 + s))).then_inc(wa_in[s], 16)
            eng.wait_ge(row_done, NCH)
            for g, c in enumerate((0, 3)):
                eng.dma_start(T["gates"][g], row[:, c * D:(c + 1) * D]).then_inc(gates_out, 16)
            eng.wait_ge(gates_out, 32)
            eng.wait_ge(state_step, 1 + 4 * NP)
            for g in range(2):
                r = slice(64 * g, 64 * g + 64)
                eng.dma_start(T["ssm_out"][r, 0, :], state[r, g * 256:(g + 1) * 256]).then_inc(st_out, 16)
            eng.wait_ge(s_taken, 2 * NSEQ)
            for g in range(2):
                eng.dma_start(T["ssm_out"][64 * g:64 * g + 64, 1:NCOND, :], own(sst, g)).then_inc(st_out, 16)
            eng.wait_ge(st_out, 64)

        @block.gpsimd
        def _(pool):
            pool.memset(state[:, :], 0.0).then_inc(state_step, 1)
            pool.memset(CTm[:, :], 0.0).then_inc(masked, 1)
            pool.memset(sst[:, :, :], 0.0).then_inc(masked, 1)
            pool.memset(CTg[:, :, :], 0.0).then_inc(staged, 1)
            pool.wait_ge(staged, 1)
            pool.wait_ge(ready, 1)

            def stage(i, sampled):
                for dst, src in ((dts, m.dt), (das, dtA)):
                    pool.tensor_copy(dst[:, :], src[:, ds(i, 1), :].rearrange("p a h -> p (a h)")
                                     if not sampled else src[:, NP, :]).then_inc(staged, 1)
                if sampled:
                    pool.tensor_copy(xt[:, :, :].rearrange("p j (b i) -> p j b i", b=NSEQ),
                                     m.xc[:, :, SEGP:].rearrange("p j (b i) -> p j b i", b=NSEQ)[:, :, :, 0:LSEQ]
                                     ).then_inc(staged, 1)
                else:
                    pool.tensor_copy(xt[:, :, :], m.xc[:, :, ds(i * P, P)]).then_inc(staged, 1)
                copied = i * 5 + 4 if sampled or isinstance(i, int) else pool.to_reg(i * 5 + 4)
                pool.wait_ge(ready, 1)
                pool.wait_ge(staged, copied)
                for g in range(2):
                    r = slice(64 * g, 64 * g + 64)
                    pool.tensor_copy(CTg[r, g, :], xt[r, 5, :]).then_inc(staged, 1)

            stage(0, False)
            with pool.Fori(1, NP) as i:
                pool.wait_ge(ready, 1)
                pool.wait_ge(y_made, i)
                pool.wait_ge(x_ready, i * 4)
                stage(i, False)
            pool.wait_ge(y_made, NP)
            pool.wait_ge(x_ready, NP * 4)
            stage(NP, True)
            pool.wait_ge(staged, 5 * NT + 1)
            pool.wait_ge(masked, 2)
            diagonal = CTm[:, :].rearrange("p (b x) -> p b x", b=NSEQ)[:, :, 0:LSEQ]
            pool.tensor_copy(diagonal, xt[:, 5, :].rearrange("p (b i) -> p b i", b=NSEQ)).then_inc(masked, 1)

        @block.tensor
        def _(pe):
            def chunk(i, s, first=False):
                pe.wait_ge(wa_in[s], i * 16 + 16)
                if not (first and s == 0):
                    pe.wait_ge(row_done, i * 2 + s)
                for k in range(KD):
                    mm = pe.matmul(ada[0:NCOND, :], m.silu_c[:, k, :], wa[:, s, k, :], start=(k == 0), stop=(k == KD - 1))
                mm.then_inc(chunk_done, 1)

            def tile(i, sampled, first):
                w = 1 if sampled else 0
                pe.wait_ge(staged, i * 5 + 6)
                if not first:
                    pe.wait_ge(y_step, i * 3)
                pe.matmul(cs[:, 0:H], m.upto[:, w, :], das[:, :], start=True, stop=True)
                pe.matmul(cs[:, H:], m.later[:, w, :], das[:, :], start=True, stop=True).then_inc(cum_made, 1)
                for h in range(H):
                    mm = pe.matmul(rows[:, h, :], das[:, h:h + 1].broadcast_to([P, P]), m.upto[:, w, :],
                                   start=True, stop=True)
                mm.then_inc(rows_made, 1)
                pe.wait_ge(seg_step, i * 4 + 1)
                pe.matmul(cb, xt[:, 4, :], CTg[:, :, :], start=True, stop=True)
                for j in range(4):
                    pe.transpose(xsP[:, j * P:(j + 1) * P], xt[:, j, :], m.ident[:, :])
                pe.transpose(bP, xt[:, 4, :], m.ident[:, :]).then_inc(cb_made, 1)
                if not sampled:
                    chunk(i, 0, first)
                pe.wait_ge(w_ready, i + 1)
                pe.wait_ge(x_ready, i * 4 + 3)
                for h in range(H):
                    pe.matmul(yd[:, h * HD:(h + 1) * HD], W[:, h, :], xdt[:, h, :], start=True, stop=True)
                if sampled:
                    pe.wait_ge(masked, 3)
                    pe.wait_ge(st_in, 32)
                    for b in range(NSEQ):
                        mm = pe.matmul(yo[:, :], CTm[:, b * P:(b + 1) * P], sst[:, b, :],
                                       start=(b == 0), stop=(b == NSEQ - 1))
                    mm.then_inc(y_made, 1)
                    pe.wait_ge(bm_ready, 1)
                    pe.wait_ge(x_ready, 4 * NT)
                    for b in range(NSEQ):
                        if b >= 2:
                            pe.wait_ge(s_taken, 2 * (b - 1))
                        pe.matmul(Spair[b % 2][:, :], Bm[:, b, :], xdte[:, :, :].rearrange("p h d -> p (h d)"),
                                  start=True, stop=True).then_inc(s_made, 1)
                else:
                    pe.wait_ge(state_step, i * 4 + 1)
                    pe.matmul(yo[:, :], xt[:, 5, :], state[:, :], start=True, stop=True)
                    pe.matmul(S[:, :], Bn[:, :], xdte[:, :, :].rearrange("p h d -> p (h d)"),
                              start=True, stop=True).then_inc(y_made, 1)
                    chunk(i, 1, first)

            tile(0, False, True)
            with pe.Fori(1, NP) as i:
                tile(i, False, False)
            pe.wait_ge(row_done, NCH)
            turn_rows(pe, m, ada, row, D).then_inc(col_done, 1)
            tile(NP, True, False)

        @block.scalar
        def _(act):
            act.activation(a8[:, :], m.a_log[:, :], ACT.Exp).then_inc(dt_act, 1)
            act.activation(sp[:, :], flat(m.dt), ACT.Abs).then_inc(dt_act, 1)
            act.wait_ge(dt_act, 2)
            act.activation(sp[:, :], sp[:, :], ACT.Exp, scale=-1.0).then_inc(dt_act, 1)
            act.wait_ge(dt_act, 3)
            act.activation(sp[:, :], sp[:, :], ACT.Ln, bias=1.0).then_inc(dt_act, 1)

            def tile(i, sampled, first):
                act.wait_ge(seg_step, i * 4 + 1)
                if not first:
                    act.wait_ge(y_step, i * 3)
                    act.wait_ge(x_ready, i * 4)
                    act.wait_ge(state_step, i * 4 + 1)
                act.activation(grow[:, :, :].rearrange("p a h -> p (a h)"), cum[:, :], ACT.Exp).then_inc(act_done, 1)
                act.wait_ge(seg_step, i * 4 + 3)
                n = NSEQ if sampled else 1
                act.activation(cdec[:, :, 0:n], lastc[:, :, 0:n], ACT.Exp).then_inc(act_done, 1)
                act.wait_ge(seg_step, i * 4 + 4)
                if not first:
                    act.wait_ge(w_ready, i)
                act.activation(dec[:, :, :], seg[:, :, :], ACT.Exp).then_inc(act_done, 1)

            tile(0, False, True)
            with act.Fori(1, NP) as i:
                tile(i, False, False)
            tile(NP, True, False)
            act.activation(m.zN[:, :, :], m.zN[:, :, :], ACT.Silu).then_inc(gate_silu, 1)

        @block.vector
        def _(dve):
            def add_bias(i, s):
                dve.wait_ge(small_in, 32)
                at = slice(i * 1024 + s * 512, i * 1024 + (s + 1) * 512) if isinstance(i, int) else ds(i * 1024 + s * 512, 512)
                dve.wait_ge(chunk_done, i * 2 + (s + 1))
                dve.tensor_tensor(row[:, at], ada[0:NCOND, :], ba[:, at], ALU.add).then_inc(row_done, 1)

            dve.wait_ge(dt_act, 4)
            dve.scalar_tensor_tensor(flat(m.dt), flat(m.dt), 0.0, sp[:, :], ALU.max, ALU.add).then_inc(dt_step, 1)
            dve.wait_ge(dt_step, 1)
            dve.scalar_tensor_tensor(dtA[:, :, :], m.dt[:, :, :], -1.0, spread(a8[:, :], 1, NT), ALU.mult,
                                     ALU.mult).then_inc(ready, 1)

            def tile(i, sampled, first):
                w = 1 if sampled else 0
                dve.wait_ge(cum_made, i + 1)
                if not first:
                    dve.wait_ge(act_done, i * 3)
                dve.tensor_copy(cum[:, :], cs).then_inc(seg_step, 1)
                dve.wait_ge(rows_made, i + 1)
                dve.wait_ge(seg_step, i * 4 + 1)
                dve.tensor_tensor(seg[:, :, :], rows[:, :, :], spread(cum[:, 0:H], 2, P), ALU.subtract
                                  ).then_inc(seg_step, 1)
                if sampled:
                    dve.tensor_copy(lastc[:, :, :], rows[:, :, LSEQ - 1:P:LSEQ]).then_inc(seg_step, 1)
                else:
                    dve.tensor_copy(lastc[:, :, 0], rows[:, :, P - 1]).then_inc(seg_step, 1)
                dve.wait_ge(seg_step, i * 4 + 2)
                dve.tensor_tensor(seg[:, :, :], seg[:, :, :], spread(m.hide_ssd[:, w, :], 1, H), ALU.min
                                  ).then_inc(seg_step, 1)
                dve.wait_ge(cb_made, i + 1)
                dve.wait_ge(staged, i * 5 + 6)
                xs = xsP[:, :].rearrange("p (h d) -> p h d", h=H)
                dve.tensor_tensor(xdt[:, :, :], xs, spread(dts[:, :], 2, HD), ALU.mult).then_inc(x_ready, 1)
                dve.tensor_copy(Bn[:, :], bP).then_inc(x_ready, 1)
                dve.wait_ge(act_done, i * 3 + 1)
                dve.wait_ge(x_ready, i * 4 + 1)
                dve.tensor_tensor(xdte[:, :, :], xdt[:, :, :], spread(grow[:, 1, :], 2, HD), ALU.mult
                                  ).then_inc(x_ready, 1)
                if not first:
                    dve.wait_ge(y_step, i * 3)
                dve.tensor_tensor(xD[:, :, :], xs, spread(m.d_skip[:, :], 2, HD), ALU.mult).then_inc(x_ready, 1)
                dve.wait_ge(act_done, i * 3 + 3)
                for g in range(2):
                    hs = slice(4 * g, 4 * g + 4)
                    op = dve.tensor_tensor(W[:, hs, :], dec[:, hs, :], spread(cb[:, g, :], 1, 4), ALU.mult)
                op.then_inc(w_ready, 1)
                if not sampled:
                    add_bias(i, 0)
                if sampled:
                    dve.wait_ge(x_ready, 4 * NP + 2)
                    dve.tensor_tensor(Bm[:, :, :], spread(Bn[:, :], 1, NSEQ), spread(m.same[:, 0:P:LSEQ], 2, P),
                                      ALU.mult).then_inc(bm_ready, 1)
                dve.wait_ge(y_made, i + 1)
                out = (m.oN[:, NP, 512:] if sampled else
                       m.oN[:, ds(i, 1), 512:].rearrange("p a n -> p (a n)")).rearrange("p (h d) -> p h d", h=H)
                by_head = lambda v: v[:, :].rearrange("p (h d) -> p h d", h=H)
                dve.tensor_tensor(out, by_head(yo), spread(grow[:, 0, :], 2, HD), ALU.mult).then_inc(y_step, 1)
                dve.wait_ge(y_step, i * 3 + 1)
                dve.tensor_tensor(out, out, by_head(yd), ALU.add).then_inc(y_step, 1)
                dve.wait_ge(y_step, i * 3 + 2)
                dve.wait_ge(x_ready, i * 4 + 4)
                dve.tensor_tensor(out, out, xD[:, :, :], ALU.add).then_inc(y_step, 1)
                if not sampled:
                    for step in range(2):
                        for g in range(2):
                            r = slice(64 * g, 64 * g + 64)
                            cols = slice(g * 256, (g + 1) * 256)
                            st = state[r, cols].rearrange("p (k d) -> p k d", k=4)
                            if step == 0:
                                dve.tensor_tensor(st, st, spread(cdec[r, 4 * g:4 * g + 4, 0], 2, HD), ALU.mult
                                                  ).then_inc(state_step, 1)
                            else:
                                dve.wait_ge(state_step, i * 4 + (2 + g))
                                dve.tensor_tensor(state[r, cols], state[r, cols], S[r, cols], ALU.add
                                                  ).then_inc(state_step, 1)
                    add_bias(i, 1)

            dve.wait_ge(state_step, 1)
            tile(0, False, True)
            with dve.Fori(1, NP) as i:
                tile(i, False, False)
            dve.wait_ge(col_done, 1)
            take_columns(dve, m, ada, gcol, 1, scaled)
            tile(NP, True, False)
            for g in range(2):
                r = slice(64 * g, 64 * g + 64)
                st = own(sst, g).rearrange("p b (k d) -> p b k d", k=4)
                by_seq = cdec[r, 4 * g:4 * g + 4, :].rearrange("p k b -> p b k")
                dve.tensor_tensor(st, st, spread(by_seq, 3, HD), ALU.mult).then_inc(aged, 1)
            dve.wait_ge(aged, 2)
            for b in range(NSEQ):
                dve.wait_ge(s_made, b + 1)
                for g in range(2):
                    r, cols = slice(64 * g, 64 * g + 64), slice(g * 256, (g + 1) * 256)
                    dve.tensor_tensor(sst[r, b, cols], sst[r, b, cols], Spair[b % 2][r, cols], ALU.add
                                      ).then_inc(s_taken, 1)
            dve.wait_ge(gate_silu, 1)
            dve.wait_ge(y_step, 3 * NT)
            dve.tensor_tensor(m.oN[:, :, 512:], m.oN[:, :, 512:], m.zN[:, :, :], ALU.mult).then_inc(gated, 1)


def attend(nc, m, T, sem, sb, psctx):
    m.sp_new = sb("sp_new", [P, H, P])
    cache = Cache(sem, sb)
    attend_own(nc, m, T, sem, sb, psctx, cache)
    attend_past(nc, m, sem, psctx, T, cache)


class Cache:

    SLOTS, NJ = 4, PAST // P

    def __init__(self, sem, sb):
        self.kT, self.v = sb("past_k", [P, self.SLOTS, 4, PAST]), sb("past_v", [P, self.SLOTS, self.NJ, 512])
        self.k_came, self.v_came = ([sem(f"past_{n}{s}") for s in range(self.SLOTS)] for n in ("k_in", "v_in"))

    def load_k(self, eng, T, b):
        s = b % self.SLOTS
        eng.dma_start(self.kT[:, s, :, :], T["cache_kT"][b]).then_inc(self.k_came[s], 16)

    def load_v(self, eng, T, b):
        s = b % self.SLOTS
        eng.dma_start(self.v[:, s, :, :], T["cache_v"][b].rearrange("(j p) n -> p j n", p=P)).then_inc(self.v_came[s], 16)


def attend_own(nc, m, T, sem, sb, psctx, cache):
    ND = NT * P
    OFF = {0: (ND, 3), 1: (ND + 3 * P, 2), 2: (ND + 5 * P, 1)}
    NW = ND + 6 * P
    SC = HD ** -0.5
    with scope(nc.sbuf_tensor) as tmp, psctx() as ps:
        kS = tmp("kS", [P, TOK])
        qB = tmp("qB", [P, 2, TOK])
        z, a, w = (tmp(n, [P, 2, NW]) for n in ("own_z", "own_a", "own_w"))
        zP, SP = ps("own_zP", [P, 1536]), ps("own_SP", [P, 1536])
        oP = ps("own_oP", [P, 2, 512])
        zeroed, staged = sem("own_zeroed"), sem("own_staged")
        z_made, z_taken, ln_step, sp_step = (sem("own_" + n) for n in ("zmade", "ztaken", "lnstep", "spstep"))
        s_made, arg_step, w_done, o_made, o_taken = (sem("own_" + n) for n in ("smade", "argstep", "wdone", "omade", "otaken"))
        with nc.Block() as block:
            @block.sync
            def _(sp):
                for b in range(cache.SLOTS):
                    cache.load_k(sp, T, b)
                    cache.load_v(sp, T, b)

            @block.gpsimd
            def _(pool):
                pool.memset(qB[:, :, :], 0.0).then_inc(zeroed, 1)
                pool.wait_ge(zeroed, 1)

                def stage(i):
                    pool.tensor_copy(kS[:, :], m.qkT[:, ds(i + 4, 1), :].rearrange("p a n -> p (a n)")).then_inc(staged, 1)
                    for g in range(2):
                        r = slice(64 * g, 64 * g + 64)
                        pool.wait_ge(zeroed, 1)
                        pool.wait_ge(staged, i * 3 + (g + 1))
                        pool.tensor_copy(qB[r, g, :], m.qkT[r, ds(i, 1), :].rearrange("p a n -> p (a n)")).then_inc(staged, 1)

                stage(0)
                with pool.Fori(1, 4) as i:
                    pool.wait_ge(zeroed, 1)
                    pool.wait_ge(z_made, i * 2)
                    stage(i)

            @block.tensor
            def _(pe):
                def scores(i, first=False):
                    pe.wait_ge(staged, i * 3 + 3)
                    for s in range(2):
                        if s or not first:
                            pe.wait_ge(z_taken, i * 2 + s)
                        for j in range(NT):
                            c = slice(j * P, (j + 1) * P)
                            mm = pe.matmul(zP[:, c], kS[:, c], qB[:, s, c], start=True, stop=True)
                            if j in OFF:
                                at, n = OFF[j]
                                mm = pe.matmul(zP[:, at:at + n * P], kS[:, c], qB[:, s, (j + 1) * P:(j + 1 + n) * P],
                                               start=True, stop=True)
                        mm.then_inc(z_made, 1)

                def sums(i, first=False):
                    for s in range(2):
                        pe.wait_ge(sp_step, i * 4 + (2 * s + 2))
                        if s or not first:
                            pe.wait_ge(arg_step, i * 4 + 2 * s)
                        sp = a[:, s, :]
                        pe.matmul(SP[:, 0:512], m.from_[:, :], sp[:, 0:512], start=True, stop=True)
                        pe.matmul(SP[:, 512:ND], m.from_[:, :], sp[:, 512:ND], start=True, stop=True)
                        for j, (at, n) in OFF.items():
                            pe.matmul(SP[:, at:at + n * P], m.from_[:, :], sp[:, at:at + n * P], start=True, stop=False)
                            for jj in range(j + 1, 4):
                                o = at + (jj - j - 1) * P
                                mm = pe.matmul(SP[:, o:o + P], m.ones[:, :], sp[:, jj * P:(jj + 1) * P],
                                               start=False, stop=(jj == 3))
                                if jj in OFF:
                                    a2, n2 = OFF[jj]
                                    mm = pe.matmul(SP[:, o + P:o + P + n2 * P], m.ones[:, :], sp[:, a2:a2 + n2 * P],
                                                   start=False, stop=False)
                        mm.then_inc(s_made, 1)

                def outputs(i, first=False):
                    for s in range(2):
                        pe.wait_ge(w_done, i * 2 + (s + 1))
                        if not first:
                            pe.wait_ge(o_taken, i * 2 - (1 - s))
                        for q in range(NT):
                            keys = range(q + 1) if q < 4 else [4]
                            for j in keys:
                                c = j * P if j == q else OFF[j][0] + (q - j - 1) * P
                                mm = pe.matmul(oP[:, s, q * HD:(q + 1) * HD], w[:, s, c:c + P],
                                               m.vN[:, j, ds(i * 128 + s * HD, HD)], start=(j == keys[0]), stop=(j == q))
                        mm.then_inc(o_made, 1)
                scores(0, True)
                sums(0, True)
                scores(1)
                outputs(0, True)
                with pe.Fori(1, 3) as i:
                    sums(i)
                    scores(i + 1)
                    outputs(i)
                sums(3)
                outputs(3)

            @block.scalar
            def _(act):
                def log_terms(i, first=False):
                    for s in range(2):
                        act.wait_ge(z_taken, i * 2 + (s + 1))
                        if not first:
                            act.wait_ge(s_made, i * 2 - (1 - s))
                        act.activation(a[:, s, :], z[:, s, :], ACT.Abs).then_inc(ln_step, 1)
                        act.wait_ge(ln_step, i * 6 + (3 * s + 1))
                        act.activation(a[:, s, :], a[:, s, :], ACT.Exp, scale=-1.0).then_inc(ln_step, 1)
                        act.wait_ge(ln_step, i * 6 + (3 * s + 2))
                        act.activation(a[:, s, :], a[:, s, :], ACT.Ln, bias=1.0).then_inc(ln_step, 1)

                def weights(i):
                    for s in range(2):
                        act.wait_ge(arg_step, i * 4 + (2 * s + 2))
                        act.activation(w[:, s, :], w[:, s, :], ACT.Exp).then_inc(w_done, 1)

                log_terms(0, True)
                with act.Fori(0, 3) as i:
                    weights(i)
                    log_terms(i + 1)
                weights(3)

            @block.vector
            def _(dve):
                def softplus(i):
                    for s in range(2):
                        dve.wait_ge(z_made, i * 2 + (s + 1))
                        dve.tensor_scalar(z[:, s, :], zP[:, 0:NW], SC, None, ALU.mult).then_inc(z_taken, 1)
                    for s in range(2):
                        dve.wait_ge(ln_step, i * 6 + (3 * s + 3))
                        dve.scalar_tensor_tensor(a[:, s, :], z[:, s, :], 0.0, a[:, s, :], ALU.max, ALU.add
                                                 ).then_inc(sp_step, 1)
                        dve.wait_ge(sp_step, i * 4 + (2 * s + 1))
                        seen = m.seen[:, :, :].rearrange("p t q -> p (t q)")
                        dve.tensor_tensor(a[:, s, 0:ND], a[:, s, 0:ND], seen, ALU.mult).then_inc(sp_step, 1)
                        dve.wait_ge(sp_step, i * 4 + (2 * s + 2))
                        dve.tensor_copy(m.sp_new[:, ds(i * 2 + s, 1), :].rearrange("p a n -> p (a n)"),
                                        a[:, s, ND - P:ND])

                def exponents(i):
                    for s in range(2):
                        dve.wait_ge(s_made, i * 2 + (s + 1))
                        dve.tensor_tensor(w[:, s, :], z[:, s, :], SP[:, 0:NW], ALU.subtract).then_inc(arg_step, 1)
                        dve.wait_ge(arg_step, i * 4 + (2 * s + 1))
                        hide = m.hide[:, :, :].rearrange("p t q -> p (t q)")
                        dve.tensor_tensor(w[:, s, 0:ND], w[:, s, 0:ND], hide, ALU.min).then_inc(arg_step, 1)

                def take(i):
                    for s in range(2):
                        dve.wait_ge(o_made, i * 2 + (s + 1))
                        dve.tensor_copy(m.oN[:, :, ds(i * 128 + s * HD, HD)],
                                        oP[:, s, 0:NT * HD].rearrange("p (t d) -> p t d", t=NT)).then_inc(o_taken, 1)

                softplus(0)
                with dve.Fori(0, 3) as i:
                    exponents(i)
                    softplus(i + 1)
                    take(i)
                exponents(3)
                take(3)


def attend_past(nc, m, sem, psctx, T, cache):
    NJ, NS = cache.NJ, cache.SLOTS
    NG = NSEQ // NS
    SC = HD ** -0.5
    kT, vb = cache.kT, cache.v
    with scope(nc.sbuf_tensor) as tmp, psctx() as ps:
        qB = tmp("past_q", [P, 4, 2, P])
        z, a, w = (tmp(n, [P, NS, NJ, P]) for n in ("past_z", "past_a", "past_w"))
        own_head = tmp("past_own", [P, H, HD])
        o_head = tmp("past_oh", [P, NSEQ, 512])
        query = tmp("past_query", [P, 2 * P - LSEQ])
        zP, SP = ps("past_zP", [P, NS, 512]), ps("past_SP", [P, NS, 512])
        oP, back = SP, zP[:, 0, :]
        zeroed, q_ready, heads_ready, query_ready = (sem("past_" + n) for n in ("zeroed", "q_ready", "heads", "query"))
        z_made, z_taken, ln_step, sp_done = (sem("past_" + n) for n in ("zmade", "ztaken", "lnstep", "spdone"))
        s_made, arg_done, w_done, o_made, o_taken = (sem("past_" + n) for n in ("smade", "argdone", "wdone", "omade", "otaken"))
        back_made, added = sem("past_back_made"), sem("past_added")
        cols = lambda g, s: slice((g * NS + s) * LSEQ, (g * NS + s + 1) * LSEQ)
        with nc.Block() as block:
            @block.sync
            def _(sp):
                for b in range(NS, NSEQ):
                    sp.wait_ge(z_made, b - NS + 1)
                    cache.load_k(sp, T, b)
                for b in range(NS, NSEQ):
                    sp.wait_ge(o_made, b - NS + 1)
                    cache.load_v(sp, T, b)

            @block.gpsimd
            def _(pool):
                pool.memset(qB[:, :, :, :], 0.0).then_inc(zeroed, 1)
                pool.memset(own_head[:, :, :], 1.0).then_inc(zeroed, 1)
                pool.memset(query[:, :], 0.0).then_inc(zeroed, 1)
                pool.wait_ge(zeroed, 3)
                for g in range(2):
                    r = slice(64 * g, 64 * g + 64)
                    if g:
                        pool.wait_ge(q_ready, g)
                    pool.tensor_copy(qB[r, :, g, :], m.qkT[r, 0:4, SEQ:TOK]).then_inc(q_ready, 1)
                pool.wait_ge(q_ready, 2)
                pool.affine_select(out=own_head[:, :, :], in_=own_head[:, :, :], compare_op=ALU.is_ge, fill=0.0, base=0,
                                   pattern=[[-LSEQ, H], [0, HD]], channel_multiplier=1).then_inc(heads_ready, 1)
                pool.wait_ge(heads_ready, 1)
                pool.affine_select(out=own_head[:, :, :], in_=own_head[:, :, :], compare_op=ALU.is_ge, fill=0.0,
                                   base=LSEQ - 1, pattern=[[LSEQ, H], [0, HD]], channel_multiplier=-1).then_inc(heads_ready, 1)

            @block.tensor
            def _(pe):
                def scores(g):
                    for s in range(NS):
                        pe.wait_ge(cache.k_came[s], g * 16 + 16)
                        if g:
                            pe.wait_ge(z_taken, g * NS - (NS - 1 - s))
                        for j in range(NJ):
                            for k in range(4):
                                mm = pe.matmul(zP[:, s, j * P + k * 32:j * P + k * 32 + 32], kT[:, s, k, j * P:(j + 1) * P],
                                               qB[:, k, :, cols(g, s)], start=True, stop=True)
                        mm.then_inc(z_made, 1)

                def sums(g):
                    for s in range(NS):
                        pe.wait_ge(sp_done, g * NS + (s + 1))
                        if g:
                            pe.wait_ge(o_taken, g * NS - (NS - 1 - s))
                        out = SP[:, s, :].rearrange("p (j c) -> p j c", j=NJ)
                        pe.matmul(out, m.from_[:, :], a[:, s, :, :], start=True, stop=False)
                        for j in range(1, NJ):
                            pe.matmul(out[:, 0:j, :], m.ones[:, :], spread(a[:, s, j, :], 1, j), start=False, stop=False)
                        pe.matmul(SP[:, s, :].rearrange("p (j h q) -> p j h q", j=NJ, h=H), m.ones[:, :],
                                  spread(m.sp_new[:, :, cols(g, s)], 1, NJ), start=False, stop=True).then_inc(s_made, 1)

                def outputs(g):
                    for s in range(NS):
                        pe.wait_ge(w_done, g * NS + (s + 1))
                        pe.wait_ge(cache.v_came[s], g * 16 + 16)
                        for j in range(NJ):
                            mm = pe.matmul(oP[:, s, :], w[:, s, j, :], vb[:, s, j, :], start=(j == 0), stop=(j == NJ - 1))
                        mm.then_inc(o_made, 1)

                pe.wait_ge(q_ready, 2)
                scores(0)
                for g in range(NG):
                    sums(g)
                    if g < NG - 1:
                        scores(g + 1)
                    outputs(g)
                pe.wait_ge(query_ready, 1)
                for b in range(NSEQ):
                    pe.wait_ge(o_taken, b + 1)
                    at = P - LSEQ - b * LSEQ
                    mm = pe.matmul(back, query[:, at:at + P], o_head[:, b, :], start=(b == 0), stop=(b == NSEQ - 1))
                mm.then_inc(back_made, 1)

            @block.scalar
            def _(act):
                def log_terms(g):
                    for step, half in ((step, half) for step in range(3) for half in range(2)):
                        two = slice(2 * half, 2 * half + 2)
                        if step == 0:
                            act.wait_ge(z_taken, g * NS + (2 * half + 2))
                            act.activation(a[:, two, :, :], z[:, two, :, :], ACT.Abs).then_inc(ln_step, 1)
                        elif step == 1:
                            act.wait_ge(ln_step, g * 6 + (half + 1))
                            act.activation(a[:, two, :, :], a[:, two, :, :], ACT.Exp, scale=-1.0).then_inc(ln_step, 1)
                        else:
                            act.wait_ge(ln_step, g * 6 + (half + 3))
                            act.activation(a[:, two, :, :], a[:, two, :, :], ACT.Ln, bias=1.0).then_inc(ln_step, 1)

                log_terms(0)
                for g in range(NG):
                    for s in range(NS):
                        act.wait_ge(arg_done, g * NS + (s + 1))
                        act.activation(w[:, s, :, :], w[:, s, :, :], ACT.Exp).then_inc(w_done, 1)
                    if g < NG - 1:
                        act.wait_ge(s_made, (g + 1) * NS)
                        log_terms(g + 1)

            @block.vector
            def _(dve):
                flat = lambda t, s: t[:, s, :, :].rearrange("p j c -> p (j c)")

                def softplus(g):
                    for s in range(NS):
                        if g:
                            dve.wait_ge(arg_done, g * NS - (NS - 1 - s))
                        dve.wait_ge(z_made, g * NS + (s + 1))
                        dve.tensor_scalar(flat(z, s), zP[:, s, :], SC, None, ALU.mult).then_inc(z_taken, 1)
                    for s in range(NS):
                        dve.wait_ge(ln_step, g * 6 + (5 + s // 2))
                        dve.scalar_tensor_tensor(flat(a, s), flat(z, s), 0.0, flat(a, s), ALU.max, ALU.add
                                                 ).then_inc(sp_done, 1)

                softplus(0)
                dve.wait_ge(zeroed, 3)
                dve.tensor_reduce(query[:, P - LSEQ:P], m.ident[:, :].rearrange("p (h q) -> p q h", h=H), AX, ALU.add
                                  ).then_inc(query_ready, 1)
                for g in range(NG):
                    for s in range(NS):
                        dve.wait_ge(s_made, g * NS + (s + 1))
                        dve.tensor_tensor(flat(w, s), flat(z, s), SP[:, s, :], ALU.subtract).then_inc(arg_done, 1)
                    if g < NG - 1:
                        softplus(g + 1)
                    dve.wait_ge(heads_ready, 2)
                    for s in range(NS):
                        dve.wait_ge(o_made, g * NS + (s + 1))
                        dve.tensor_tensor(o_head[:, g * NS + s, :], oP[:, s, :],
                                          own_head[:, :, :].rearrange("p h d -> p (h d)"), ALU.mult).then_inc(o_taken, 1)
                dve.wait_ge(back_made, 1)
                dve.tensor_tensor(m.oN[:, NT - 1, 0:512], m.oN[:, NT - 1, 0:512], back, ALU.add).then_inc(added, 1)


class Residual:

    def __init__(self, sem, sb, name, base, g_post, gate, keep, gates, late=0):
        self.gates = gates
        self.late = late
        self.post = sb(name + "_post", [P, D])
        self.base, self.g_post, self.gate, self.keep = base, g_post, gate, keep
        self.came, self.base_in = sem(name + "_ld"), [sem(f"{name}_base{t}") for t in range(NT)]

    def load(self, sp, T):
        sp.dma_start(self.post[:, :], self.g_post.partition_broadcast(P)).then_inc(self.came, 16)
        sp.dma_start(self.gates[:, 0, :], T["gates"][self.gate, 0].partition_broadcast(P)).then_inc(self.came, 16)
        for b in range(NSEQ):
            sp.dma_start(self.gates[b * LSEQ:(b + 1) * LSEQ, 1, :],
                         T["gates"][self.gate, b + 1].partition_broadcast(LSEQ)).then_inc(self.came, 16)
        self.load_base(sp, range(NT - self.late))

    def load_base(self, sp, tiles):
        for t in tiles:
            sp.dma_start(self.keep[t], self.base[t * P:(t + 1) * P, :]).then_inc(self.base_in[t], 16)


def add_residual(nc, m, sem, name, res, src, store, junk):
    gates, post, keep = res.gates, res.post, res.keep
    ld, base_in = res.came, res.base_in
    gate_ready, squared, mean, rstd, step, stored = (
        sem(f"{name}_{n}") for n in ("gate", "sq", "mean", "rstd", "step", "stored"))
    with nc.Block() as block:
        @block.sync
        def _(sp):
            res.load_base(sp, range(NT - res.late, NT))
            for t in range(NT):
                sp.wait_ge(step, 2 * t + 2)
                sp.dma_start(store[t * P:(t + 1) * P, :], keep[t]).then_inc(stored, 16)
            sp.wait_ge(stored, 16 * NT)

        @block.scalar
        def _(act):
            for t in range(NT):
                if t >= 2:
                    act.wait_ge(squared, t - 1)
                act.activation(junk[:, t % 2, :], src[:, t, :], ACT.Square,
                               accum_out=m.stat[:, t:t + 1]).then_inc(squared, 1)

        @block.gpsimd
        def _(pool):
            pool.wait_ge(mean, 1)
            pool.tensor_tensor(m.rstd[:, :], m.stat[:, :], m.mhalf[:, 0:NT], ALU.pow).then_inc(rstd, 1)

        @block.vector
        def _(dve):
            dve.wait_ge(ld, 16 * (2 + NSEQ))
            dve.tensor_tensor(gates[:, :, :], gates[:, :, :], spread(post[:, :], 1, 2), ALU.mult).then_inc(gate_ready, 1)
            dve.wait_ge(squared, NT)
            dve.tensor_scalar(m.stat[:, :], m.stat[:, :], 1.0 / D, EPS, ALU.mult, ALU.add).then_inc(mean, 1)
            dve.wait_ge(rstd, 1)
            dve.wait_ge(gate_ready, 1)
            for t in range(NT):
                dve.scalar_tensor_tensor(src[:, t, :], src[:, t, :], m.rstd[:, t:t + 1], gates[:, t // (NT - 1), :],
                                         ALU.mult, ALU.mult).then_inc(step, 1)
                dve.wait_ge(step, 2 * t + 1)
                dve.wait_ge(base_in[t], 16)
                dve.tensor_tensor(keep[t], keep[t], src[:, t, :], ALU.add).then_inc(step, 1)


def mixer_columns(nc, m, T, sem, sb, ps, oT, junk, ahead):
    NH = 2 * NT
    g = sb("g_mix", [P, KD])
    stat, rstd = sb("mix_stat", [P, NH]), sb("mix_rstd", [P, NH])
    pr, sa = ps("mixc_p", [P, 2, 512]), ps("mixc_s", [P, 2, 512])
    ld, squared, mean, rooted, normed, turned, taken = (
        sem("mixc_" + n) for n in ("ld", "sq", "mean", "rstd", "normed", "turned", "taken"))
    with nc.Block() as block:
        @block.sync
        def _(sp):
            sp.dma_start(g[:, :], T["g_mix"]).then_inc(ld, 16)
            ahead(sp)

        @block.scalar
        def _(act):
            for n in range(NH):
                t, half = n // 2, n % 2
                if n >= 2:
                    act.wait_ge(squared, n - 1)
                act.activation(junk[:, n % 2, :], m.oN[:, t, half * 512:(half + 1) * 512], ACT.Square,
                               accum_out=stat[:, n:n + 1]).then_inc(squared, 1)

        @block.gpsimd
        def _(pool):
            pool.wait_ge(mean, 1)
            pool.tensor_tensor(rstd[:, :], stat[:, :], m.mhalf[:, :], ALU.pow).then_inc(rooted, 1)

        @block.vector
        def _(dve):
            dve.wait_ge(squared, NH)
            dve.tensor_scalar(stat[:, :], stat[:, :], 1.0 / 512, EPS, ALU.mult, ALU.add).then_inc(mean, 1)
            dve.wait_ge(rooted, 1)
            for n in range(NH):
                v = m.oN[:, n // 2, (n % 2) * 512:(n % 2 + 1) * 512]
                dve.tensor_scalar(v, v, rstd[:, n:n + 1], None, ALU.mult).then_inc(normed, 1)
            dve.wait_ge(ld, 16)
            for k in range(KD):
                dve.wait_ge(turned, k + 1)
                dve.tensor_scalar(oT[:, k, 0:SEQ], pr[:, k % 2, :], g[:, k:k + 1], None, ALU.mult).then_inc(taken, 1)
                dve.tensor_scalar(oT[:, k, SEQ:], sa[:, k % 2, 0:P], g[:, k:k + 1], None, ALU.mult).then_inc(taken, 1)

        @block.tensor
        def _(pe):
            pe.wait_ge(normed, NH)
            for k in range(KD):
                if k >= 2:
                    pe.wait_ge(taken, 2 * (k - 1))
                for t in range(NT):
                    out = pr[:, k % 2, t * P:(t + 1) * P] if t < NT - 1 else sa[:, k % 2, 0:P]
                    mm = pe.transpose(out, m.oN[:, t, k * P:(k + 1) * P], m.ident[:, :])
                mm.then_inc(turned, 1)


def mix(nc, m, T, sem, sb, psctx):
    with scope(nc.sbuf_tensor) as tmp:
        x1 = tmp("x1", [P, NT, D])
        mx = tmp("mx", [P, NT, D])
        res = Residual(sem, tmp, "res1", T["x"], T["g_post_mix"], 0, [x1[:, t, :] for t in range(NT)],
                       tmp("res1_gates", [P, 2, D]))
        with scope(nc.sbuf_tensor) as tmp2:
            oT = m.qhT
            w = tmp2("w_out", [P, KD, D])
            w_in, made, taken = [sem(f"w_out{k}") for k in range(KD)], sem("mix_made"), sem("mix_taken")

            def load_w(sp):
                for k in range(KD):
                    sp.dma_start(w[:, k, :], T["w_out"][k * P:(k + 1) * P, :]).then_inc(w_in[k], 16)

            with psctx() as ps:
                mixer_columns(nc, m, T, sem, tmp2, ps, oT, mx[:, 0, :].rearrange("p (a n) -> p a n", a=2), load_w)
            with psctx() as ps, nc.Block() as block:
                acc = ps("mix_ps", [P, 2, 2, 512])

                @block.sync
                def _(sp):
                    res.load(sp, T)

                @block.tensor
                def _(pe):
                    for t in range(NT):
                        if t >= 2:
                            pe.wait_ge(taken, t - 1)
                        for k in range(KD):
                            if t == 0:
                                pe.wait_ge(w_in[k], 16)
                            for h in range(2):
                                mm = pe.matmul(acc[:, t % 2, h, :], oT[:, k, t * P:(t + 1) * P],
                                               w[:, k, h * 512:(h + 1) * 512], start=(k == 0), stop=(k == KD - 1))
                        mm.then_inc(made, 1)

                @block.scalar
                def _(act):
                    for t in range(NT):
                        act.wait_ge(made, t + 1)
                        act.copy(mx[:, t, :].rearrange("p (h n) -> p h n", h=2), acc[:, t % 2, :, :]).then_inc(taken, 1)
        with scope(nc.sbuf_tensor) as tmp2:
            add_residual(nc, m, sem, "res1", res, mx, T["x1"], tmp2("res1_junk", [P, 2, D]))
        m.junk = mx
        with scope(nc.sbuf_tensor) as tmp2:
            h2T = tmp2("h2T", [P, KD, TOK])
            ring = SplitRing(sem, "pq_w", T["w_pq"], memory=m.u)

            def load_weights(sp):
                for n in range(2):
                    ring.load(sp, n, n, True)

            with psctx() as ps:
                norm_to_columns(nc, m, sem, ps, "n2", None, x1, h2T, 1, load_weights)

            def sink(act, acc, made, taken):
                with act.Fori(0, 4) as i:
                    for s in range(2):
                        act.wait_ge(made, i * 2 + (s + 1))
                        act.copy(m.qhT[:, ds(i * 2 + s, 1), :].rearrange("p a (h n) -> p (a h) n", h=2),
                                 acc[:, s, :, 0:HALF]).then_inc(taken, 1)
            with psctx() as ps:
                column_products(nc, sem, ps, "pq", ring, 8, h2T, m.h2h, m.h2l, sink)


HT = 32
NHT = TOK // HT
GB = 4
TOPB, STEPB = 8, 8
NPRE = NT * (TOPB + STEPB)


def route(nc, m, T, sem, sb, psctx):
    NG = 2 * H
    NC = TOPK * TOPK
    skb = sb("skb", [P, 2, NKEY])
    rowv = lambda a, b: m.oN[:, a:b, :].rearrange("p a n -> p (a n)")
    s = rowv(0, 2).rearrange("p (g k) -> p g k", g=NG)
    cand = rowv(2, 4).rearrange("p (h c) -> p h c", h=H)
    qs = m.oN[:, 4, :].rearrange("p (h t) -> p h t", h=H)
    top, itop, itopf = sb("top", [P, NG, TOPK]), sb("itop", [P, NG, TOPK], U32), sb("itopf", [P, NG, TOPK])
    best, ci = sb("best", [P, H, TOPK]), sb("ci", [P, H, TOPK], U32)
    cab, cabf = sb("cab", [P, 2, H, TOPK], U32), sb("cabf", [P, 2, H, TOPK])
    hit = rowv(2, 4).rearrange("p (h r c) -> p h r c", h=H, r=TOPK)
    picks = sb("picks", [P, 3, H, TOPK])
    zs, rz = sb("zs", [P, H]), sb("rz", [P, H])
    picksT = sb("picksT", [P, 3, P])
    iota16 = sb("iota16", [P, TOPK])
    UN = 8
    NW = 3
    iota = sb("iota", [P, NKEY, UN], BF16)
    keyb, wb, rest = sb("keyb", [P, 2, P], BF16), sb("wb", [P, NW, P], BF16), sb("rest", [P, NW - 1, P])
    hot = sb("hot", [P, 2, 2, NKEY, UN], BF16)
    whot = sb("whot", [P, 2, NW, NKEY, UN], BF16)
    Gs = sb("Gs", [P, 2 * NKEY, HT])
    ga = sb("pre_ga", [P, 2, TOK])
    u = m.u
    setup, zeroed, keys_in = sem("route_setup"), sem("route_zeroed"), sem("keys_in")
    q_in, s_made, s_taken = sem("rq_in"), sem("rs_made"), sem("rs_taken")
    stepA, stepB, stepC = sem("routeA"), sem("routeB"), sem("routeC")
    exp_done, t_made, t_taken = sem("r_exp"), sem("rt_made"), sem("rt_taken")
    parts, hot_done, whot_done = sem("weight_parts"), sem("hot_done"), sem("whot_done")
    g_made, g_taken = sem("g_made"), sem("g_taken")
    g_out = [sem(f"g_out{n}") for n in range(2)]
    h_made, gelu_done, h_out = sem("pre_hmade"), sem("pre_gelu"), [sem(f"pre_out{n}") for n in range(2)]
    NA, NB, NCC = 5 * NG + 1, 5 * H + 2, 12
    EV = UN // 4
    STEPS = P // UN
    HS = HT // UN
    TB = TOPB + STEPB
    slots = lambda n: 8 * n

    def u_free(eng, n):
        eng.wait_ge(h_made, n * 2 - 2)

    with psctx() as ps, nc.Block() as block:
        sP = ps("route_s", [P, H, NKEY])
        tP = ps("route_t", [P, 512])
        gP = ps("route_g", [P, 2, 4, NKEY])
        hP = ps("pre_h", [P, 2, 512])

        @block.gpsimd
        def _(pool):
            pool.iota(iota[:, :, :], pattern=[[1, NKEY], [0, UN]], base=0, channel_multiplier=0,
                      allow_small_or_imprecise_dtypes=True).then_inc(setup, 1)
            pool.iota(iota16[:, :], pattern=[[1, TOPK]], base=0, channel_multiplier=0,
                      allow_small_or_imprecise_dtypes=True).then_inc(setup, 1)
            pool.memset(skb[:, :, :], 0.0).then_inc(zeroed, 1)
            for n in range(2):
                u.split_low(pool, n, n)
            with pool.Fori(1, NPRE // 2 + 1) as i:
                for n in range(2):
                    u_free(pool, i * 2 + n)
                    u.split_low(pool, i * 2 + n, n)

        @block.sync
        def _(sp):
            def store(n, slot):
                sp.wait_ge(gelu_done, n * 2 + 2)
                dst = T["HG"][n] if isinstance(n, int) else T["HG"][ds(n, 1)].rearrange("a p t -> (a p) t")
                sp.dma_start(dst, ga[:, slot, :]).then_inc(h_out[slot], 16)

            def blocks(base, count):
                for n in range(count):
                    u.load(sp, base + (n + 2), n % 2)
                    store(base + n, n % 2)

            for n in range(2):
                u.load(sp, n, n, True)
            sp.dma_start(qs, m.qhT[:, :, 0:P]).then_inc(q_in, 16)
            sp.wait_ge(zeroed, 1)
            for c in range(2):
                sp.dma_start(skb[64 * c:64 * c + 64, c, :], T["sub_keys"][64 * c:64 * c + 64, :]).then_inc(keys_in, 16)

            def tile(i, last):
                if not last:
                    sp.wait_ge(s_made, i * 2 + 2)
                    sp.dma_start(qs, m.qhT[:, :, ds(i * P + P, P)]).then_inc(q_in, 16)
                with sp.Fori(0, TOPB // 2) as j:
                    blocks(i * TB + j * 2, 2)
                with sp.Fori(0, STEPB // 2) as j:
                    blocks(i * TB + j * 2 + TOPB, 2)

            with sp.Fori(0, NT - 1) as i:
                tile(i, False)
            tile(NT - 1, True)
            for n in range(2):
                sp.wait_ge(h_out[n], 16 * (NPRE // 2))
            for slot in range(2):
                sp.wait_ge(g_out[slot], 8 * NHT)

        @block.tensor
        def _(pe):
            def scores(i, first):
                pe.wait_ge(q_in, i * 16 + 16)
                if first:
                    pe.wait_ge(keys_in, 32)
                for part in range(2):
                    if part or not first:
                        pe.wait_ge(s_taken, i * 2 + part)
                    for h in range(4):
                        mm = pe.matmul(sP[:, 2 * h:2 * h + 2, :], qs[:, part * 4 + h, :], skb[:, :, :],
                                       start=True, stop=True)
                    mm.then_inc(s_made, 1)

            def hidden(n, slot, half, first=False):
                if half == 0:
                    pe.wait_ge(u.low_done, n + 1)
                    pe.wait_ge(u.high_done, n + 1)
                if not first:
                    pe.wait_ge(gelu_done, n * 2 + (half - 1))
                c = slice(half * HALF, (half + 1) * HALF)
                for k in range(KD):
                    for w, x in ((u.high, m.h2h), (u.high, m.h2l), (u.low, m.h2h)):
                        mm = pe.matmul(hP[:, half, 0:HALF], w[:, slot, k, :], x[:, k, c],
                                       start=(k == 0 and w is u.high and x is m.h2h), stop=(k == KD - 1 and w is u.low))
                mm.then_inc(h_made, 1)

            def token_step(n, b):
                pe.wait_ge(whot_done, n + 1)
                for v in range(UN):
                    if v % 4 == 0:
                        pe.wait_ge(g_taken, n * EV + (v // 4 + 1))
                    for k in range(NW):
                        mm = pe.matmul(gP[:, v // 4, v % 4, :], hot[:, b, 0, :, v], whot[:, b, k, :, v],
                                       start=(k == 0), stop=(k == NW - 1))
                    if v % 4 == 3:
                        mm.then_inc(g_made, 1)

            def tile(i, first, last):
                for n in range(TOPB):
                    for half in range(2):
                        hidden(i * TB + n, n % 2, half, first and n == 0)
                pe.wait_ge(stepC, i * NCC + NCC)
                for c in range(3):
                    mm = pe.transpose(tP[:, c * P:(c + 1) * P], picks[:, c, :, :].rearrange("p h r -> p (h r)"), m.ident[:, :])
                mm.then_inc(t_made, 1)
                if not last:
                    scores(i + 1, False)
                for q in range(STEPS):
                    n = TOPB + q // 2
                    hidden(i * TB + n, n % 2, q % 2)
                    token_step(i * STEPS + q, q % 2)

            pe.sem_inc(g_made, 2 * EV)
            scores(0, True)
            tile(0, True, False)
            with pe.Fori(1, NT - 1) as i:
                tile(i, False, False)
            tile(NT - 1, False, True)

        @block.scalar
        def _(act):
            def split(n, slot, arrived, first=False):
                act.wait_ge(u.came[slot], arrived)
                if not first:
                    u_free(act, n)
                act.copy(u.high[:, slot, :, :], u.raw[:, slot, :, :]).then_inc(u.high_done, 1)

            def gelu(n, slot, half, stored=None):
                act.wait_ge(h_made, n * 2 + (half + 1))
                if stored is not None and half == 0:
                    act.wait_ge(h_out[slot], stored)
                act.activation(ga[:, slot, half * HALF:(half + 1) * HALF], hP[:, half, 0:HALF], ACT.Gelu_apprx_tanh
                               ).then_inc(gelu_done, 1)

            def take(i, first):
                for part in range(2):
                    act.wait_ge(s_made, i * 2 + (part + 1))
                    if not first and part == 0:
                        act.wait_ge(stepA, i * NA)
                    act.copy(s[:, 8 * part:8 * part + 8, :], sP[:, :, :]).then_inc(s_taken, 1)

            def gelu_and_split(i, n, half, first):
                stored = None if half or (first and n < 2) else i * slots(TB) + slots(n - n % 2)
                gelu(i * TB + n, n % 2, half, stored)
                if half:
                    split(i * TB + (n + 2), n % 2, i * slots(TB) + slots(n - n % 2 + 4))

            def tile(i, first, last):
                for n in range(TOPB):
                    if n == TOPB - 1:
                        act.wait_ge(stepB, i * (NB + 1) + (NB + 1))
                        act.activation(best[:, :, :], best[:, :, :], ACT.Exp).then_inc(exp_done, 1)
                    for half in range(2):
                        gelu_and_split(i, n, half, first)
                act.wait_ge(t_made, i + 1)
                act.copy(picksT[:, :, :].rearrange("p c t -> p (c t)"), tP[:, 0:3 * P]).then_inc(t_taken, 1)
                if not last:
                    take(i + 1, False)
                for q in range(STEPS):
                    part, hf = q // HS, q // HS % 2
                    gelu_and_split(i, TOPB + q // 2, q % 2, first)
                    if q % HS == 0 and not (first and part < 2):
                        act.wait_ge(g_out[hf], i * 32 + 16 * (part // 2))
                    for e in range(EV):
                        act.wait_ge(g_made, (i * STEPS + q) * EV + (2 * EV + e + 1))
                        t = q % HS * UN + 4 * e
                        act.copy(Gs[:, hf * NKEY:(hf + 1) * NKEY, t:t + 4].rearrange("p j t -> p t j"), gP[:, e, :, :]
                                 ).then_inc(g_taken, 1)
                    if q % HS == HS - 1:
                        act.wait_ge(g_taken, (i * STEPS + q) * EV + 2 * EV)
                        act.dma_start(T["G"][ds(i * (P // HT) + part, 1)].rearrange("a p j t -> (a p) j t")
                                      if not isinstance(i, int) else T["G"][i * (P // HT) + part], Gs[:, hf * NKEY:(hf + 1) * NKEY, :]).then_inc(g_out[hf], 16)

            act.sem_inc(g_taken, EV)
            for n in range(2):
                split(n, n, 16, True)
            take(0, True)
            tile(0, True, False)
            with act.Fori(1, NT - 1) as i:
                tile(i, False, False)
            tile(NT - 1, False, True)

        @block.vector
        def _(dve):
            def after(what, value):
                value = value if isinstance(value, int) else dve.to_reg(value)
                dve.wait_ge(setup, 2)
                dve.wait_ge(what, value)

            def tile(i, first):
                a0, b0, c0 = i * NA, i * (NB + 1), i * NCC
                after(s_taken, i * 2 + 2)
                for g in range(NG):
                    dve.max(top[:, g, 0:8], s[:, g, :]).then_inc(stepA, 1)
                after(stepA, a0 + NG)
                for g in range(NG):
                    dve.max_index(itop[:, g, 0:8], top[:, g, 0:8], s[:, g, :]).then_inc(stepA, 1)
                after(stepA, a0 + 2 * NG)
                for g in range(NG):
                    dve.match_replace(s[:, g, :], top[:, g, 0:8], s[:, g, :], -3e38).then_inc(stepA, 1)
                after(stepA, a0 + 3 * NG)
                for g in range(NG):
                    dve.max(top[:, g, 8:16], s[:, g, :]).then_inc(stepA, 1)
                after(stepA, a0 + 4 * NG)
                for g in range(NG):
                    dve.max_index(itop[:, g, 8:16], top[:, g, 8:16], s[:, g, :]).then_inc(stepA, 1)
                dve.wait_ge(stepA, a0 + 5 * NG)
                dve.tensor_copy(itopf[:, :, :], itop[:, :, :]).then_inc(stepA, 1)
                dve.tensor_tensor(cand[:, :, :].rearrange("p h (a b) -> p h a b", a=TOPK),
                                  spread(top[:, 0:NG:2, :], 3, TOPK), spread(top[:, 1:NG:2, :], 2, TOPK), ALU.add
                                  ).then_inc(stepB, 1)
                after(stepB, b0 + 1)
                for h in range(H):
                    dve.max(best[:, h, 0:8], cand[:, h, :]).then_inc(stepB, 1)
                after(stepB, b0 + (1 + H))
                for h in range(H):
                    dve.max_index(ci[:, h, 0:8], best[:, h, 0:8], cand[:, h, :]).then_inc(stepB, 1)
                after(stepB, b0 + (1 + 2 * H))
                for h in range(H):
                    dve.match_replace(cand[:, h, :], best[:, h, 0:8], cand[:, h, :], -3e38).then_inc(stepB, 1)
                after(stepB, b0 + (1 + 3 * H))
                for h in range(H):
                    dve.max(best[:, h, 8:16], cand[:, h, :]).then_inc(stepB, 1)
                after(stepB, b0 + (1 + 4 * H))
                for h in range(H):
                    dve.max_index(ci[:, h, 8:16], best[:, h, 8:16], cand[:, h, :]).then_inc(stepB, 1)
                dve.tensor_copy(zs[:, :], best[:, :, 0]).then_inc(stepB, 1)
                dve.wait_ge(stepB, b0 + NB)
                dve.tensor_tensor(best[:, :, :], best[:, :, :], spread(zs[:, :], 2, TOPK), ALU.subtract
                                  ).then_inc(stepB, 1)
                dve.tensor_scalar(cab[:, 0, :, :], ci[:, :, :], 4, None, ALU.logical_shift_right).then_inc(stepC, 1)
                dve.tensor_scalar(cab[:, 1, :, :], ci[:, :, :], 15, None, ALU.bitwise_and).then_inc(stepC, 1)
                dve.wait_ge(stepC, c0 + 2)
                dve.tensor_copy(cabf[:, :, :, :], cab[:, :, :, :]).then_inc(stepC, 1)
                dve.wait_ge(stepA, a0 + NA)
                if not first:
                    dve.wait_ge(t_made, i)
                for c in range(2):
                    dve.wait_ge(stepC, c0 + (3 + 3 * c))
                    dve.tensor_tensor(hit[:, :, :, :], spread(cabf[:, c, :, :], 3, TOPK),
                                      spread(spread(iota16[:, :], 1, TOPK), 1, H), ALU.is_equal).then_inc(stepC, 1)
                    dve.wait_ge(stepC, c0 + (4 + 3 * c))
                    dve.tensor_tensor(hit[:, :, :, :], hit[:, :, :, :], spread(itopf[:, c:NG:2, :], 2, TOPK), ALU.mult
                                      ).then_inc(stepC, 1)
                    dve.wait_ge(stepC, c0 + (5 + 3 * c))
                    dve.tensor_reduce(picks[:, c, :, :], hit[:, :, :, :], AX, ALU.add).then_inc(stepC, 1)
                dve.wait_ge(exp_done, i + 1)
                dve.tensor_reduce(zs[:, :], best[:, :, :], AX, ALU.add).then_inc(stepC, 1)
                dve.wait_ge(stepC, c0 + 10)
                dve.reciprocal(rz[:, :], zs[:, :]).then_inc(stepC, 1)
                dve.wait_ge(stepC, c0 + 11)
                dve.tensor_tensor(picks[:, 2, :, :], best[:, :, :], spread(rz[:, :], 2, TOPK), ALU.mult
                                  ).then_inc(stepC, 1)
                after(t_taken, i + 1)
                dve.tensor_copy(keyb[:, :, :], picksT[:, 0:2, :]).then_inc(parts, 1)
                dve.tensor_copy(wb[:, 0, :], picksT[:, 2, :]).then_inc(parts, 1)
                for k in range(1, NW):
                    whole = picksT[:, 2, :] if k == 1 else rest[:, k - 2, :]
                    dve.wait_ge(parts, i * (2 * NW) + 2 * k)
                    dve.tensor_tensor(rest[:, k - 1, :], whole, wb[:, k - 1, :], ALU.subtract).then_inc(parts, 1)
                    dve.wait_ge(parts, i * (2 * NW) + (2 * k + 1))
                    dve.tensor_copy(wb[:, k, :], rest[:, k - 1, :]).then_inc(parts, 1)
                after(parts, i * (2 * NW) + 2 * NW)
                with dve.Fori(0, STEPS // 2) as q:
                    for b in range(2):
                        n = i * STEPS + q * 2 + b
                        t = ds(q * (2 * UN) + b * UN, UN)
                        dve.wait_ge(g_made, n * EV + EV)
                        dve.tensor_tensor(hot[:, b, :, :, :], spread(iota[:, :, :], 1, 2), spread(keyb[:, :, t], 2, NKEY),
                                          ALU.is_equal).then_inc(hot_done, 1)
                        dve.wait_ge(hot_done, n + 1)
                        dve.tensor_tensor(whot[:, b, :, :, :], spread(hot[:, b, 1, :, :], 1, NW),
                                          spread(wb[:, :, t], 2, NKEY), ALU.mult).then_inc(whot_done, 1)

            tile(0, True)
            with dve.Fori(1, NT) as i:
                tile(i, False)


def experts(nc, m, T, sem, psctx, stored):
    NB = NKEY - NPRE
    NGR = NB // GB
    Y = m.oN
    u = m.u
    with scope(nc.sbuf_tensor) as tmp, psctx() as ps, nc.Block() as block:
        vr, vh, vl = tmp("vr", [P, 2, D]), tmp("vh", [P, GB, D], F32R), tmp("vl", [P, GB, D], F32R)
        gr = tmp("gr", [P, NHT, GB * HT])
        ga = tmp("ga", [P, 2, TOK])
        ah, al = tmp("ah", [P, GB, TOK], F32R), tmp("al", [P, GB, TOK], F32R)
        hP = ps("ex_h", [P, 2, 2, 512])
        yP = ps("ex_y", [P, 4, 512])
        v_in = [sem(f"v_in{n}") for n in range(2)]
        g_in = sem("G_in")
        vh_done, vl_done = sem("vh_done"), sem("vl_done")
        h_made, gelu_done, weighted, ah_done, al_done = (sem("ex_" + n) for n in ("hmade", "gelu", "weighted", "ah", "al"))
        y_made, y_taken, y_zero = sem("ex_ymade"), sem("ex_ytaken"), sem("ex_yzero")
        NY = 2 * NT
        YB = [max(y for y in range(NY) if y % 4 == a) for a in range(4)]
        Glayout = T["G"].rearrange("t p j n -> p t (j n)")

        @block.sync
        def _(sp):
            def load_g(g, first=False):
                if not first:
                    sp.wait_ge(weighted, g * GB)
                start = g * (GB * HT) + NPRE * HT
                sp.dma_start(gr[:, :, :], Glayout[:, :, start:start + GB * HT] if first
                             else Glayout[:, :, ds(start, GB * HT)]).then_inc(g_in, 16)

            load_g(0, True)
            with sp.Fori(0, NGR - 1) as g:
                for s in range(GB):
                    u.load(sp, g * GB + (NPRE + s + 2), s % 2)
                load_g(g + 1)
            for s in range(GB - 2):
                u.load(sp, NKEY - 2 + s, s % 2)
            stored.start(sp, T)

        @block.gpsimd
        def _(pool):
            def load_v(n, s, first=False):
                if not first:
                    pool.wait_ge(vl_done, n - 1)
                    pool.wait_ge(vh_done, n - 1)
                src = (T["v_tab"][NPRE + n] if isinstance(n, int)
                       else T["v_tab"][ds(n + NPRE, 1)].rearrange("a p n -> (a p) n"))
                pool.dma_start(vr[:, s, :], src).then_inc(v_in[s], 16)

            for n in range(2):
                load_v(n, n, True)
            with pool.Fori(1, NB // 2) as i:
                for s in range(2):
                    load_v(i * 2 + s, s)
            stored.start_v(pool, T)

        @block.tensor
        def _(pe):
            def hidden(n, s, first=False):
                pe.wait_ge(u.low_done, n + (NPRE + 1))
                pe.wait_ge(u.high_done, n + (NPRE + 1))
                if not first:
                    pe.wait_ge(gelu_done, n - 1)
                for k in range(KD):
                    for w, x in ((u.high, m.h2h), (u.high, m.h2l), (u.low, m.h2h)):
                        for half in range(2):
                            mm = pe.matmul(hP[:, s, half, 0:HALF], w[:, s, k, :], x[:, k, half * HALF:(half + 1) * HALF],
                                           start=(k == 0 and w is u.high and x is m.h2h),
                                           stop=(k == KD - 1 and w is u.low))
                mm.then_inc(h_made, 1)

            def outputs(g, first=False):
                pe.wait_ge(al_done, g * GB + GB)
                pe.wait_ge(vl_done, g * GB + GB)
                pe.wait_ge(vh_done, g * GB + GB)
                for y in range(NY):
                    t, d = y // 2, slice((y % 2) * 512, (y % 2 + 1) * 512)
                    if y >= 4 or not first:
                        before = y - 4 if y >= 4 else (YB[y] - NY)
                        pe.wait_ge(y_taken, g * NY + (before + 1))
                    for b in range(GB):
                        for a, v in ((ah, vh), (al, vh), (ah, vl)):
                            mm = pe.matmul(yP[:, y % 4, :], a[:, b, t * P:(t + 1) * P], v[:, b, d],
                                           start=(b == 0 and a is ah and v is vh), stop=(b == GB - 1 and v is vl))
                    mm.then_inc(y_made, 1)

            hidden(0, 0, True)
            hidden(1, 1, True)
            for s in range(2, GB + 1):
                hidden(s, s % 2)
            outputs(0, True)
            with pe.Fori(1, NGR - 1) as g:
                for s in range(1, GB + 1):
                    hidden(g * GB + s, s % 2)
                outputs(g)
            for s in range(1, GB):
                hidden(NB - GB + s, s % 2)
            outputs(NGR - 1)

        @block.scalar
        def _(act):
            def split_u(g, b):
                s = b % 2
                act.wait_ge(u.came[s], g * (8 * GB) + (8 * NPRE + 16 * (b // 2) + 16))
                act.wait_ge(h_made, g * GB + (b - 1))
                act.copy(u.high[:, s, :, :], u.raw[:, s, :, :]).then_inc(u.high_done, 1)

            def body(g, first, last):
                for s in range(GB):
                    n = g * GB + s
                    act.wait_ge(h_made, n + 1)
                    if not (first and s < 2):
                        act.wait_ge(al_done, n - 1)
                    act.activation(ga[:, s % 2, :].rearrange("p (h n) -> p h n", h=2), hP[:, s % 2, :, 0:HALF],
                                   ACT.Gelu_apprx_tanh).then_inc(gelu_done, 1)
                    if not (last and s >= GB - 2):
                        split_u(g, s + 2)
                    act.wait_ge(v_in[s % 2], g * (8 * GB) + (16 * (s // 2) + 16))
                    if not first and s == 0:
                        act.wait_ge(y_made, g * NY)
                    act.copy(vh[:, s, :], vr[:, s % 2, :]).then_inc(vh_done, 1)

            body(0, True, False)
            with act.Fori(1, NGR - 1) as g:
                body(g, False, False)
            body(NGR - 1, False, True)

        @block.vector
        def _(dve):
            dve.memset(Y[:, :, :], 0.0).then_inc(y_zero, 1)

            def split_u(n, s):
                u.split_low(dve, n + NPRE, s)

            def body(g, first, last):
                dve.wait_ge(g_in, g * 16 + 16)
                for s in range(GB):
                    n = g * GB + s
                    ga_s = ga[:, s % 2, :]
                    dve.wait_ge(gelu_done, n + 1)
                    dve.tensor_tensor(ga_s.rearrange("p (t n) -> p t n", t=NHT), ga_s.rearrange("p (t n) -> p t n", t=NHT),
                                      gr[:, :, s * HT:(s + 1) * HT], ALU.mult).then_inc(weighted, 1)
                    if not first and s == 0:
                        dve.wait_ge(y_made, g * NY)
                    dve.wait_ge(weighted, n + 1)
                    dve.tensor_copy(ah[:, s, :], ga_s).then_inc(ah_done, 1)
                    dve.wait_ge(ah_done, n + 1)
                    dve.tensor_tensor(al[:, s, :], ga_s, ah[:, s, :].bitcast(F32), ALU.subtract).then_inc(al_done, 1)
                    if not (last and s >= GB - 2):
                        split_u(n + 2, s % 2)
                    dve.wait_ge(vh_done, n + 1)
                    dve.tensor_tensor(vl[:, s, :], vr[:, s % 2, :], vh[:, s, :].bitcast(F32), ALU.subtract
                                      ).then_inc(vl_done, 1)
                for y in range(NY):
                    out = Y[:, y // 2, (y % 2) * 512:(y % 2 + 1) * 512]
                    dve.wait_ge(y_made, g * NY + (y + 1))
                    dve.tensor_tensor(out, out, yP[:, y % 4, :], ALU.add).then_inc(y_taken, 1)

            dve.wait_ge(y_zero, 1)
            body(0, True, False)
            with dve.Fori(1, NGR - 1) as g:
                body(g, False, False)
            body(NGR - 1, False, True)


class Stored:

    def __init__(self, sem, sb):
        self.v, self.a, self.g = sb("s_vr", [P, GB, D]), sb("s_ar", [P, GB, TOK]), sb("s_gr", [P, NHT, GB * HT])
        self.v_in, self.a_in = [sem(f"sv_in{n}") for n in range(GB)], [sem(f"sa_in{n}") for n in range(GB)]
        self.g_in = sem("sG_in")

    def start(self, eng, T):
        eng.dma_start(self.g[:, :, :], T["G"].rearrange("t p j n -> p t (j n)")[:, :, 0:GB * HT]).then_inc(self.g_in, 16)
        for s in range(GB):
            eng.dma_start(self.a[:, s, :], T["HG"][s]).then_inc(self.a_in[s], 16)

    def start_v(self, eng, T):
        for s in range(GB):
            eng.dma_start(self.v[:, s, :], T["v_tab"][s]).then_inc(self.v_in[s], 16)


def stored_experts(nc, m, T, sem, sb, psctx, stored, ahead):
    NGR = NPRE // GB
    NY = 2 * NT
    Y = m.oN
    vr, ar, gr = stored.v, stored.a, stored.g
    v_in, a_in, g_in = stored.v_in, stored.a_in, stored.g_in
    vh, vl = sb("s_vh", [P, 2, GB, D], F32R), sb("s_vl", [P, 2, GB, D], F32R)
    ah, al = (t[:, :, :].rearrange("p (a b) t -> p a b t", a=2) for t in (m.h2h, m.h2l))
    weighted = sem("s_weighted")
    vh_done, vl_done, ah_done, al_done = sem("s_vh"), sem("s_vl"), sem("s_ah"), sem("s_al")
    y_made, y_taken = sem("s_ymade"), sem("s_ytaken")
    Glayout = T["G"].rearrange("t p j n -> p t (j n)")
    with psctx() as ps, nc.Block() as block:
        yP = ps("s_y", [P, 4, 512])
        YB = [max(y for y in range(NY) if y % 4 == a) for a in range(4)]

        @block.sync
        def _(sp):
            ahead(sp)
            with sp.Fori(1, NGR) as g:
                sp.wait_ge(weighted, g * GB)
                sp.dma_start(gr[:, :, :], Glayout[:, :, ds(g * (GB * HT), GB * HT)]).then_inc(g_in, 16)
                for s in range(GB):
                    sp.wait_ge(al_done, g * GB - (GB - 1 - s))
                    sp.dma_start(ar[:, s, :], T["HG"][ds(g * GB + s, 1)].rearrange("a p t -> (a p) t")).then_inc(a_in[s], 16)

        @block.gpsimd
        def _(pool):
            with pool.Fori(1, NGR) as g:
                for s in range(GB):
                    pool.wait_ge(vl_done, g * GB - (GB - 1 - s))
                    pool.dma_start(vr[:, s, :], T["v_tab"][ds(g * GB + s, 1)].rearrange("a p n -> (a p) n")
                                   ).then_inc(v_in[s], 16)

        @block.tensor
        def _(pe):
            def outputs(g, par, first=False):
                pe.wait_ge(al_done, g * GB + GB)
                pe.wait_ge(vl_done, g * GB + GB)
                pe.wait_ge(vh_done, g * GB + GB)
                for y in range(NY):
                    t, d = y // 2, slice((y % 2) * 512, (y % 2 + 1) * 512)
                    if y >= 4 or not first:
                        before = y - 4 if y >= 4 else (YB[y] - NY)
                        pe.wait_ge(y_taken, g * NY + (before + 1))
                    for b in range(GB):
                        for a, v in ((ah, vh), (al, vh), (ah, vl)):
                            mm = pe.matmul(yP[:, y % 4, :], a[:, par, b, t * P:(t + 1) * P], v[:, par, b, d],
                                           start=(b == 0 and a is ah and v is vh), stop=(b == GB - 1 and v is vl))
                    mm.then_inc(y_made, 1)

            outputs(0, 0, True)
            outputs(1, 1)
            with pe.Fori(1, NGR // 2) as i:
                for par in range(2):
                    outputs(i * 2 + par, par)

        @block.scalar
        def _(act):
            def split(g, par, first=False):
                for s in range(GB):
                    act.wait_ge(v_in[s], g * 16 + 16)
                    if not first:
                        act.wait_ge(y_made, g * NY - NY)
                    act.copy(vh[:, par, s, :], vr[:, s, :]).then_inc(vh_done, 1)
                    act.wait_ge(weighted, g * GB + (s + 1))
                    act.copy(ah[:, par, s, :], ar[:, s, :]).then_inc(ah_done, 1)

            split(0, 0, True)
            split(1, 1, True)
            with act.Fori(1, NGR // 2) as i:
                for par in range(2):
                    split(i * 2 + par, par)

        @block.vector
        def _(dve):
            def prepare(g, s, par, first=False):
                dve.wait_ge(g_in, g * 16 + 16)
                dve.wait_ge(a_in[s], g * 16 + 16)
                a = ar[:, s, :].rearrange("p (t n) -> p t n", t=NHT)
                dve.tensor_tensor(a, a, gr[:, :, s * HT:(s + 1) * HT], ALU.mult).then_inc(weighted, 1)
                if not first:
                    dve.wait_ge(y_made, g * NY - NY)
                dve.wait_ge(vh_done, g * GB + (s + 1))
                dve.tensor_tensor(vl[:, par, s, :], vr[:, s, :], vh[:, par, s, :].bitcast(F32), ALU.subtract
                                  ).then_inc(vl_done, 1)
                dve.wait_ge(ah_done, g * GB + (s + 1))
                dve.tensor_tensor(al[:, par, s, :], ar[:, s, :], ah[:, par, s, :].bitcast(F32), ALU.subtract
                                  ).then_inc(al_done, 1)

            def add(g, par, first=False, last=False):
                for y in range(NY):
                    out = Y[:, y // 2, (y % 2) * 512:(y % 2 + 1) * 512]
                    dve.wait_ge(y_made, g * NY + (y + 1))
                    dve.tensor_tensor(out, out, yP[:, y % 4, :], ALU.add).then_inc(y_taken, 1)
                    if not last and y % 2 and y // 2 < GB:
                        prepare(g + 1, y // 2, 1 - par, first)

            for s in range(GB):
                prepare(0, s, 0, True)
            add(0, 0, True)
            with dve.Fori(0, NGR // 2 - 1) as i:
                add(i * 2 + 1, 1)
                add(i * 2 + 2, 0)
            add(NGR - 1, 1, False, True)


@contextmanager
def scope(alloc):
    with ExitStack() as stack:
        yield lambda name, shape, dt=F32: stack.enter_context(alloc(name, shape, dt))


def program(nc, T):
    with ExitStack() as whole:
        def sem(name):
            return nc.alloc_semaphore(name=name)

        def recycle(since):
            nc.clear_and_free_semaphores(nc.allocated_since(since))
            nc.all_engine_barrier()

        def sb(name, shape, dt=F32):
            return whole.enter_context(nc.sbuf_tensor(name, shape, dt))

        def sbctx():
            return scope(nc.sbuf_tensor)

        def psctx():
            return scope(nc.psum_tensor)

        m = Memory()
        none_yet = nc.snapshot_sems()
        build_constants(nc, m, sem, sb)
        m.scale, m.shift = sb("scale", [P, 2, KD, NCOND]), sb("shift", [P, 2, KD, NCOND])
        m.silu_c = sb("silu_c", [P, KD, NCOND])
        m.stat, m.rstd = sb("stat", [P, NT]), sb("rstd", [P, NT])
        m.oN = sb("oN", [P, NT, D])
        with sbctx() as s2:
            m.qkT = s2("qkT", [P, 8, TOK])
            m.xc = s2("xc", [P, 6, CONVW])
            m.vN, m.zN = s2("vN", [P, NT, 512]), s2("zN", [P, NT, 512])
            m.dt = s2("dt", [P, NT, H])
            m.a_log, m.d_skip = s2("a_log", [P, H]), s2("d_skip", [P, H])
            with sbctx() as s3:
                m.hT = s3("hT", [P, KD, TOK])
                x = m.qkT[:, :, :].rearrange("p k t -> p (k t)").rearrange("p (t d) -> p t d", t=NT)
                x_in = [sem(f"x_in{t}") for t in range(NT)]

                def load_x(sp):
                    for t in range(NT):
                        sp.dma_start(x[:, t, :], T["x"][t * P:(t + 1) * P, :]).then_inc(x_in[t], 16)

                with sbctx() as s4, psctx() as pp:
                    modulate(nc, m, T, sem, s4, pp, load_x)
                ring = SplitRing(sem, "proj_w", T["w_cols"], s3)

                def load_weights(sp):
                    for n in range(2):
                        ring.load(sp, n, n, True)

                with sbctx() as s4, psctx() as pp:
                    m.junk = s4("junk1", [P, 2, D])
                    norm_to_columns(nc, m, sem, pp, "n1", x_in, x, m.hT, 0, load_weights)
                m.xpad = s3("xpad", [P, 6, CONVW])
                m.conv_w, m.conv_b = s3("conv_w", [P, 6, CW]), s3("conv_b", [P, 6])
                m.dt_bias = s3("dt_bias", [P, H])
                project(nc, m, T, sem, s3, ring, psctx)
            with sbctx() as s3, psctx() as pp:
                scan(nc, m, T, sem, s3, pp)
            with sbctx() as s3:
                attend(nc, m, T, sem, s3, psctx)
        recycle(none_yet)
        with sbctx() as s1:
            m.u = SplitRing(sem, "u", T["uT"], s1)
            m.h2h, m.h2l = s1("h2h", [P, KD, TOK], F32R), s1("h2l", [P, KD, TOK], F32R)
            kept = nc.snapshot_sems()
            with sbctx() as s2:
                m.qhT = s2("qhT", [P, KD, TOK])
                with sbctx() as s3:
                    mix(nc, m, T, sem, s3, psctx)
                with sbctx() as s3:
                    route(nc, m, T, sem, s3, psctx)
            recycle(kept)
            stored = Stored(sem, s1)
            experts(nc, m, T, sem, psctx, stored)
            with sbctx() as s2:
                more = s2("x1_again", [P, 2, D])
                keep = [more[:, 0, :], more[:, 1, :], stored.v[:, 2, :], stored.v[:, 3, :],
                        stored.a[:, :, :].rearrange("p s t -> p (s t)")[:, 0:D]]
                gates = m.u.raw[:, :, :, :].rearrange("p s k c -> p s (k c)")
                res = Residual(sem, s2, "res2", T["x1"], T["g_post_ffn"], 1, keep, gates, 3)
                stored_experts(nc, m, T, sem, s2, psctx, stored, lambda sp: res.load(sp, T))
                add_residual(nc, m, sem, "res2", res, m.oN, T["y_out"], stored.v[:, 0:2, :])


INS = dict(x=[TOK, D], cT=[P, KD, NCOND], w_ada=[D, ADA], b_ada=[ADA], g_pre_mix=[P, KD], g_pre_ffn=[P, KD],
           w_cols=[14, P, KD, P], w_vz=[P, KD, 1024 + H], state_conv=[P, 6, NSEQ, CW - 1], conv_w=[P, 6, CW],
           conv_b=[P, 6], dt_bias=[H], a_log=[H], d_skip=[H],
           state_ssm=[P, NSEQ, 256], g_mix=[P, KD], cache_kT=[NSEQ, P, 4, PAST], cache_v=[NSEQ, PAST, 512],
           w_out=[D, D], g_post_mix=[D], g_post_ffn=[D], w_pq=[8, P, KD, P], sub_keys=[P, NKEY],
           uT=[NKEY, P, KD, P], v_tab=[NKEY, P, D])
OUTS = dict(kT_out=[P, 4, TOK], v_out=[TOK, 512], conv_out=[P, 6, NCOND, CW - 1], ssm_out=[P, NCOND, 256], y_out=[TOK, D])
SCRATCH = dict(gates=[2, NCOND, D], G=[NHT, P, NKEY, HT], HG=[NPRE, P, TOK], x1=[TOK, D])


def layout(x_prompt, x_sample, c_prompt, c_sample, cache_k, cache_v, state_ssm, state_conv, w_ada, b_ada, g_pre_mix,
           g_post_mix, g_pre_ffn, g_post_ffn, w_in, conv_w, conv_b, dt_bias, a_log, d_skip, g_attn_norm, g_ssd_norm,
           w_out, w_pq, sub_keys, u_tab, v_tab):
    def col_blocks(w):
        return w.reshape(KD, P, -1, P).transpose(2, 1, 0, 3)

    def by_column(g):
        return g.reshape(-1, P).T

    w = w_in[0]
    att, ssd = 3 * 512, 3 * 512 + 512
    return dict(
        x=np.concatenate([x_prompt.reshape(SEQ, D), x_sample.reshape(P, D)]),
        cT=np.concatenate([c_prompt, c_sample]).reshape(NCOND, KD, P).transpose(2, 1, 0),
        w_ada=w_ada[0], b_ada=b_ada[0], g_pre_mix=by_column(g_pre_mix), g_pre_ffn=by_column(g_pre_ffn),
        w_cols=col_blocks(np.concatenate([w[:, :1024], w[:, ssd:ssd + 768]], 1)),
        w_vz=np.concatenate([w[:, 1024:ssd], w[:, ssd + 768:]], 1).reshape(KD, P, -1).transpose(1, 0, 2),
        state_conv=state_conv[0].reshape(NSEQ, CW - 1, 6, P).transpose(3, 2, 0, 1),
        conv_w=conv_w[0].reshape(CW, 6, P).transpose(2, 1, 0), conv_b=by_column(conv_b),
        dt_bias=dt_bias[0], a_log=a_log[0], d_skip=d_skip[0],
        state_ssm=state_ssm[0].reshape(NSEQ, 2, 4, HD, 64).transpose(1, 4, 0, 2, 3).reshape(P, NSEQ, 256),
        g_mix=by_column(np.concatenate([g_attn_norm, g_ssd_norm], 1)),
        cache_kT=cache_k[0].reshape(NSEQ, PAST, 4, P).transpose(0, 3, 2, 1),
        cache_v=cache_v[0].reshape(NSEQ, PAST, 512),
        w_out=w_out[0], g_post_mix=g_post_mix[0], g_post_ffn=g_post_ffn[0], w_pq=col_blocks(w_pq[0]),
        sub_keys=sub_keys[0].transpose(0, 2, 1).reshape(P, NKEY),
        uT=u_tab[0].reshape(P, NKEY, KD, P).transpose(1, 3, 2, 0),
        v_tab=v_tab[0].reshape(P, NKEY, D).transpose(1, 0, 2))


def unlayout(r):
    y, v = r["y_out"], r["v_out"]
    k = r["kT_out"].transpose(2, 1, 0).reshape(TOK, 512)
    conv = r["conv_out"].transpose(2, 3, 1, 0).reshape(NCOND, CW - 1, 768)
    ssm = r["ssm_out"].reshape(2, 64, NCOND, 4, HD).transpose(2, 0, 3, 4, 1).reshape(NCOND, H, HD, 64)
    c = np.ascontiguousarray
    return (c(y[:SEQ]).reshape(1, SEQ, D), c(y[SEQ:]).reshape(NSEQ, LSEQ, D),
            c(k[:SEQ]).reshape(1, 1, SEQ, H, HD), c(v[:SEQ]).reshape(1, 1, SEQ, H, HD), c(ssm[None, :1]), c(conv[None, :1]),
            c(k[SEQ:]).reshape(1, NSEQ, LSEQ, H, HD), c(v[SEQ:]).reshape(1, NSEQ, LSEQ, H, HD), c(ssm[None, 1:]),
            c(conv[None, 1:]))


def build(nc):
    T = {}
    for name, shape in INS.items():
        T[name] = nc.dram_tensor("in_" + name, shape, F32, kind="ExternalInput").ap()
    for name, shape in OUTS.items():
        T[name] = nc.dram_tensor("out_" + name, shape, F32, kind="ExternalOutput").ap()
    for name, shape in SCRATCH.items():
        T[name] = nc.dram_tensor("scratch_" + name, shape, F32).ap()
    program(nc, T)


def kernel(**inputs):
    import concourse.bacc as bacc
    from concourse.bass_utils import run_bass_kernel_spmd

    nc = bacc.Bacc("TRN2", target_bir_lowering=False, num_devices=1)
    build(nc)
    arrays = {"in_" + k: np.ascontiguousarray(a) for k, a in layout(**inputs).items()}
    r = run_bass_kernel_spmd(nc, [arrays], core_ids=[0]).results[0]
    return unlayout({k: r["out_" + k] for k in OUTS})
```
